# Optimizing a Trainium2 kernel written in Bass

```python
import jax, jax.numpy as jnp
from jax import lax
import numpy as np

D_MODEL = 1024
BATCH = 1
SEQ = 512
DEPTH = 1

N_HEADS = 8
QK_NOPE_DIM = 64
QK_ROPE_DIM = 32
V_HEAD_DIM = 64
Q_LORA_RANK = 256
KV_LORA_RANK = 128
ATTN_WIDTH = N_HEADS * V_HEAD_DIM
CONV_WIDTH = 512
CONV_K = 3
N_BRANCH = 2
BRANCH_WIDTH = 512
D_FF = 2816
N_SUB = 3
ROPE_THETA = 10000.0
Q_BLOCK = 128
EPS = 1e-6
IN_COLS = Q_LORA_RANK + KV_LORA_RANK + QK_ROPE_DIM + 3 * CONV_WIDTH + N_BRANCH * D_MODEL


def rms_norm(x, w):
    xf = x.astype(jnp.float32)
    y = xf * lax.rsqrt(jnp.mean(xf * xf, axis=-1, keepdims=True) + EPS)
    return (y * w.astype(jnp.float32)).astype(x.dtype)

def modulate(x, w, shift, scale):
    return rms_norm(x, w) * (1 + scale[:, None, :]) + shift[:, None, :]

def swiglu(h, w13, w2):
    gu = jnp.einsum('bsd,df->bsf', h, w13)
    g, u = jnp.split(gu, 2, axis=-1)
    return jnp.einsum('bsf,fd->bsd', jax.nn.silu(g) * u, w2)

def rope_tables(positions):
    inv_freq = 1.0 / (ROPE_THETA ** (jnp.arange(0, QK_ROPE_DIM, 2, dtype=jnp.float32) / QK_ROPE_DIM))
    ang = positions.astype(jnp.float32)[..., None] * inv_freq
    return jnp.cos(ang), jnp.sin(ang)

def apply_rope(x, cos, sin):
    xf = x.astype(jnp.float32)
    x1, x2 = jnp.split(xf, 2, axis=-1)
    return jnp.concatenate([x1 * cos - x2 * sin, x2 * cos + x1 * sin], axis=-1).astype(x.dtype)

def causal_mla_attention(q_nope, q_rope, k_nope, k_rope, v):
    b, s, h, _ = q_nope.shape
    nb = s // Q_BLOCK
    scale = (QK_NOPE_DIM + QK_ROPE_DIM) ** -0.5
    key_idx = jnp.arange(s)

    def to_blocks(t):
        return jnp.moveaxis(t.reshape(b, nb, Q_BLOCK, *t.shape[2:]), 1, 0)

    def block(args):
        qn, qr, i = args
        sc = (jnp.einsum('bqhd,bkhd->bhqk', qn, k_nope, preferred_element_type=jnp.float32)
              + jnp.einsum('bqhr,bkr->bhqk', qr, k_rope, preferred_element_type=jnp.float32))
        q_idx = i * Q_BLOCK + jnp.arange(Q_BLOCK)
        mask = key_idx[None, :] <= q_idx[:, None]
        sc = jnp.where(mask, sc * scale, -jnp.inf)
        p = jax.nn.softmax(sc, axis=-1).astype(v.dtype)
        return jnp.einsum('bhqk,bkhd->bqhd', p, v)

    out = lax.map(block, (to_blocks(q_nope), to_blocks(q_rope), jnp.arange(nb)))
    return jnp.moveaxis(out, 0, 1).reshape(b, s, h * V_HEAD_DIM)

def hybrid_mixer(h, cos, sin, w_in, q_a_norm, w_uq, kv_a_norm, w_ukv,
                 q_norm_nope, k_norm_nope, q_norm_rope, k_norm_rope,
                 conv_w, w_branch, w_out):
    b, s, _ = h.shape
    proj = jnp.einsum('bsd,dn->bsn', h, w_in)
    i1 = Q_LORA_RANK
    i2 = i1 + KV_LORA_RANK
    i3 = i2 + QK_ROPE_DIM
    i4 = i3 + 3 * CONV_WIDTH
    c_q, c_kv, k_rope, conv_in, gate_logits = jnp.split(proj, [i1, i2, i3, i4], axis=-1)

    q = jnp.einsum('bsr,rn->bsn', rms_norm(c_q, q_a_norm), w_uq)
    q = q.reshape(b, s, N_HEADS, QK_NOPE_DIM + QK_ROPE_DIM)
    q_nope, q_rope = q[..., :QK_NOPE_DIM], q[..., QK_NOPE_DIM:]
    kv = jnp.einsum('bsr,rn->bsn', rms_norm(c_kv, kv_a_norm), w_ukv)
    kv = kv.reshape(b, s, N_HEADS, QK_NOPE_DIM + V_HEAD_DIM)
    k_nope, v = kv[..., :QK_NOPE_DIM], kv[..., QK_NOPE_DIM:]
    q_nope = rms_norm(q_nope, q_norm_nope)
    k_nope = rms_norm(k_nope, k_norm_nope)
    q_rope = apply_rope(rms_norm(q_rope, q_norm_rope), cos[:, :, None, :], sin[:, :, None, :])
    k_rope = apply_rope(rms_norm(k_rope, k_norm_rope), cos, sin)
    o_attn = causal_mla_attention(q_nope, q_rope, k_nope, k_rope, v)

    xv, gate_b, gate_c = jnp.split(conv_in, 3, axis=-1)
    u = gate_c * xv
    u = lax.conv_general_dilated(u, conv_w[:, None, :], window_strides=(1,),
                                 padding=[(CONV_K - 1, 0)],
                                 dimension_numbers=('NWC', 'WIO', 'NWC'),
                                 feature_group_count=CONV_WIDTH)
    o_conv = gate_b * u

    branches = jnp.stack([o_attn, o_conv], axis=2)
    y_br = jnp.einsum('bsgk,gkd->bsgd', branches, w_branch)
    gates = jax.nn.sigmoid(gate_logits.reshape(b, s, N_BRANCH, D_MODEL))
    merged = jnp.sum(gates * y_br, axis=2)
    return jnp.einsum('bsd,de->bse', merged, w_out)

def first_inputs(seed: int = 0) -> dict:
    key = jax.random.key(seed)
    ks = jax.random.split(key, 20)
    f32 = jnp.float32

    def nrm(k, shape, fan_in):
        return jax.random.normal(k, shape, f32) * (fan_in ** -0.5)

    def gain(k, shape):
        return 1.0 + 0.02 * jax.random.normal(k, shape, f32)

    x = jax.random.normal(ks[0], (BATCH, SEQ, D_MODEL), f32)
    c = jax.random.normal(ks[1], (BATCH, D_MODEL), f32)
    offsets = jax.random.randint(ks[2], (BATCH, 1), 0, 1024, dtype=jnp.int32)
    positions = jnp.arange(SEQ, dtype=jnp.int32)[None, :] + offsets
    return {
        "x": x,
        "c": c,
        "positions": positions,
        "w_ada": nrm(ks[3], (DEPTH, D_MODEL, 3 * N_SUB * D_MODEL), D_MODEL),
        "b_ada": 0.01 * jax.random.normal(ks[4], (DEPTH, 3 * N_SUB * D_MODEL), f32),
        "norm_w": gain(ks[5], (DEPTH, N_SUB, D_MODEL)),
        "ffn_w13": nrm(ks[6], (DEPTH, 2, D_MODEL, 2 * D_FF), D_MODEL),
        "ffn_w2": nrm(ks[7], (DEPTH, 2, D_FF, D_MODEL), D_FF),
        "w_in": nrm(ks[8], (DEPTH, D_MODEL, IN_COLS), D_MODEL),
        "q_a_norm": gain(ks[9], (DEPTH, Q_LORA_RANK)),
        "w_uq": nrm(ks[10], (DEPTH, Q_LORA_RANK, N_HEADS * (QK_NOPE_DIM + QK_ROPE_DIM)), Q_LORA_RANK),
        "kv_a_norm": gain(ks[11], (DEPTH, KV_LORA_RANK)),
        "w_ukv": nrm(ks[12], (DEPTH, KV_LORA_RANK, N_HEADS * (QK_NOPE_DIM + V_HEAD_DIM)), KV_LORA_RANK),
        "q_norm_nope": gain(ks[13], (DEPTH, QK_NOPE_DIM)),
        "k_norm_nope": gain(ks[14], (DEPTH, QK_NOPE_DIM)),
        "q_norm_rope": gain(ks[15], (DEPTH, QK_ROPE_DIM)),
        "k_norm_rope": gain(ks[16], (DEPTH, QK_ROPE_DIM)),
        "conv_w": nrm(ks[17], (DEPTH, CONV_K, CONV_WIDTH), CONV_K),
        "w_branch": nrm(ks[18], (DEPTH, N_BRANCH, BRANCH_WIDTH, D_MODEL), BRANCH_WIDTH),
        "w_out": nrm(ks[19], (DEPTH, D_MODEL, D_MODEL), D_MODEL),
    }

def first_block(x, c, positions, w_ada, b_ada, norm_w, ffn_w13, ffn_w2, w_in,
              q_a_norm, w_uq, kv_a_norm, w_ukv, q_norm_nope, k_norm_nope,
              q_norm_rope, k_norm_rope, conv_w, w_branch, w_out):
    b = x.shape[0]
    cos, sin = rope_tables(positions)
    c_act = jax.nn.silu(c)
    for l in range(DEPTH):
        mod = (jnp.einsum('bd,dn->bn', c_act, w_ada[l]) + b_ada[l]).reshape(b, N_SUB, 3, D_MODEL)
        h = modulate(x, norm_w[l, 0], mod[:, 0, 0], mod[:, 0, 1])
        x = x + 0.5 * mod[:, 0, 2][:, None, :] * swiglu(h, ffn_w13[l, 0], ffn_w2[l, 0])
        h = modulate(x, norm_w[l, 1], mod[:, 1, 0], mod[:, 1, 1])
        y = hybrid_mixer(h, cos, sin, w_in[l], q_a_norm[l], w_uq[l], kv_a_norm[l], w_ukv[l],
                         q_norm_nope[l], k_norm_nope[l], q_norm_rope[l], k_norm_rope[l],
                         conv_w[l], w_branch[l], w_out[l])
        x = x + mod[:, 1, 2][:, None, :] * y
        h = modulate(x, norm_w[l, 2], mod[:, 2, 0], mod[:, 2, 1])
        x = x + 0.5 * mod[:, 2, 2][:, None, :] * swiglu(h, ffn_w13[l, 1], ffn_w2[l, 1])
    return x


GRID_W = 64
CTX_LEN = 256
D_FOURIER = 256
FOURIER_GROUPS = 4
D_CONV = 256
CONV_WIDTH_2 = 31
N_NA_HEADS = 8
NA_HEAD_DIM = 64
D_NA = N_NA_HEADS * NA_HEAD_DIM
WIN_ROWS = 8
WIN_COLS = 16
QKV_START = D_FOURIER + 2 * D_CONV
KV_START = QKV_START + D_NA
D_IN = QKV_START + 3 * D_NA
D_MIX = D_FOURIER + D_CONV + D_NA
D_FF_2 = 4 * D_MODEL
N_MOD = 6
RMS_EPS = 1e-6
LN_EPS = 1e-5


def rms_norm_2(x, g):
    xf = x.astype(jnp.float32)
    y = xf * lax.rsqrt(jnp.mean(xf * xf, axis=-1, keepdims=True) + RMS_EPS)
    return (y * g.astype(jnp.float32)).astype(x.dtype)

def layer_norm(x, g, b):
    xf = x.astype(jnp.float32)
    mu = jnp.mean(xf, axis=-1, keepdims=True)
    var = jnp.mean(jnp.square(xf - mu), axis=-1, keepdims=True)
    y = (xf - mu) * lax.rsqrt(var + LN_EPS)
    return (y * g.astype(jnp.float32) + b.astype(jnp.float32)).astype(x.dtype)

def modulate_2(x, shift, scale):
    return x * (1 + scale) + shift

def split_heads(u):
    b, l, _ = u.shape
    qkv = u[..., QKV_START:].reshape(b, l, 3, N_NA_HEADS, NA_HEAD_DIM)
    return u[..., :D_FOURIER], u[..., D_FOURIER:QKV_START], qkv[:, :, 0], qkv[:, :, 1], qkv[:, :, 2]

def fourier_mix(u, w):
    b, l, _ = u.shape
    ug = u.reshape(b, l, FOURIER_GROUPS, D_FOURIER // FOURIER_GROUPS).astype(jnp.float32)
    f = jnp.fft.fftn(ug, axes=(1, 3), norm="ortho").real
    return f.reshape(b, l, D_FOURIER).astype(u.dtype) @ w

def conv_module(u, dw_w, dw_b, ln_g, ln_b, pw_w, pw_b):
    a, gt = jnp.split(u, 2, axis=-1)
    v = a * jax.nn.sigmoid(gt)
    pad = CONV_WIDTH_2 // 2
    v = lax.conv_general_dilated(v, dw_w[:, None, :].astype(v.dtype), window_strides=(1,), padding=[(pad, pad)],
                                 dimension_numbers=("NWC", "WIO", "NWC"), feature_group_count=D_CONV) + dw_b
    v = jax.nn.silu(layer_norm(v, ln_g, ln_b))
    return v @ pw_w + pw_b

def context_attention(q, k, v):
    s = jnp.einsum("bqhd,bkhd->bhqk", q, k).astype(jnp.float32) * (NA_HEAD_DIM ** -0.5)
    p = jax.nn.softmax(s, axis=-1).astype(v.dtype)
    o = jnp.einsum("bhqk,bkhd->bqhd", p, v)
    return o.reshape(q.shape[0], q.shape[1], D_NA)

def neighbourhood_attention(q, k, v, k_ctx, v_ctx, rpb):
    b, l, h, dh = q.shape
    rows = l // GRID_W
    kr = min(WIN_ROWS, rows)
    r = np.arange(rows)
    row_start = np.clip(r - kr // 2, 0, rows - kr)
    key_rows = row_start[:, None] + np.arange(kr)[None, :]
    col = np.arange(GRID_W)
    col_start = np.clip(col - WIN_COLS // 2, 0, GRID_W - WIN_COLS)
    col_valid = (col[None, :] >= col_start[:, None]) & (col[None, :] < col_start[:, None] + WIN_COLS)
    row_off = key_rows - r[:, None] + (WIN_ROWS - 1)
    col_off = np.clip(col[None, :] - col[:, None] + (WIN_COLS - 1), 0, 2 * WIN_COLS - 2)
    bias = rpb[:, row_off[:, :, None, None], col_off[None, None]].astype(jnp.float32)
    bias = jnp.where(jnp.asarray(col_valid)[None, None, None], bias, -jnp.inf)
    bias = bias.transpose(0, 1, 3, 2, 4).reshape(h, rows, GRID_W, kr * GRID_W)
    qg = q.reshape(b, rows, GRID_W, h, dh)
    kg = k.reshape(b, rows, GRID_W, h, dh)[:, key_rows].reshape(b, rows, kr * GRID_W, h, dh)
    vg = v.reshape(b, rows, GRID_W, h, dh)[:, key_rows].reshape(b, rows, kr * GRID_W, h, dh)
    scale = NA_HEAD_DIM ** -0.5
    s_loc = jnp.einsum("brqhd,brkhd->bhrqk", qg, kg).astype(jnp.float32) * scale + bias[None]
    s_ctx = jnp.einsum("brqhd,bchd->bhrqc", qg, k_ctx).astype(jnp.float32) * scale
    p = jax.nn.softmax(jnp.concatenate([s_loc, s_ctx], axis=-1), axis=-1).astype(v.dtype)
    n_loc = kr * GRID_W
    o = (jnp.einsum("bhrqk,brkhd->brqhd", p[..., :n_loc], vg)
         + jnp.einsum("bhrqc,bchd->brqhd", p[..., n_loc:], v_ctx))
    return o.reshape(b, l, D_NA)

def second_inputs(seed: int = 0) -> dict:
    key = jax.random.key(seed)
    ks = jax.random.split(key, 24)

    def nrm(k, shape, scale):
        return jax.random.normal(k, shape, jnp.float32) * scale

    return {
        "x": nrm(ks[0], (BATCH, SEQ, D_MODEL), 1.0),
        "c": nrm(ks[1], (BATCH, D_MODEL), 1.0),
        "ctx": nrm(ks[2], (BATCH, CTX_LEN, D_MODEL), 1.0),
        "c_ctx": nrm(ks[3], (D_MODEL,), 1.0),
        "ada_w": nrm(ks[4], (DEPTH, D_MODEL, N_MOD * D_MODEL), D_MODEL ** -0.5),
        "ada_b": nrm(ks[5], (DEPTH, N_MOD * D_MODEL), 0.02),
        "norm1_g": 1.0 + nrm(ks[6], (DEPTH, D_MODEL), 0.05),
        "norm2_g": 1.0 + nrm(ks[7], (DEPTH, D_MODEL), 0.05),
        "w_in": nrm(ks[8], (DEPTH, D_MODEL, D_IN), D_MODEL ** -0.5),
        "w_fourier": nrm(ks[9], (DEPTH, D_FOURIER, D_FOURIER), D_FOURIER ** -0.5),
        "conv_dw_w": nrm(ks[10], (DEPTH, CONV_WIDTH_2, D_CONV), CONV_WIDTH_2 ** -0.5),
        "conv_dw_b": nrm(ks[11], (DEPTH, D_CONV), 0.02),
        "conv_norm_g": 1.0 + nrm(ks[12], (DEPTH, D_CONV), 0.05),
        "conv_norm_b": nrm(ks[13], (DEPTH, D_CONV), 0.02),
        "conv_pw_w": nrm(ks[14], (DEPTH, D_CONV, D_CONV), D_CONV ** -0.5),
        "conv_pw_b": nrm(ks[15], (DEPTH, D_CONV), 0.02),
        "na_rpb": nrm(ks[16], (DEPTH, N_NA_HEADS, 2 * WIN_ROWS - 1, 2 * WIN_COLS - 1), 0.1),
        "w_out": nrm(ks[17], (DEPTH, D_MIX, D_MODEL), D_MIX ** -0.5),
        "mlp_w1": nrm(ks[18], (DEPTH, D_MODEL, D_FF_2), D_MODEL ** -0.5),
        "mlp_w2": nrm(ks[19], (DEPTH, D_FF_2, D_MODEL), D_FF_2 ** -0.5),
        "final_norm_g": 1.0 + nrm(ks[20], (D_MODEL,), 0.05),
    }

def second_block(x, c, ctx, c_ctx, ada_w, ada_b, norm1_g, norm2_g, w_in, w_fourier, conv_dw_w, conv_dw_b,
              conv_norm_g, conv_norm_b, conv_pw_w, conv_pw_b, na_rpb, w_out, mlp_w1, mlp_w2, final_norm_g):
    h_lat, h_ctx = x, ctx
    b = x.shape[0]
    n_ctx = ctx.shape[1]
    for i in range(DEPTH):
        last = i == DEPTH - 1
        conv_p = (conv_dw_w[i], conv_dw_b[i], conv_norm_g[i], conv_norm_b[i], conv_pw_w[i], conv_pw_b[i])
        mod = (jax.nn.silu(c) @ ada_w[i] + ada_b[i])[:, None, :]
        sh1, sc1, g1, sh2, sc2, g2 = jnp.split(mod, N_MOD, axis=-1)
        n_ctx_mod = (2 if last else N_MOD) * D_MODEL
        mod_c = (jax.nn.silu(c_ctx) @ ada_w[i][:, :n_ctx_mod] + ada_b[i][:n_ctx_mod])[None, None, :]
        mods_c = jnp.split(mod_c, n_ctx_mod // D_MODEL, axis=-1)

        hn_ctx = modulate_2(rms_norm_2(h_ctx, norm1_g[i]), mods_c[0], mods_c[1])
        if last:
            kv = (hn_ctx @ w_in[i][:, KV_START:]).reshape(b, n_ctx, 2, N_NA_HEADS, NA_HEAD_DIM)
            k_ctx, v_ctx = kv[:, :, 0], kv[:, :, 1]
        else:
            uf_c, uc_c, q_ctx, k_ctx, v_ctx = split_heads(hn_ctx @ w_in[i])
            mix_ctx = jnp.concatenate([fourier_mix(uf_c, w_fourier[i]), conv_module(uc_c, *conv_p),
                                       context_attention(q_ctx, k_ctx, v_ctx)], axis=-1)

        hn_lat = modulate_2(rms_norm_2(h_lat, norm1_g[i]), sh1, sc1)
        uf, uc, q, k, v = split_heads(hn_lat @ w_in[i])
        mix_lat = jnp.concatenate([fourier_mix(uf, w_fourier[i]), conv_module(uc, *conv_p),
                                   neighbourhood_attention(q, k, v, k_ctx, v_ctx, na_rpb[i])], axis=-1)
        h_lat = h_lat + g1 * (mix_lat @ w_out[i])

        hn = modulate_2(rms_norm_2(h_lat, norm2_g[i]), sh2, sc2)
        h_lat = h_lat + g2 * (jnp.square(jax.nn.relu(hn @ mlp_w1[i])) @ mlp_w2[i])

        if not last:
            h_ctx = h_ctx + mods_c[2] * (mix_ctx @ w_out[i])
            hn_c2 = modulate_2(rms_norm_2(h_ctx, norm2_g[i]), mods_c[3], mods_c[4])
            h_ctx = h_ctx + mods_c[5] * (jnp.square(jax.nn.relu(hn_c2 @ mlp_w1[i])) @ mlp_w2[i])
    return rms_norm_2(h_lat, final_norm_g)


def setup_inputs(seed=0):
    out = dict(first_inputs(seed))
    for name, value in second_inputs(seed + 1).items():
        if name != "x":
            out[name + "_2"] = value
    return out


def reference(
    x, c, positions, w_ada, b_ada, norm_w, ffn_w13, ffn_w2, w_in, q_a_norm, w_uq, kv_a_norm,
    w_ukv, q_norm_nope, k_norm_nope, q_norm_rope, k_norm_rope, conv_w, w_branch, w_out, c_2,
    ctx_2, c_ctx_2, ada_w_2, ada_b_2, norm1_g_2, norm2_g_2, w_in_2, w_fourier_2, conv_dw_w_2,
    conv_dw_b_2, conv_norm_g_2, conv_norm_b_2, conv_pw_w_2, conv_pw_b_2, na_rpb_2, w_out_2,
    mlp_w1_2, mlp_w2_2, final_norm_g_2,
):
    x = first_block(
        x, c, positions, w_ada, b_ada, norm_w, ffn_w13, ffn_w2, w_in, q_a_norm, w_uq, kv_a_norm,
        w_ukv, q_norm_nope, k_norm_nope, q_norm_rope, k_norm_rope, conv_w, w_branch, w_out,
    )
    return second_block(
        x, c_2, ctx_2, c_ctx_2, ada_w_2, ada_b_2, norm1_g_2, norm2_g_2, w_in_2, w_fourier_2,
        conv_dw_w_2, conv_dw_b_2, conv_norm_g_2, conv_norm_b_2, conv_pw_w_2, conv_pw_b_2,
        na_rpb_2, w_out_2, mlp_w1_2, mlp_w2_2, final_norm_g_2,
    )


_drawn_inputs = setup_inputs


def setup_inputs(seed=0):
    import zlib

    import numpy as np

    out = dict(_drawn_inputs(seed))
    spreads = {}
    factors = {'b_ada': 2.979,
     'q_a_norm': 8.0,
     'kv_a_norm': 8.0,
     'q_norm_nope': 8.0,
     'k_norm_nope': 8.0,
     'q_norm_rope': 8.0,
     'k_norm_rope': 8.0,
     'norm1_g_2': 4.511,
     'conv_dw_b_2': 30.781,
     'conv_norm_g_2': 20.909,
     'conv_norm_b_2': 49.707,
     'conv_pw_b_2': 44.007,
     'na_rpb_2': 8.0,
     'norm2_g_2': 3.664}
    for name, (base, spread) in spreads.items():
        noise = np.random.default_rng([zlib.crc32(name.encode()), seed]).standard_normal(out[name].shape)
        drawn = base * np.exp(spread * noise) if base else spread * noise
        out[name] = __import__('jax').numpy.asarray(drawn.astype(out[name].dtype))
    for name, factor in factors.items():
        out[name] = (out[name] * factor).astype(out[name].dtype)
    return out
```

```python
import numpy as np
import concourse.bass as bass
from concourse import mybir
from contextlib import ExitStack, contextmanager

F32 = mybir.dt.float32
F32R = mybir.dt.float32r
I32 = mybir.dt.int32
ALU = mybir.AluOpType
ACT = mybir.ActivationFunctionType
AX = mybir.AxisListType

P = 128
D = 1024
KC = D // P
S = 512
TT = S // P
CTX = 256
FF = 2816
EPS, LN_EPS = 1e-6, 1e-5
H = 8
DN, DR, DV = 64, 32, 64
DQ = DN + DR
QR, KR = 256, 128
CW, CK = 512, 3
COLS, ROWS = 64, 8
WIN = 16
QC = 16
KW = 32
NEAR = (0, QC // 2, QC // 2 + WIN, 2 * WIN)
VARIANT = (0, 1, 1, 2)
RPB_R, RPB_C = 2 * ROWS - 1, 2 * WIN - 1
SPAN = (ROWS - 1) * RPB_C + KW + WIN
SPAN_IN = SPAN - SPAN % 16
CW2, CK2 = 256, 31
PAD2 = CK2 // 2
DH = 64
NEG = -1e30
ROUND = 1.5 * 2.0 ** 23
HALF_TURN = float(np.float32(np.pi)) - 2.0 ** -22
TURN = (6.28125, 0.0019354820251464844, -1.7484555314695172e-07)

RING = 4
LEAD = 3
STRIP = KC * P
GEM = 256
FOLD = GEM // 32

FFN_PARTS = [(0, 8), (8, 8), (16, 6)]
FFN_STRIPS = sum(2 * n + KC for _, n in FFN_PARTS)
U_FFN0 = 0
U_LATENT = U_FFN0 + FFN_STRIPS
U_CONV = U_LATENT + 4
U_GATE = U_CONV + 12
U_BRANCH = U_GATE + 16
U_OUT = U_BRANCH + KC
U_FFN1 = U_OUT + KC
U_CTX = U_FFN1 + FFN_STRIPS
U_IN2 = U_CTX + 8
U_OUT2 = U_IN2 + 18
U_MLP = U_OUT2 + KC
MLP_PARTS = 4
STRIPS = U_MLP + MLP_PARTS * 2 * KC

V_C, V_C2, V_CCTX, V_NORM, V_N1G, V_N2G, V_FIN = 0, 8, 16, 24, 48, 56, 64
V_QA, V_KVA, V_DWB, V_LNG, V_LNB, V_PWB, V_CONV, V_ROWS = 72, 74, 75, 77, 79, 81, 83, 95
M_2, M_CTX, M_COLS = 72, 120, 136
A_1, A_2, A_CTX, A_COLS = 0, 24, 40, 48


class Tally:

    def __init__(self, sem):
        self.sem, self.n, self.it, self.per, self.start = sem, 0, None, 0, 0

    def enter(self, it, per):
        self.it, self.per, self.start = it, per, self.n

    def leave(self, times):
        assert self.n == self.start + self.per, (self.sem, self.n, self.start, self.per)
        self.n, self.it = self.start + self.per * times, None

    def add(self, k=1):
        self.n += k
        return self.n if self.it is None else self.it * self.per + self.n


@contextmanager
def loop(eng, times, *tallies):
    if times == 1:
        yield 0
        return
    with eng.Fori(0, times) as it:
        for t, per in tallies:
            t.enter(it, per)
        yield it
        for t, per in tallies:
            t.leave(times)


def block_pair_kernel(nc, a, out):
    with ExitStack() as ctx:
        place = [(nc.sbuf_base + 63) // 64 * 64]

        def sb(name, shape, dt=F32, over=None):
            size = int(np.prod(shape[1:])) * 4
            offset = place[0] if over is None else over
            if over is None:
                place[0] += (size + 63) // 64 * 64
            t = nc.alloc_sbuf_tensor_at(name, shape, dt, offset=offset)
            where[name] = offset
            return t

        where = {}
        X = sb("X", [P, KC * S])
        H_HI = sb("H_HI", [P, KC * S], F32R)
        H_LO = sb("H_LO", [P, KC * S], F32R)
        place[0] += 64
        A_HI = sb("A_HI", [P, KC * S], F32R)
        A_LO = sb("A_LO", [P, KC * S], F32R)
        RAW = sb("RAW", [P, RING * STRIP])
        W_HI = sb("W_HI", [P, RING * STRIP], F32R)
        W_LO = sb("W_LO", [P, RING * STRIP], F32R)
        COL1 = sb("COL1", [P, V_ROWS + 1])
        COL2 = sb("COL2", [P, M_CTX])
        COL3 = sb("COL3", [P, 2 * CK2])
        CSIL = sb("CSIL", [P, 3 * KC])
        IDENT = sb("IDENT", [P, P])
        ONES = sb("ONES", [P, P])
        FLIP = sb("FLIP", [P, P])
        SUM32 = sb("SUM32", [P, 32])
        MOD = sb("MOD", [P, M_COLS])
        AMOD = sb("AMOD", [P, A_COLS])
        GHALF = sb("GHALF", [P, 3 * KC])
        CONST = sb("CONST", [P, 4])
        STAT = sb("STAT", [P, 256])
        FOLDED = sb("FOLDED", [P, M_COLS * 4])
        SQ = sb("SQ", [P, 2 * S])
        UN = sb("UN", [P, 2 * S])
        RINV = sb("RINV", [P, S])
        SG = sb("SG", [P, 2 * S], over=where["SQ"])
        HF = sb("HF", [P, 2 * S], over=where["UN"])
        SSUM = sb("SSUM", [P, S])
        scratch = place[0]
        assert scratch + 60 * 1024 <= nc.sbuf_usable_end, (scratch, nc.sbuf_usable_end)
        GBUF = sb("GBUF", [P, 3 * KC * GEM], over=scratch)
        GACC = sb("GACC", [P, GEM], over=scratch + 3 * KC * GEM * 4)
        GTURN = sb("GTURN", [P, GEM], over=where["GACC"] + GEM * 4)
        GATES = sb("GATES", [P, 2 * KC * S], over=scratch)
        XV = sb("XV", [P, 4 * S], over=scratch)
        UPAD = S + CK - 1
        UB = sb("UB", [P, 4 * UPAD], over=scratch + 4 * S * 4)
        QTOK = sb("QTOK", [P, TT * H * DQ], over=scratch + 2 * KC * S * 4)
        KTOK = sb("KTOK", [P, TT * H * DQ], over=where["QTOK"] + TT * H * DQ * 4)
        KRF = sb("KRF", [DR, S], over=where["QTOK"])
        V = sb("V", [P, TT * H * DV], over=where["QTOK"])
        small = [where["KTOK"] + TT * H * DQ * 4]

        def small_sb(name, shape, dt=F32):
            t = sb(name, shape, dt, over=small[0])
            small[0] += (int(np.prod(shape[1:])) * 4 + 31) // 32 * 32
            assert small[0] <= nc.sbuf_usable_end
            return t

        POS = small_sb("POS", [P, TT], I32)
        FREQ = small_sb("FREQ", [P, DR // 2])
        HEADW = small_sb("HEADW", [P, 2 * DN + 2 * DR])
        KRT = small_sb("KRT", [P, TT * DR])
        CAUSAL = small_sb("CAUSAL", [P, P])
        ANGLE = small_sb("ANGLE", [P, 3 * TT * DR // 2])
        COS = small_sb("COS", [P, TT * DR // 2])
        SIN = small_sb("SIN", [P, TT * DR // 2])
        UQ = sb("UQ", [P, 2 * H * DQ], over=where["A_HI"])
        CKVT = sb("CKVT", [P, S], over=where["A_HI"] + 2 * H * DQ * 4)
        UKV = sb("UKV", [P, H * (DN + DV)], over=where["A_LO"])
        CQT = sb("CQT", [P, 2 * S], over=where["A_LO"] + H * (DN + DV) * 4)
        QT = sb("QT", [DQ, H * S], over=where["H_HI"])
        KT = sb("KT", [DQ, H * S], over=where["H_LO"])
        PROB = sb("PROB", [P, 4 * S], over=where["KTOK"])
        PT = sb("PT", [P, 2 * S], over=where["KTOK"] + 4 * S * 4)
        TQ0 = sb("TQ0", [P, H * DQ], over=where["SQ"])
        TQ1 = sb("TQ1", [P, H * DQ], over=where["UN"])
        CTOK = sb("CTOK", [P, 2 * D], over=scratch + 28 * 1024)
        C_HI = sb("C_HI", [P, KC * CTX], F32R, over=scratch + 36 * 1024)
        C_LO = sb("C_LO", [P, KC * CTX], F32R, over=scratch + 44 * 1024)
        KEYS = S + CTX
        KT2 = sb("KT2", [P, 4 * KEYS], over=scratch)
        QZ = sb("QZ", [P, 8 * S], over=scratch + 12 * 1024)
        VT = sb("VT", [P, 2 * TT * ROWS * KW], over=scratch + 28 * 1024)
        VW = sb("VW", [P, 8 * H * DH], over=scratch + 36 * 1024)
        VTC = sb("VTC", [P, 4 * CTX], over=scratch + 52 * 1024)
        VC = sb("VC", [P, 2 * H * DH], over=scratch + 56 * 1024)
        MASK = sb("MASK", [P, 3 * KW], over=scratch + 60 * 1024)
        assert scratch + 60 * 1024 + 3 * KW * 4 <= nc.sbuf_usable_end
        TCOS = sb("TCOS", [P, TT * S], over=where["A_HI"])
        TSIN = sb("TSIN", [P, TT * S], over=where["A_LO"])
        UT = sb("UT", [P, 2 * S], over=where["A_HI"] + 4 * S * 4)
        FT = sb("FT", [P, 2 * S], over=where["A_HI"] + 4 * S * 4)
        ACC = sb("ACC", [P, 2 * S], over=where["A_HI"] + 6 * S * 4)
        CPAD = S + CK2 - 1
        CV = sb("CV", [P, 2 * CPAD], over=where["A_LO"] + 4 * S * 4)
        DFEAT = sb("DFEAT", [P, 2 * P], over=where["CV"] + 2 * CPAD * 4 // 64 * 64 + 64)
        WF = sb("WF", [P, 2 * 2 * P], over=where["DFEAT"] + 2 * P * 4)
        assert where["WF"] + 4 * P * 4 <= where["A_LO"] + KC * S * 4
        PW = sb("PW", [P, 2 * CW2], over=where["RINV"])
        BIAS = sb("BIAS", [P, 3 * H * ROWS * KW], over=where["H_HI"])
        RPB = sb("RPB", [P, H * SPAN_IN + 16], over=where["H_LO"] + 4 * S * 4)
        assert where["RPB"] + H * SPAN_IN * 4 + 64 == where["A_HI"]
        CSQ = sb("CSQ", [P, 2 * S], over=where["CV"])
        UC = sb("UC", [P, TT * S], over=where["SQ"])
        PT2 = sb("PT2", [P, 2 * S], over=where["RPB"])
        PROB2 = sb("PROB2", [P, 4 * S], over=where["SQ"])
        XTOK = sb("XTOK", [P, TT * D], over=where["A_HI"])
        ROWS1 = sb("ROWS1", [V_ROWS, P], over=where["A_LO"])
        ROWS2 = sb("ROWS2", [M_CTX, P], over=where["A_LO"] + 512)
        ROWS3 = sb("ROWS3", [2 * CK2, P], over=where["A_LO"] + 1024)
        YT = sb("YT", [P, KC * S], over=where["A_HI"])
        YTOK = sb("YTOK", [P, TT * D], over=where["H_HI"])

        bank = [ctx.enter_context(nc.psum_tensor(f"bank{i}", [P, S], F32)) for i in range(8)]

        def sem(name):
            return ctx.enter_context(nc.semaphore(name))

        raw_in = [sem(f"raw_in{i}") for i in range(RING)]
        hi_ready = sem("hi_ready")
        lo_ready = sem("lo_ready")
        strip_done = sem("strip_done")
        bank_free = sem("bank_free")
        rows_in = sem("rows_in")
        x_in = sem("x_in")
        gem_in = [sem(f"gem_in{i}") for i in range(3)]
        gem_done = sem("gem_done")
        ident_ready = sem("ident_ready")
        const_ready = sem("const_ready")
        cols_turned = sem("cols_turned")
        cols_ready = sem("cols_ready")
        cond_ready = sem("cond_ready")
        x_turned = sem("x_turned")
        x_ready = sem("x_ready")
        mod_summed = sem("mod_summed")
        mod_ready = sem("mod_ready")
        sq_ready = sem("sq_ready")
        sq_used = sem("sq_used")
        stat_ready = sem("stat_ready")
        std_ready = sem("std_ready")
        un_ready = sem("un_ready")
        nhi_ready = sem("nhi_ready")
        h_ready = sem("h_ready")
        silu_ready = sem("silu_ready")
        ahi_ready = sem("ahi_ready")
        alo_ready = sem("alo_ready")
        dve_seq = sem("dve_seq")
        pool_seq = sem("pool_seq")
        up_in = sem("up_in")
        head_in = sem("head_in")
        lat_sq = sem("lat_sq")
        lat_sum = sem("lat_sum")
        lat_std = sem("lat_std")
        lat_ready = sem("lat_ready")
        kr_turned = sem("kr_turned")
        angle_ready = sem("angle_ready")
        sin_ready = sem("sin_ready")
        up_done = sem("up_done")
        up_read = sem("up_read")
        head_sq = sem("head_sq")
        head_sum = sem("head_sum")
        head_std = sem("head_std")
        k_ready = sem("k_ready")
        turned = sem("turned")
        turn_act = sem("turn_act")
        turn_dve = sem("turn_dve")
        score_done = sem("score_done")
        neg_ready = sem("neg_ready")
        exp_done = sem("exp_done")
        prob_ready = sem("prob_ready")
        prob_turned = sem("prob_turned")
        pt_ready = sem("pt_ready")
        pv_done = sem("pv_done")
        ohi_ready = sem("ohi_ready")
        olo_ready = sem("olo_ready")
        mixed = sem("mixed")
        merged = sem("merged")
        mhi_ready = sem("mhi_ready")
        mlo_ready = sem("mlo_ready")
        ctx_in = sem("ctx_in")
        ctx_sq = sem("ctx_sq")
        ctx_std = sem("ctx_std")
        ctx_ready = sem("ctx_ready")
        ctx_mod = sem("ctx_mod")
        ctx_turned = sem("ctx_turned")
        ctx_full = sem("ctx_full")
        chi_ready = sem("chi_ready")
        clo_ready = sem("clo_ready")
        flip_ready = sem("flip_ready")
        rpb_in = sem("rpb_in")
        table_in = sem("table_in")
        zeros_ready = sem("zeros_ready")
        sig_ready = sem("sig_ready")
        conv_ready = sem("conv_ready")
        ln_sum = sem("ln_sum")
        dev_ready = sem("dev_ready")
        ln_sq = sem("ln_sq")
        ln_std = sem("ln_std")
        z_ready = sem("z_ready")
        act_ready = sem("act_ready")
        uc_done = sem("uc_done")
        uc_act = sem("uc_act")
        uc_dve = sem("uc_dve")
        ft_done = sem("ft_done")
        ft_act = sem("ft_act")
        ft_dve = sem("ft_dve")
        rpb_turned = sem("rpb_turned")
        bias_ready = sem("bias_ready")
        vw_turned = sem("vw_turned")
        vw_act = sem("vw_act")
        vw_dve = sem("vw_dve")
        mix_done = sem("mix_done")
        mix_hi = sem("mix_hi")
        y_ready = sem("y_ready")
        y_turned = sem("y_turned")
        ytok_ready = sem("ytok_ready")
        out_done = sem("out_done")

        def chunk(t, k, n=S):
            return t[:, bass.ds(k * n, n)]

        def heads(t):
            return t.rearrange("p (h d) -> p h d", h=H)

        def soft(n, i):
            return STAT[:, 128 + n % 4 * 4 + i:128 + n % 4 * 4 + i + 1]

        def by_rows(t):
            return t.rearrange("p (r j c) -> p j r c", r=ROWS, j=TT)

        def by_tiles(t):
            return t.rearrange("p (j r c) -> p j r c", j=TT, r=ROWS)

        def window_values(n):
            if n >= 8:
                return chunk(VC, n - 8)
            c, half = n // 2, n % 2
            return VW[:, half * 4 * S:(half + 1) * 4 * S].rearrange("p (t f) -> p t f", t=4)[:, :, c * P:(c + 1) * P]

        def window_bank(n):
            b = bank[4 + n % 4][:, :]
            return b if n >= 8 else b.rearrange("p (t f) -> p t f", t=4)

        def strip_of(t, slot):
            return t[:, slot * STRIP:(slot + 1) * STRIP]

        def rows_of(w):
            return w.rearrange("(k p) n -> p k n", p=P)

        w13 = [rows_of(a["ffn_w13"][0, f]) for f in range(2)]
        w2 = [rows_of(a["ffn_w2"][0, f]) for f in range(2)]
        w_in, w_out = rows_of(a["w_in"][0]), rows_of(a["w_out"][0])
        w_branch = rows_of(a["w_branch"][0].rearrange("g k d -> (g k) d"))
        w_ada, ada_2 = rows_of(a["w_ada"][0]), rows_of(a["ada_w_2"][0])
        w_in2, w_out2 = rows_of(a["w_in_2"][0]), rows_of(a["w_out_2"][0])
        w_mlp1, w_mlp2 = rows_of(a["mlp_w1_2"][0]), rows_of(a["mlp_w2_2"][0])

        def gem_src(t):
            return w_ada[:, :, bass.ds(t * GEM, GEM)]

        def gem_src2(t):
            return ada_2[:, :, bass.ds((t - T_ADA) * GEM, GEM)]

        T_ADA = 9 * D // GEM
        T_2 = T_ADA + 6 * D // GEM

        rpb = nc.dram_tensor("rpb_padded", (2 * WIN + H * RPB_R * RPB_C,), F32, kind="Internal").ap()
        IN2_COLS = [c * P for c in (0, 1, 4, 2, 5, 3)] + [c * P for c in range(6, 18)]

        block = ctx.enter_context(nc.Block())

        @block.sync
        def _(sp):
            gem = [Tally(gem_in[i]) for i in range(3)]

            def load_strip(u, slot, src):
                dst = strip_of(RAW, slot)[:, 0:src.shape[1] * src.shape[2]]
                sp.wait_ge(lo_ready, u + 1)
                sp.dma_start(dst.rearrange("p (k n) -> p k n", k=src.shape[1]), src).then_inc(raw_in[slot], 16)

            def load_gem(slot, src):
                dst = GBUF[:, slot * KC * GEM:(slot + 1) * KC * GEM].rearrange("p (k n) -> p k n", k=KC)
                sp.dma_start(dst, src).then_inc(gem_in[slot], 16)

            def load_strips(u0, count, src):
                with loop(sp, count // RING) as it:
                    for j in range(RING):
                        load_strip(it * RING + (u0 + j), (u0 + j) % RING, src(it * RING + j))

            def load_up(u0, w, width, c0, chunks, gem0=None, src=None):
                with loop(sp, chunks // 2) as it:
                    for j in range(RING):
                        col = (it * 2 + (j // 2 + c0)) * P + (j % 2) * width
                        load_strip(it * RING + (u0 + j), (u0 + j) % RING, w[:, :, bass.ds(col, P)])
                        if gem0 is not None and j % 2:
                            sp.wait_ge(gem_done, it * 2 + (gem0 + j // 2 - 1))
                            load_gem(j // 2, src(it * 2 + (gem0 + j // 2)))

            def load_down(u0, w, c0, chunks, gem0=None, src=None):
                with loop(sp, KC // RING) as it:
                    for j in range(RING):
                        load_strip(it * RING + (u0 + j), (u0 + j) % RING,
                                   w[:, c0:c0 + chunks, bass.ds((it * RING + j) * P, P)])
                        if gem0 is not None and j == RING - 1:
                            sp.wait_ge(gem_done, it + gem0)
                            load_gem(2, src(it + gem0))

            def rows(dst, names):
                at = 0
                for name in names:
                    v = a[name]
                    flat = v.rearrange(" ".join("abc"[:len(v.shape)]) + " -> (" + " ".join("abc"[:len(v.shape)]) + ")") if len(v.shape) > 1 else v
                    n = int(np.prod(v.shape)) // P
                    sp.dma_start(dst[at:at + n, :], flat.rearrange("(r p) -> r p", p=P)).then_inc(rows_in, 16)
                    at += n

            rows(ROWS1, ["c", "c_2", "c_ctx_2", "norm_w", "norm1_g_2", "norm2_g_2", "final_norm_g_2", "q_a_norm",
                         "kv_a_norm", "conv_dw_b_2", "conv_norm_g_2", "conv_norm_b_2", "conv_pw_b_2", "conv_w"])
            rows(ROWS2, ["b_ada", "ada_b_2"])
            rows(ROWS3, ["conv_dw_w_2"])
            load_gem(0, gem_src(0))
            with nc.allow_non_contiguous_dma(reason="512 positions, one to a partition"):
                sp.dma_start(POS[:, :], a["positions"].rearrange("a (t p) -> p (a t)", p=P)).then_inc(head_in, 16)
            sp.dma_start(FREQ[:, :], a["rope_freq"]).then_inc(head_in, 16)
            sp.dma_start(CAUSAL[:, :], a["causal"]).then_inc(head_in, 16)
            flat = a["na_rpb_2"].rearrange("a h r c -> (a h r c)")
            n, pad = H * RPB_R * RPB_C, WIN
            for to, frm, size in ((pad, 0, n), (0, 0, pad), (pad + n, n - pad, pad)):
                sp.dma_start(rpb[to:to + size], flat[frm:frm + size]).then_inc(rpb_in, 16)
            at = 0
            for name, n in (("q_norm_nope", DN), ("k_norm_nope", DN), ("q_norm_rope", DR), ("k_norm_rope", DR)):
                sp.dma_start(HEADW[:, at:at + n], a[name].to_broadcast([P, n])).then_inc(head_in, 16)
                at += n
            sp.dma_start(XTOK[:, :].rearrange("p (t d) -> p t d", t=TT),
                         a["x"][0].rearrange("(t p) d -> p t d", p=P)).then_inc(x_in, 16)
            load_gem(1, gem_src(1))
            load_gem(2, gem_src(2))
            for t in range(3, 8):
                sp.wait_ge(gem_done, t - 2)
                load_gem(t % 3, gem_src(t))
            u, t = U_FFN0, 8
            for c0, chunks in FFN_PARTS:
                load_up(u, w13[0], FF, c0, chunks, t, gem_src)
                u, t = u + 2 * chunks, t + chunks
                load_down(u, w2[0], c0, chunks, t, gem_src)
                u, t = u + KC, t + 2
            for j, cols in enumerate((P, P, P, DR)):
                load_strip(U_LATENT + j, (U_LATENT + j) % RING, w_in[:, :, j * P:j * P + cols])
            i3 = QR + KR + DR
            for part in (0, 2, 1):
                u = U_CONV + 4 * (0, 2, 1)[part]
                load_strips(u, 4, lambda m: w_in[:, :, i3 + part * CW + m * P:i3 + part * CW + (m + 1) * P])
                if part == 0:
                    sp.wait_ge(strip_done, U_LATENT + RING)
                    sp.dma_start(UQ[:, :].rearrange("p (k n) -> p k n", k=2), rows_of(a["w_uq"][0])).then_inc(up_in, 16)
                    sp.dma_start(UKV[:, :], a["w_ukv"][0]).then_inc(up_in, 16)
            load_strips(U_GATE, 2 * KC, lambda m: w_in[:, :, bass.ds(m * P + (i3 + 3 * CW), P)])
            load_strips(U_BRANCH, KC, lambda m: w_branch[:, :, bass.ds(m * P, P)])
            load_strips(U_OUT, KC, lambda m: w_out[:, :, bass.ds(m * P, P)])
            sp.wait_ge(mlo_ready, KC)
            sp.dma_start(CTOK[:, :].rearrange("p (t d) -> p t d", t=2),
                         a["ctx_2"][0].rearrange("(t p) d -> p t d", p=P)).then_inc(ctx_in, 16)
            u, t = U_FFN1, T_ADA
            for i, (c0, chunks) in enumerate(FFN_PARTS):
                load_up(u, w13[1], FF, c0, chunks, t, gem_src2)
                u, t = u + 2 * chunks, t + chunks
                load_down(u, w2[1], c0, chunks, t if i == 0 else None, gem_src2)
                u, t = u + KC, t + (2 if i == 0 else 0)
            load_strips(U_CTX, 8, lambda m: w_in2[:, :, bass.ds(m * P + 10 * P, P)])
            for s, col in enumerate(IN2_COLS):
                load_strip(U_IN2 + s, (U_IN2 + s) % RING, w_in2[:, :, col:col + P])
                if s == 8:
                    sp.wait_ge(strip_done, U_IN2 + 1 + RING)
                    for dst, i in ((TCOS, 0), (TSIN, 1)):
                        sp.dma_start(dst[:, :].rearrange("p (t s) -> p t s", t=TT),
                                     a["dft_tok"][i].rearrange("(t p) s -> p t s", p=P)).then_inc(table_in, 16)
                    sp.dma_start(DFEAT[:, :], a["dft_feat"]).then_inc(table_in, 16)
                    sp.dma_start(MASK[:, :], a["near"].rearrange("p v k -> p (v k)")).then_inc(table_in, 16)
                    sp.dma_start(WF[:, :].rearrange("p (k n) -> p k n", k=2), rows_of(a["w_fourier_2"][0])).then_inc(table_in, 16)
                    sp.dma_start(PW[:, :].rearrange("p (k n) -> p k n", k=2), rows_of(a["conv_pw_w_2"][0])).then_inc(table_in, 16)
            load_strips(U_OUT2, RING, lambda m: w_out2[:, :, bass.ds(m * P, P)])
            sp.wait_ge(strip_done, U_OUT2 + RING)
            sp.wait_ge(rpb_in, 16 * 3)
            for r in range(ROWS):
                src = bass.AP(rpb.tensor, r * RPB_C, [[1, QC], [RPB_R * RPB_C, H], [1, SPAN_IN]])
                sp.dma_start(RPB[r * QC:(r + 1) * QC, 0:H * SPAN_IN].rearrange("p (h c) -> p h c", h=H), src).then_inc(table_in, 16)
            load_strips(U_OUT2 + RING, RING, lambda m: w_out2[:, :, bass.ds((m + RING) * P, P)])
            for part in range(MLP_PARTS):
                u = U_MLP + 2 * KC * part
                load_strips(u, KC, lambda m: w_mlp1[:, :, bass.ds(m * P + part * D, P)])
                load_strips(u + KC, KC, lambda m: w_mlp2[:, part * KC:(part + 1) * KC, bass.ds(m * P, P)])
            for t in range(TT):
                sp.wait_ge(ytok_ready, 2 * t + 2)
                sp.dma_start(out[0, t * P:(t + 1) * P, :], YTOK[:, t * D:(t + 1) * D]).then_inc(out_done, 16)
            sp.wait_ge(out_done, 16 * TT)

        @block.gpsimd
        def _(pool):
            pool.memset(IDENT[:, :], 0.0).then_inc(pool_seq, 1)
            pool.memset(ONES[:, :], 1.0).then_inc(const_ready, 1)
            pool.memset(CONST[:, 0:1], EPS).then_inc(const_ready, 1)
            pool.memset(CONST[:, 1:2], LN_EPS).then_inc(const_ready, 1)
            pool.memset(RPB[:, H * SPAN_IN:], 0.0)
            pool.memset(SSUM[:, :], 0.0).then_inc(pool_seq, 1)
            pool.wait_ge(pool_seq, 1)
            pool.affine_select(out=IDENT[:, :], in_=IDENT[:, :], compare_op=ALU.not_equal, fill=1.0, base=0,
                               pattern=[[-1, P]], channel_multiplier=1).then_inc(ident_ready, 1)
            pool.memset(FLIP[:, :], 0.0).then_inc(pool_seq, 1)
            pool.wait_ge(pool_seq, 3)
            pool.affine_select(out=FLIP[:, :], in_=FLIP[:, :], compare_op=ALU.not_equal, fill=1.0, base=1 - P,
                               pattern=[[1, P]], channel_multiplier=1).then_inc(flip_ready, 1)
            sq, seq = Tally(sq_ready), Tally(pool_seq)
            seq.n = 3

            def sum_squares(clear):
                if clear:
                    pool.wait_ge(stat_ready, clear)
                    pool.memset(SSUM[:, :], 0.0).then_inc(pool_seq, 1)
                    seq.add()
                pool.wait_ge(pool_seq, seq.n)
                with loop(pool, KC // 2, (sq, 2), (seq, 2)) as _:
                    for j in range(2):
                        pool.wait_ge(sq_ready, sq.add())
                        pool.tensor_tensor(SSUM[:, :], SSUM[:, :], SQ[:, j * S:(j + 1) * S], ALU.add).then_inc(pool_seq, 1)
                        pool.wait_ge(pool_seq, seq.add())
                        pool.sem_inc(sq_used, 1)

            sum_squares(0)
            for norms in range(1, 4):
                sum_squares(norms)
            pool.wait_ge(stat_ready, 4)
            pool.memset(QZ[:, :], 0.0).then_inc(zeros_ready, 1)
            for norms in range(4, 6):
                sum_squares(norms)
        @block.tensor
        def _(pe):
            def wait_strip(u):
                pe.wait_ge(lo_ready, u + (1 + RING))
                pe.wait_ge(bank_free, u + 1)

            def products(dst, slot, blocks, hi, lo, n, cols=P, first=True, last=True):
                for i, (b, k) in enumerate(blocks):
                    w_hi = W_HI[:, slot * STRIP + b * cols:slot * STRIP + (b + 1) * cols]
                    w_lo = W_LO[:, slot * STRIP + b * cols:slot * STRIP + (b + 1) * cols]
                    x_hi, x_lo = hi[:, k * n:(k + 1) * n], lo[:, k * n:(k + 1) * n]
                    pe.matmul(dst, w_hi, x_hi, start=first and i == 0, stop=False)
                    pe.matmul(dst, w_hi, x_lo, start=False, stop=False)
                    mm = pe.matmul(dst, w_lo, x_hi, start=False, stop=last and i == len(blocks) - 1)
                return mm

            def strip(u, slot, hi, lo, chunks=KC, n=S, cols=P, each=None):
                wait_strip(u)
                for k in range(chunks):
                    if each is not None:
                        pe.wait_ge(each[0], each[1] + k + 1)
                    mm = products(bank[slot][0:cols, 0:n], slot, [(k, k)], hi, lo, n, cols,
                                  first=k == 0, last=k == chunks - 1)
                mm.then_inc(strip_done, 1)

            def strips(u0, count, hi, lo, chunks=KC, n=S, each=None):
                with loop(pe, count // RING) as it:
                    for j in range(RING):
                        strip(it * RING + (u0 + j), (u0 + j) % RING, hi, lo, chunks, n, each=each if j == 0 else None)

            sq = Tally(sq_used)
            h, alo = Tally(h_ready), Tally(alo_ready)
            h.n = alo.n = 2
            pe.sem_inc(strip_done, RING)

            def stat():
                pe.wait_ge(sq_used, sq.add(KC))
                pe.matmul(bank[4][:, :], ONES[:, :], SSUM[:, :], start=True, stop=True).then_inc(stat_ready, 1)

            def fold(c0, c1, tiles):
                pe.wait_ge(gem_done, tiles)
                for r in range(4):
                    mm = pe.matmul(bank[5][32 * r:32 * r + 32, c0:c1], SUM32[:, :],
                                   FOLDED[:, 4 * c0 + r:4 * c1:4], start=True, stop=True)
                mm.then_inc(mod_summed, 1)

            def normed():
                return h_ready, h.add(KC) - KC

            def widened(chunks):
                return alo_ready, alo.add(chunks) - chunks

            def ffn(u, parts):
                for i, (_, chunks) in enumerate(parts):
                    strips(u, 2 * chunks, H_HI, H_LO, each=normed() if i == 0 else None)
                    u += 2 * chunks
                    if u == U_FFN0 + 2 * parts[0][1]:
                        fold(16, 24, 12)
                    strips(u, KC, A_HI, A_LO, chunks, each=widened(chunks))
                    u += KC
                    if u == U_FFN1 + 2 * parts[0][1] + KC:
                        context()

            def attend(n0, scores, keys, prob, pt, values):
                for n in range(TT * H + 3):
                    if n < TT * H:
                        if n >= 4:
                            pe.wait_ge(exp_done, n0 + n - 3)
                        for dst, q, k in scores(n, bank[n % 4]):
                            mm = pe.matmul(dst, q, k, start=True, stop=True)
                        mm.then_inc(score_done, 1)
                    if 0 <= n - 2 < TT * H:
                        m = n - 2
                        pe.wait_ge(prob_ready, n0 + m + 1)
                        if m >= 2:
                            pe.wait_ge(pt_ready, n0 + m - 1)
                        for k in range(keys(m)):
                            mm = pe.transpose(bank[4 + m % 2][:, k * P:(k + 1) * P],
                                              prob[:, m % 4 * S + k * P:m % 4 * S + (k + 1) * P], IDENT[:, :])
                        mm.then_inc(prob_turned, 1)
                    if n >= 3:
                        m = n - 3
                        h, i = m // TT, m % TT
                        pe.wait_ge(pt_ready, n0 + m + 1)
                        if h >= 4 and h % 2 == 0 and i == 0:
                            pe.wait_ge(olo_ready, (n0 // TT + h) // 2 - 1)
                        for k in range(keys(m)):
                            mm = pe.matmul(bank[6 + h // 2 % 2][DV * (h % 2):DV * (h % 2) + DV, i * P:(i + 1) * P],
                                           values(m, k), pt[:, m % 2 * S + k * P:m % 2 * S + (k + 1) * P],
                                           start=k == 0, stop=k == keys(m) - 1)
                        mm.then_inc(pv_done, 1)
                pe.wait_ge(exp_done, n0 + TT * H)
                pe.wait_ge(olo_ready, (n0 // TT + H) // 2)

            def mixer1():
                fold(24, 72, T_ADA)
                stat()
                each = normed()
                for j, cols in enumerate((P, P, P, DR)):
                    strip(U_LATENT + j, (U_LATENT + j) % RING, H_HI, H_LO, cols=cols, each=each if j == 0 else None)
                strips(U_CONV, 4, H_HI, H_LO)
                pe.wait_ge(lat_sq, 3)
                pe.matmul(bank[4][:, :], ONES[:, :], SQ[:, 0:S], start=True, stop=False)
                pe.matmul(bank[4][:, :], ONES[:, :], SQ[:, S:2 * S], start=False, stop=True)
                pe.matmul(bank[5][:, :], ONES[:, :], UN[:, 0:S], start=True, stop=True).then_inc(lat_sum, 1)
                pe.wait_ge(bank_free, U_CONV + RING)
                for t in range(TT):
                    mm = pe.transpose(bank[6][:, t * DR:(t + 1) * DR], KRF[:, t * P:(t + 1) * P], IDENT[0:DR, 0:DR])
                mm.then_inc(kr_turned, 1)
                strips(U_CONV + 4, 8, H_HI, H_LO)
                pe.wait_ge(up_in, 32)
                pe.wait_ge(lat_ready, 1)
                half = H * DQ // 2
                for n in range(3 * TT):
                    b = bank[4 + n % 4]
                    if n >= 4:
                        pe.wait_ge(up_read, n - 3)
                    if n < 2 * TT:
                        t, c = n // 2, n % 2 * half
                        for k in range(2):
                            mm = pe.matmul(b[:, 0:half], CQT[:, k * S + t * P:k * S + (t + 1) * P],
                                           UQ[:, k * H * DQ + c:k * H * DQ + c + half], start=k == 0, stop=k == 1)
                    else:
                        t = n - 2 * TT
                        mm = pe.matmul(b[:, :], CKVT[:, t * P:(t + 1) * P],
                                       UKV[:, :].rearrange("p (h d) -> p h d", h=H)[:, :, 0:DN], start=True, stop=True)
                    mm.then_inc(up_done, 1)
                strips(U_GATE, 2 * KC, H_HI, H_LO)
                pe.wait_ge(k_ready, TT)
                for n in range(2 * H + TT):
                    b = bank[4 + n % 4]
                    if n >= 4:
                        pe.wait_ge((turn_act, turn_dve)[n % 2], n // 2 - 1)
                    if n < 2 * H:
                        for t in range(TT):
                            at = (t * H + n // 2) * DQ
                            mm = pe.transpose(b[0:DQ, t * P:(t + 1) * P], (QTOK, KTOK)[n % 2][:, at:at + DQ], IDENT[:, :])
                    else:
                        t = n - 2 * H
                        mm = pe.matmul(b[:, :], CKVT[:, t * P:(t + 1) * P],
                                       UKV[:, :].rearrange("p (h d) -> p h d", h=H)[:, :, DN:], start=True, stop=True)
                    mm.then_inc(turned, 1)
                pe.wait_ge(turn_act, H + TT // 2)
                pe.wait_ge(turn_dve, H + TT // 2)
                pe.wait_ge(bank_free, U_BRANCH + RING)
                attend(0, lambda n, dst: [(dst[:, 0:(n % TT + 1) * P],
                                           QT[:, n // TT * S + n % TT * P:n // TT * S + (n % TT + 1) * P],
                                           KT[:, n // TT * S:n // TT * S + (n % TT + 1) * P])],
                       lambda n: n % TT + 1, PROB, PT,
                       lambda n, k: V[:, (k * H + n // TT) * DV:(k * H + n // TT + 1) * DV])
                with loop(pe, KC // RING) as it:
                    for j in range(RING):
                        u = it * RING + (U_BRANCH + j)
                        slot = (U_BRANCH + j) % RING
                        wait_strip(u)
                        products(bank[slot][:, :], slot, [(k, k) for k in range(4)], A_HI, A_LO, S)
                        products(bank[4 + slot][:, :], slot, [(k, k) for k in range(4, KC)], A_HI, A_LO, S).then_inc(strip_done, 1)
                strips(U_OUT, KC, H_HI, H_LO, each=(mlo_ready, 0))

            def context():
                fold(M_CTX, M_COLS, T_ADA + KC)
                pe.wait_ge(ctx_ready, 2)
                for i, b in enumerate((4, 6, 7, 5)):
                    if b == 5:
                        pe.wait_ge(ctx_mod, 1)
                    for k in (2 * i, 2 * i + 1):
                        for t in range(2):
                            mm = pe.transpose(bank[b][:, k % 2 * CTX + t * P:k % 2 * CTX + (t + 1) * P],
                                              CTOK[:, t * D + k * P:t * D + (k + 1) * P], IDENT[:, :])
                    mm.then_inc(ctx_turned, 1)

            def mixer2():
                pe.wait_ge(clo_ready, KC)
                strips(U_CTX, 4, C_HI, C_LO, n=CTX)
                fold(M_2, M_CTX, T_2)
                stat()
                strips(U_CTX + 4, 4, C_HI, C_LO, n=CTX)
                each = normed()
                def turn_values(c):
                    for n in (2 * c, 2 * c + 1):
                        if n >= 4:
                            pe.wait_ge((vw_act, vw_dve)[n % 2], n // 2 - 1)
                        for i in range(4):
                            tile = n % 2 * 4 + i
                            mm = pe.transpose(bank[4 + n % 4][:, i * P:(i + 1) * P],
                                              VT[:, (c % 2 * 8 + tile) * P:(c % 2 * 8 + tile + 1) * P], IDENT[:, :])
                        mm.then_inc(vw_turned, 1)

                for s in range(len(IN2_COLS)):
                    strip(U_IN2 + s, (U_IN2 + s) % RING, H_HI, H_LO, each=each if s == 0 else None)
                    if s >= 15:
                        pe.wait_ge(bank_free, U_IN2 + s + RING)
                        turn_values(s - 15)
                pe.wait_ge(table_in, 16 * 6)
                pe.wait_ge(bank_free, U_OUT2 + RING)
                for t in range(TT):
                    for c in range(2):
                        mm = pe.matmul(bank[t][:, c * 2 * P:(c + 1) * 2 * P], UT[:, c * S + t * P:c * S + (t + 1) * P],
                                       DFEAT[:, :], start=True, stop=True)
                    mm.then_inc(uc_done, 1)
                turn_values(3)
                for t in range(2):
                    pe.wait_ge((vw_act, vw_dve)[t], 3)
                    for c in range(4):
                        mm = pe.transpose(bank[4 + t][:, c * P:(c + 1) * P], VTC[:, c * CTX + t * P:c * CTX + (t + 1) * P],
                                          IDENT[:, :])
                    mm.then_inc(vw_turned, 1)
                pe.wait_ge(vw_act, 5)
                pe.wait_ge(vw_dve, 5)
                pe.wait_ge(conv_ready, 2)
                for c in range(2):
                    mm = pe.matmul(bank[4][:, :], ONES[:, :], chunk(ACC, c), start=c == 0, stop=c == 1)
                mm.then_inc(ln_sum, 1)
                pe.wait_ge(uc_act, 2)
                pe.wait_ge(uc_dve, 2)
                for c in range(2):
                    for t in range(TT):
                        for i, table in enumerate((TCOS, TSIN)):
                            at = t * S + (2 * c + i) * P
                            mm = pe.matmul(bank[c][:, :], UC[:, at:at + P], chunk(table, t),
                                           start=t + i == 0, stop=t + i == TT)
                    mm.then_inc(ft_done, 1)
                pe.wait_ge(ln_sq, 2)
                for c in range(2):
                    mm = pe.matmul(bank[4][:, :], ONES[:, :], chunk(CSQ, c), start=c == 0, stop=c == 1)
                mm.then_inc(ln_sum, 1)
                pe.wait_ge(flip_ready, 1)
                pe.wait_ge(table_in, 16 * (6 + ROWS))
                for h in range(H):
                    if h >= 3:
                        pe.wait_ge(bias_ready, h - 2)
                    pe.matmul(bank[5 + h % 3][:, 0:SPAN], FLIP[:, :], RPB[:, h * SPAN_IN:h * SPAN_IN + SPAN],
                              start=True, stop=True).then_inc(rpb_turned, 1)
                pe.wait_ge(ft_act, 1)
                pe.wait_ge(ft_dve, 1)
                for m in range(2):
                    for c in range(2):
                        mm = pe.matmul(bank[2 + m][:, :], WF[:, (2 * c + m) * P:(2 * c + m + 1) * P], chunk(FT, c),
                                       start=c == 0, stop=c == 1)
                    mm.then_inc(mix_done, 1)
                pe.wait_ge(act_ready, 2)
                for m in range(2):
                    for c in range(2):
                        mm = pe.matmul(bank[m][:, :], PW[:, (2 * c + m) * P:(2 * c + m + 1) * P], chunk(ACC, c),
                                       start=c == 0, stop=c == 1)
                    mm.then_inc(mix_done, 1)
                pe.wait_ge(bias_ready, H)
                pe.wait_ge(mixed, 8)

                def scores(n, dst):
                    h, j = n // TT, n % TT
                    c = h // 2
                    q = QZ[:, h * S + j * P:h * S + (j + 1) * P]
                    near = KT2[:, c * KEYS:c * KEYS + S].rearrange("p (r c) -> p r c", r=ROWS)[:, :, NEAR[j]:NEAR[j] + KW]
                    return [(dst[:, 0:CTX], q, near), (dst[:, CTX:], q, KT2[:, c * KEYS + S:(c + 1) * KEYS])]

                def values(n, k):
                    h, j = n // TT, n % TT
                    if k < 2:
                        return VW[:, ((2 * j + k) * H + h) * DH:((2 * j + k) * H + h + 1) * DH]
                    return VC[:, ((k - 2) * H + h) * DH:((k - 2) * H + h + 1) * DH]

                attend(TT * H, scores, lambda n: 4, PROB2, PT2, values)
                strips(U_OUT2, KC, A_HI, A_LO)

            def mlp():
                stat()
                for part in range(MLP_PARTS):
                    u = U_MLP + 2 * KC * part
                    strips(u, KC, H_HI, H_LO, each=normed() if part == 0 else None)
                    strips(u + KC, KC, A_HI, A_LO, each=widened(KC))

            pe.wait_ge(ident_ready, 1)
            pe.wait_ge(rows_in, 16 * 17)
            for b, rows, dst in ((4, ROWS1, V_ROWS), (5, ROWS2, M_CTX), (6, ROWS3, 2 * CK2)):
                pe.transpose(bank[b][:, 0:dst], rows[:, :], IDENT[0:dst, 0:dst]).then_inc(cols_turned, 1)
            pe.wait_ge(x_in, 16)
            for k in range(KC):
                if k >= 2:
                    pe.wait_ge(x_ready, k - 1)
                for t in range(TT):
                    mm = pe.transpose(bank[k % 2][:, t * P:(t + 1) * P], XTOK[:, t * D + k * P:t * D + (k + 1) * P],
                                      IDENT[:, :])
                mm.then_inc(x_turned, 1)
            pe.wait_ge(const_ready, 3)
            stat()
            pe.wait_ge(cols_ready, 4)
            fold(0, 16, 8)
            ffn(U_FFN0, FFN_PARTS)
            mixer1()
            stat()
            ffn(U_FFN1, FFN_PARTS)
            mixer2()
            mlp()
            stat()
            for t in range(TT):
                for half in range(2):
                    if t:
                        pe.wait_ge(ytok_ready, 2 * t)
                    for i in range(4):
                        k = 4 * half + i
                        if t == 0:
                            pe.wait_ge(y_ready, k + 1)
                        mm = pe.transpose(bank[6 + half][:, i * P:(i + 1) * P],
                                          YT[:, k * S + t * P:k * S + (t + 1) * P], IDENT[:, :])
                    mm.then_inc(y_turned, 1)

        @block.scalar
        def _(act):
            def split_hi(u, slot, turn):
                act.wait_ge(raw_in[slot], turn * 16 + 16)
                act.wait_ge(strip_done, u + 1)
                act.activation(strip_of(W_HI, slot), strip_of(RAW, slot), ACT.Copy).then_inc(hi_ready, 1)

            def split_next(u0, it, j):
                u = u0 + j + LEAD
                if not isinstance(it, int) or it * RING + u < STRIPS:
                    split_hi(it * RING + u, u % RING, it + u // RING)

            silu, ahi, un = Tally(silu_ready), Tally(ahi_ready), Tally(un_ready)
            std, nhi, hsum = Tally(stat_ready), Tally(nhi_ready), Tally(head_sum)

            def square(k, j):
                act.activation(SQ[:, j * S:(j + 1) * S], chunk(X, k), ACT.Square).then_inc(sq_ready, 1)

            def norm(shift, between=None):
                act.wait_ge(stat_ready, std.add())
                act.activation(RINV[:, :], bank[4][:, :], ACT.Sqrt, bias=CONST[:, 0:1], scale=1.0 / D).then_inc(std_ready, 1)

                def pair(it):
                    for j in range(2):
                        act.wait_ge(un_ready, un.add())
                        act.activation(chunk(H_HI, it * 2 + j), UN[:, j * S:(j + 1) * S], ACT.Identity,
                                       bias=MOD[:, bass.ds(it * 2 + (shift + j), 1)]).then_inc(nhi_ready, 1)

                if between is not None:
                    for i in range(KC // 2):
                        pair(i)
                        between(i)
                    return
                with loop(act, KC // 2, (un, 2)) as it:
                    pair(it)

            def ffn_up(u0, chunks):
                with loop(act, chunks // 2) as it:
                    for p in range(2):
                        split_next(u0, it, 2 * p)
                        split_next(u0, it, 2 * p + 1)
                        g = u0 + 2 * p
                        act.wait_ge(strip_done, it * RING + (g + 1 + RING))
                        act.activation(SG[:, p * S:(p + 1) * S], bank[g % RING][:, :], ACT.Silu).then_inc(silu_ready, 1)
                        act.wait_ge(bank_free, it * RING + (g + 2 + RING))
                        act.activation(chunk(A_HI, it * 2 + p), HF[:, p * S:(p + 1) * S], ACT.Copy).then_inc(ahi_ready, 1)

            def down(u0, squares):
                def turn(it):
                    for j in range(RING):
                        split_next(u0, it, j)
                        if squares:
                            act.wait_ge(bank_free, it * RING + (u0 + j + 1 + RING))
                            act.wait_ge(sq_used, squares + (it * RING + j) - 1)
                            square(it * RING + j, j % 2)

                if u0 + KC == STRIPS:
                    for it in range(KC // RING):
                        turn(it)
                    return
                with loop(act, KC // RING) as it:
                    turn(it)

            def attend(n0, keys, scale, prob, pt, output):
                for n in range(TT * H + 4):
                    if n < TT * H:
                        act.wait_ge(neg_ready, n0 + n + 1)
                        if n >= 4:
                            act.wait_ge(prob_turned, n0 + n - 3)
                        act.activation(prob[:, n % 4 * S:n % 4 * S + keys(n)], bank[n % 4][:, 0:keys(n)], ACT.Exp,
                                       bias=soft(n, 1), scale=scale, accum_out=soft(n, 2)).then_inc(exp_done, 1)
                    if 0 <= n - 2 < TT * H:
                        m = n - 2
                        act.wait_ge(prob_turned, n0 + m + 1)
                        if m >= 2:
                            act.wait_ge(pv_done, n0 + m - 1)
                        act.activation(pt[:, m % 2 * S:m % 2 * S + keys(m)], bank[4 + m % 2][:, 0:keys(m)],
                                       ACT.Copy).then_inc(pt_ready, 1)
                    if n >= 4 and (n - 3) % (2 * TT) == 0:
                        c = (n - 3) // (2 * TT) - 1
                        act.wait_ge(pv_done, n0 + (c + 1) * 2 * TT)
                        output(c, bank[6 + c % 2][:, :]).then_inc(ohi_ready, 1)

            def mixer1():
                norm(24)
                for j in range(4):
                    split_next(U_LATENT, 0, j)
                    if j < 3:
                        act.wait_ge(bank_free, U_LATENT + j + 1 + RING)
                        act.activation((SQ[:, 0:S], SQ[:, S:2 * S], UN[:, 0:S])[j],
                                       (CQT[:, 0:S], CQT[:, S:2 * S], CKVT[:, :])[j], ACT.Square).then_inc(lat_sq, 1)
                for j in range(4):
                    split_next(U_CONV, 0, j)
                act.wait_ge(lat_sum, 1)
                act.activation(UN[:, S:2 * S], bank[4][:, :], ACT.Sqrt, bias=CONST[:, 0:1], scale=1.0 / QR).then_inc(lat_std, 1)
                act.activation(RINV[:, :], bank[5][:, :], ACT.Sqrt, bias=CONST[:, 0:1], scale=1.0 / KR).then_inc(lat_std, 1)
                with loop(act, 2) as it:
                    for j in range(4):
                        split_next(U_CONV + 4, it, j)
                act.wait_ge(angle_ready, 1)
                act.activation(SIN[:, :], ANGLE[:, TT * DR // 2:TT * DR], ACT.Sin).then_inc(sin_ready, 1)
                act.activation(COS[:, :], ANGLE[:, TT * DR:], ACT.Sin).then_inc(sin_ready, 1)
                half = H * DQ // 2
                for n in range(3 * TT):
                    act.wait_ge(up_done, n + 1)
                    if n < 2 * TT:
                        act.activation(chunk(QTOK, n, half), bank[4 + n % 4][:, 0:half], ACT.Copy).then_inc(up_read, 1)
                    else:
                        act.activation(heads(chunk(KTOK, n - 2 * TT, H * DQ))[:, :, 0:DN],
                                       bank[4 + n % 4][:, :].rearrange("p (h d) -> p h d", h=H), ACT.Copy).then_inc(up_read, 1)
                act.wait_ge(bank_free, U_GATE + RING)
                act.wait_ge(mixed, 4)
                act.wait_ge(up_read, 3 * TT)
                with loop(act, TT, (hsum, 1)) as t:
                    act.activation(TQ0[:, :], chunk(QTOK, t, H * DQ), ACT.Square).then_inc(head_sq, 1)
                    act.activation(TQ1[:, 0:H * DN], heads(chunk(KTOK, t, H * DQ))[:, :, 0:DN], ACT.Square).then_inc(head_sq, 1)
                    act.activation(TQ1[:, H * DN:H * DN + DR], chunk(KRT, t, DR), ACT.Square).then_inc(head_sq, 1)
                    for j in range(RING):
                        split_next(U_GATE, t, j)
                        act.wait_ge(strip_done, t * RING + (U_GATE + j + 1 + RING))
                        act.activation(chunk(GATES, t * RING + j), bank[(U_GATE + j) % RING][:, :],
                                       ACT.Sigmoid).then_inc(bank_free, 1)
                        if j == 0:
                            act.wait_ge(head_sum, hsum.add())
                            act.activation(STAT[:, 0:2 * H], STAT[:, 0:2 * H], ACT.Sqrt, bias=CONST[:, 0:1],
                                           scale=1.0 / DN).then_inc(head_std, 1)
                            act.activation(STAT[:, 2 * H:3 * H + 1], STAT[:, 2 * H:3 * H + 1], ACT.Sqrt, bias=CONST[:, 0:1],
                                           scale=1.0 / DR).then_inc(head_std, 1)
                for n in range(0, 2 * H + TT, 2):
                    act.wait_ge(turned, n + 1)
                    if n < 2 * H:
                        ins = act.activation(chunk(QT, n // 2), bank[4 + n % 4][0:DQ, :], ACT.Copy)
                    else:
                        ins = act.activation(chunk(V, n - 2 * H), bank[4 + n % 4][:, :], ACT.Copy)
                    ins.then_inc(turn_act, 1)
                attend(0, lambda n: (n % TT + 1) * P, DQ ** -0.5, PROB, PT,
                       lambda c, src: act.activation(chunk(A_HI, c), src, ACT.Copy))
                with loop(act, KC // RING) as it:
                    for j in range(RING):
                        split_next(U_BRANCH, it, j)
                        act.wait_ge(merged, it * RING + (j + 1))
                        act.activation(chunk(H_HI, it * RING + j), UN[:, j % 2 * S:(j % 2 + 1) * S], ACT.Copy).then_inc(mhi_ready, 1)
                down(U_OUT, 2 * KC)

            def mixer2():
                for j in range(4):
                    split_next(U_CTX, 0, j)
                norm(M_2, lambda i: split_next(U_CTX + 4, 0, i))

                def turned_values(n):
                    act.wait_ge(vw_turned, n + 1)
                    act.activation(window_values(n), window_bank(n), ACT.Copy).then_inc(vw_act, 1)

                for s in range(len(IN2_COLS)):
                    u = U_IN2 + s
                    split_next(U_IN2, 0, s)
                    src = bank[u % RING]
                    if s in (2, 4):
                        act.wait_ge(strip_done, u + 1 + RING)
                        p = s // 2 - 1
                        act.activation(SQ[:, p * S:(p + 1) * S], src[:, :], ACT.Sigmoid).then_inc(sig_ready, 1)
                    if s == 6:
                        act.wait_ge(bank_free, u + RING)
                        act.wait_ge(zeros_ready, 1)
                    if s >= 6:
                        act.wait_ge(strip_done, u + 1 + RING)
                        part, c = (s - 6) // 4, (s - 6) % 4
                        if part == 0:
                            for i in range(2):
                                rows = slice(DH * i, DH * i + DH)
                                ins = act.activation(
                                    by_tiles(chunk(QZ, 2 * c + i)[rows, :]), by_rows(src[rows, :]), ACT.Copy, scale=DH ** -0.5)
                        elif part == 1:
                            ins = act.activation(KT2[:, c * KEYS:c * KEYS + S], src[:, :], ACT.Copy)
                        else:
                            if c >= 2:
                                act.wait_ge(vw_turned, 2 * c - 2)
                            for j in range(TT):
                                ins = act.activation(
                                    chunk(VT, c % 2 * TT + j, ROWS * KW).rearrange("p (r c) -> p r c", r=ROWS),
                                    src[:, :].rearrange("p (r c) -> p r c", r=ROWS)[:, :, NEAR[j]:NEAR[j] + KW], ACT.Copy)
                        ins.then_inc(bank_free, 1)
                        if s >= 15:
                            turned_values(2 * (s - 15))
                for t in (0, 2):
                    act.wait_ge(uc_done, t + 1)
                    act.activation(chunk(UC, t), bank[t][:, :], ACT.Copy).then_inc(uc_act, 1)
                for n in (6, 8):
                    turned_values(n)
                for c in range(2):
                    act.wait_ge(dev_ready, c + 1)
                    act.activation(chunk(CSQ, c), chunk(ACC, c), ACT.Square).then_inc(ln_sq, 1)
                act.wait_ge(ft_done, 2)
                act.activation(chunk(FT, 0), bank[0][:, :], ACT.Copy).then_inc(ft_act, 1)
                act.wait_ge(ln_sum, 2)
                act.activation(bank[4][:, :], bank[4][:, :], ACT.Sqrt, bias=CONST[:, 1:2], scale=1.0 / CW2).then_inc(ln_std, 1)
                for c in range(2):
                    act.wait_ge(z_ready, c + 1)
                    act.activation(chunk(ACC, c), chunk(ACC, c), ACT.Silu, bias=COL1[:, V_LNB + c:V_LNB + c + 1],
                                   scale=COL1[:, V_LNG + c:V_LNG + c + 1]).then_inc(act_ready, 1)
                for m in range(4):
                    act.wait_ge(mix_done, m + 1)
                    if m < 2:
                        ins = act.activation(chunk(A_HI, m), bank[2 + m][:, :], ACT.Copy)
                    else:
                        ins = act.activation(chunk(A_HI, m), bank[m - 2][:, :], ACT.Identity,
                                             bias=COL1[:, V_PWB + m - 2:V_PWB + m - 1])
                    ins.then_inc(mix_hi, 1)
                attend(TT * H, lambda n: S, 1.0, PROB2, PT2,
                       lambda c, src: act.activation(by_rows(chunk(A_HI, 4 + c)), by_tiles(src), ACT.Copy))
                down(U_OUT2, 4 * KC)

            def mlp():
                norm(M_2 + 3 * KC)
                for part in range(MLP_PARTS):
                    u = U_MLP + 2 * KC * part
                    with loop(act, KC // RING) as it:
                        for j in range(RING):
                            split_next(u, it, j)
                            act.wait_ge(strip_done, it * RING + (u + j + 1 + RING))
                            act.activation(SG[:, j % 2 * S:(j % 2 + 1) * S], bank[(u + j) % RING][:, :],
                                           ACT.Relu).then_inc(silu_ready, 1)
                            act.wait_ge(bank_free, it * RING + (u + j + 1 + RING))
                            act.activation(chunk(A_HI, it * RING + j), HF[:, j % 2 * S:(j % 2 + 1) * S],
                                           ACT.Copy).then_inc(ahi_ready, 1)
                    down(u + KC, 5 * KC if part == MLP_PARTS - 1 else 0)

            act.wait_ge(cols_ready, 1)
            act.activation(CSIL[:, :], COL1[:, V_C:V_C + 3 * KC], ACT.Silu).then_inc(cond_ready, 1)
            for k in range(KC):
                act.wait_ge(x_ready, k + 1)
                if k >= 2:
                    act.wait_ge(sq_used, k - 1)
                square(k, k % 2)
            for u in range(LEAD):
                act.wait_ge(raw_in[u], 16)
                act.activation(strip_of(W_HI, u), strip_of(RAW, u), ACT.Copy).then_inc(hi_ready, 1)
            act.wait_ge(mod_ready, 1)
            norm(0)
            u = U_FFN0
            for i, (_, chunks) in enumerate(FFN_PARTS):
                ffn_up(u, chunks)
                u += 2 * chunks
                down(u, KC if i == 2 else 0)
                u += KC
            mixer1()
            norm(48)
            u = U_FFN1
            for i, (_, chunks) in enumerate(FFN_PARTS):
                ffn_up(u, chunks)
                u += 2 * chunks
                if i == 0:
                    act.wait_ge(ctx_in, 16)
                    for t in range(2):
                        act.activation(SQ[:, :], CTOK[:, t * D:(t + 1) * D], ACT.Square,
                                       accum_out=STAT[:, 200 + t:201 + t]).then_inc(ctx_sq, 1)
                        act.wait_ge(ctx_sq, t + 1)
                    act.activation(STAT[:, 200:202], STAT[:, 200:202], ACT.Sqrt, bias=CONST[:, 0:1],
                                   scale=1.0 / D).then_inc(ctx_std, 1)
                down(u, 3 * KC if i == 2 else 0)
                u += KC
                if i == 0:
                    for k in range(KC):
                        act.wait_ge(ctx_full, k + 1)
                        act.activation(chunk(C_HI, k, CTX), chunk(HF, k % 4, CTX), ACT.Copy).then_inc(chi_ready, 1)
            mixer2()
            mlp()
            act.wait_ge(stat_ready, std.add())
            act.activation(RINV[:, :], bank[4][:, :], ACT.Sqrt, bias=CONST[:, 0:1], scale=1.0 / D).then_inc(std_ready, 1)
            for t in range(TT):
                act.wait_ge(y_turned, 2 * t + 1)
                act.activation(YTOK[:, t * D:t * D + S], bank[6][:, :], ACT.Copy).then_inc(ytok_ready, 1)

        @block.vector
        def _(dve):
            seq = Tally(dve_seq)

            def after(ins):
                ins.then_inc(dve_seq, 1)
                dve.wait_ge(dve_seq, seq.add())

            def split_lo(u, slot):
                dve.wait_ge(hi_ready, u + 1)
                dve.tensor_tensor(strip_of(W_LO, slot), strip_of(RAW, slot), strip_of(W_HI, slot).bitcast(F32),
                                  ALU.subtract).then_inc(lo_ready, 1)

            def split_next(u0, it, j):
                u = u0 + j + LEAD
                if not isinstance(it, int) or it * RING + u < STRIPS:
                    split_lo(it * RING + u, u % RING)

            silu, ahi, nhi, std = Tally(silu_ready), Tally(ahi_ready), Tally(nhi_ready), Tally(std_ready)
            hsq, hstd = Tally(head_sq), Tally(head_std)
            gem_seq = KC + 1
            h_own, alo_own = Tally(h_ready), Tally(alo_ready)
            h_own.n = alo_own.n = 2
            gem_of = [Tally(gem_in[i]) for i in range(3)]

            def gem_tile(slot, vec, at):
                g = GBUF[:, slot * KC * GEM:(slot + 1) * KC * GEM]
                after(dve.tensor_scalar(GACC[:, :], g[:, 0:GEM], CSIL[:, vec:vec + 1], None, ALU.mult))
                for k in range(1, KC):
                    after(dve.scalar_tensor_tensor(out=GACC[:, :], in0=g[:, k * GEM:(k + 1) * GEM],
                                                   scalar=CSIL[:, vec + k:vec + k + 1], in1=GACC[:, :],
                                                   op0=ALU.mult, op1=ALU.add))
                after(dve.transpose(GTURN[:, :], GACC[:, :]))
                return dve.tensor_reduce(FOLDED[:, bass.ds(at * FOLD, FOLD)],
                                         GTURN[:, :].rearrange("p (b i) -> p b i", i=32), AX.X, ALU.add)

            def gem_step(slot, vec, at, also=None):
                dve.wait_ge(gem_in[slot], gem_of[slot].add(16))
                if not isinstance(at, int) or at:
                    dve.wait_ge(gem_done, at)
                if also is not None:
                    after(gem_tile(slot, also, at + (T_2 - T_ADA)))
                gem_tile(slot, vec, at).then_inc(gem_done, 1)

            summed = [0]

            def mod_columns(c0, c1, bias):
                summed[0] += 1
                dve.wait_ge(mod_summed, summed[0])
                after(dve.tensor_tensor(MOD[:, c0:c1], bank[5][:, c0:c1], COL2[:, bias:bias + c1 - c0], ALU.add))

            def factors(dst, scale, weight):
                return dve.scalar_tensor_tensor(out=AMOD[:, dst:dst + KC], in0=MOD[:, scale:scale + KC], scalar=1.0,
                                                in1=COL1[:, weight:weight + KC], op0=ALU.add, op1=ALU.mult)

            def half_gate(i):
                return dve.tensor_scalar(GHALF[:, i * KC:(i + 1) * KC], MOD[:, i * 24 + 16:i * 24 + 24], 0.5, None, ALU.mult)

            def norm(factor, shift, between=None):
                dve.wait_ge(std_ready, std.add())
                after(dve.reciprocal(RINV[:, :], RINV[:, :]))

                def pair(it):
                    dve.wait_ge(h_ready, h_own.add(0))
                    h_own.add(2)
                    for j in range(2):
                        dve.scalar_tensor_tensor(out=UN[:, j * S:(j + 1) * S], in0=chunk(X, it * 2 + j),
                                                 scalar=AMOD[:, bass.ds(it * 2 + (factor + j), 1)], in1=RINV[:, :],
                                                 op0=ALU.mult, op1=ALU.mult).then_inc(un_ready, 1)
                    for j in range(2):
                        dve.wait_ge(nhi_ready, nhi.add())
                        dve.scalar_tensor_tensor(out=chunk(H_LO, it * 2 + j), in0=UN[:, j * S:(j + 1) * S],
                                                 scalar=MOD[:, bass.ds(it * 2 + (shift + j), 1)],
                                                 in1=chunk(H_HI, it * 2 + j).bitcast(F32),
                                                 op0=ALU.add, op1=ALU.subtract).then_inc(h_ready, 1)

                if between is not None:
                    for i in range(KC // 2):
                        pair(i)
                        between(i)
                    return
                with loop(dve, KC // 2, (nhi, 2), (h_own, 2)) as it:
                    pair(it)

            def ffn_up(u0, chunks, vec, gem0, also=None):
                gem = [(gem_of[0], 16), (gem_of[1], 16), (seq, 2 * (gem_seq if also is None else 2 * gem_seq + 1))]
                with loop(dve, chunks // 2, (silu, 2), (ahi, 2), (alo_own, 2), *gem) as it:
                    dve.wait_ge(alo_ready, alo_own.add(0))
                    alo_own.add(2)
                    for p in range(2):
                        g = u0 + 2 * p
                        dve.wait_ge(silu_ready, silu.add())
                        dve.wait_ge(strip_done, it * RING + (g + 2 + RING))
                        dve.tensor_tensor(HF[:, p * S:(p + 1) * S], SG[:, p * S:(p + 1) * S], bank[(g + 1) % RING][:, :],
                                          ALU.mult).then_inc(bank_free, 2)
                        split_next(u0, it, 2 * p)
                        split_next(u0, it, 2 * p + 1)
                        gem_step(p, vec, it * 2 + (gem0 + p), also)
                        dve.wait_ge(ahi_ready, ahi.add())
                        dve.tensor_tensor(chunk(A_LO, it * 2 + p), HF[:, p * S:(p + 1) * S],
                                          chunk(A_HI, it * 2 + p).bitcast(F32), ALU.subtract).then_inc(alo_ready, 1)

            def down(u0, gate, gate0, vec=None, gem0=0):
                gem = [(gem_of[2], 16), (seq, gem_seq)] if vec is not None else []

                def turn(it):
                    for j in range(RING):
                        split_next(u0, it, j)
                        dve.wait_ge(strip_done, it * RING + (u0 + j + 1 + RING))
                        dve.scalar_tensor_tensor(out=chunk(X, it * RING + j), in0=bank[(u0 + j) % RING][:, :],
                                                 scalar=gate[:, bass.ds(it * RING + (gate0 + j), 1)],
                                                 in1=chunk(X, it * RING + j), op0=ALU.mult, op1=ALU.add).then_inc(bank_free, 1)
                    if vec is not None:
                        gem_step(2, vec, it + gem0)

                if u0 + KC == STRIPS:
                    for it in range(KC // RING):
                        turn(it)
                    return
                with loop(dve, KC // RING, *gem) as it:
                    turn(it)

            def attend(n0, keys, masked, scale, prob, output):
                for n in range(TT * H + 4):
                    if n < TT * H:
                        dve.wait_ge(score_done, n0 + n + 1)
                        after(masked(n, bank[n % 4]))
                        after(dve.tensor_reduce(soft(n, 0), bank[n % 4][:, 0:keys(n)], AX.X, ALU.max))
                        dve.tensor_scalar(soft(n, 1), soft(n, 0), -scale, None, ALU.mult).then_inc(neg_ready, 1)
                    if 0 <= n - 1 < TT * H:
                        m = n - 1
                        dve.wait_ge(exp_done, n0 + m + 1)
                        after(dve.reciprocal(soft(m, 3), soft(m, 2)))
                        p = prob[:, m % 4 * S:m % 4 * S + keys(m)]
                        dve.tensor_scalar(p, p, soft(m, 3), None, ALU.mult).then_inc(prob_ready, 1)
                    if n >= 4 and (n - 3) % (2 * TT) == 0:
                        c = (n - 3) // (2 * TT) - 1
                        dve.wait_ge(ohi_ready, n0 // (2 * TT) + c + 1)
                        output(c, bank[6 + c % 2][:, :]).then_inc(olo_ready, 1)

            def mixer1():
                mod_columns(24, 72, 24)
                factors(A_1 + KC, 24 + 8, V_NORM + KC)
                factors(A_1 + 2 * KC, 48 + 8, V_NORM + 2 * KC)
                after(half_gate(2))
                norm(A_1 + KC, 24)
                for j in range(4):
                    split_next(U_LATENT, 0, j)
                    dve.wait_ge(strip_done, U_LATENT + j + 1 + RING)
                    cols = DR if j == 3 else P
                    dve.tensor_copy((CQT[:, 0:S], CQT[:, S:2 * S], CKVT[:, :], KRF[:, :])[j],
                                    bank[(U_LATENT + j) % RING][0:cols, :]).then_inc(bank_free, 1)
                ub = [UB[:, j * UPAD:(j + 1) * UPAD] for j in range(4)]
                for j in range(4):
                    ins = dve.memset(ub[j][:, 0:CK - 1], 0.0)
                after(ins)
                for j in range(4):
                    split_next(U_CONV, 0, j)
                    dve.wait_ge(strip_done, U_CONV + j + 1 + RING)
                    dve.tensor_copy(chunk(XV, j), bank[(U_CONV + j) % RING][:, :]).then_inc(bank_free, 1)
                dve.wait_ge(lat_std, 2)
                after(dve.reciprocal(UN[:, S:2 * S], UN[:, S:2 * S]))
                after(dve.reciprocal(RINV[:, :], RINV[:, :]))
                for k in range(2):
                    after(dve.scalar_tensor_tensor(out=chunk(CQT, k), in0=chunk(CQT, k), scalar=COL1[:, V_QA + k:V_QA + k + 1],
                                                   in1=UN[:, S:2 * S], op0=ALU.mult, op1=ALU.mult))
                after(dve.scalar_tensor_tensor(out=CKVT[:, :], in0=CKVT[:, :], scalar=COL1[:, V_KVA:V_KVA + 1],
                                               in1=RINV[:, :], op0=ALU.mult, op1=ALU.mult))
                dve.wait_ge(kr_turned, 1)
                after(dve.tensor_copy(KRT[:, :], bank[6][:, 0:TT * DR]))
                dve.sem_inc(lat_ready, 1)
                for j in range(4):
                    split_next(U_CONV + 4, 0, j)
                    dve.wait_ge(strip_done, U_CONV + 4 + j + 1 + RING)
                    ins = dve.tensor_tensor(ub[j][:, CK - 1:], bank[(U_CONV + j) % RING][:, :], chunk(XV, j), ALU.mult)
                    ins.then_inc(bank_free, 1)
                    dve.wait_ge(bank_free, U_CONV + 4 + j + 1 + RING)
                    taps = [COL1[:, V_CONV + t * 4 + j:V_CONV + t * 4 + j + 1] for t in range(CK)]
                    after(dve.tensor_scalar(chunk(XV, j), ub[j][:, 0:S], taps[0], None, ALU.mult))
                    for t in range(1, CK):
                        after(dve.scalar_tensor_tensor(out=chunk(XV, j), in0=ub[j][:, t:t + S], scalar=taps[t],
                                                       in1=chunk(XV, j), op0=ALU.mult, op1=ALU.add))
                dve.wait_ge(head_in, 16 * 7)
                n = TT * DR // 2
                ang, tmp = ANGLE[:, 0:n], SIN[:, :]
                after(dve.tensor_copy(STAT[:, 100:100 + TT], POS[:, :]))
                for t in range(TT):
                    ins = dve.tensor_scalar(ang[:, t * DR // 2:(t + 1) * DR // 2], FREQ[:, :], STAT[:, 100 + t:101 + t], None, ALU.mult)
                after(ins)
                for i, (quarter, add) in enumerate(((0.0, 0.0), (0.25, np.pi / 2))):
                    r = ANGLE[:, (i + 1) * n:(i + 2) * n]
                    after(dve.tensor_scalar(tmp, ang, 1 / (2 * np.pi), quarter, ALU.mult, ALU.add))
                    after(dve.tensor_scalar(tmp, tmp, ROUND, ROUND, ALU.add, ALU.subtract))
                    src = ang
                    for part in TURN:
                        after(dve.scalar_tensor_tensor(out=r, in0=tmp, scalar=-part, in1=src, op0=ALU.mult, op1=ALU.add))
                        src = r
                    after(dve.tensor_scalar(r, r, float(add), None, ALU.add))
                    after(dve.tensor_scalar(r, r, HALF_TURN, -HALF_TURN, ALU.min, ALU.max))
                dve.sem_inc(angle_ready, 1)
                for j in range(4):
                    split_next(U_CONV + 8, 0, j)
                    dve.wait_ge(strip_done, U_CONV + 8 + j + 1 + RING)
                    dve.tensor_tensor(chunk(XV, j), bank[(U_CONV + j) % RING][:, :], chunk(XV, j), ALU.mult).then_inc(bank_free, 1)
                    dve.wait_ge(bank_free, U_CONV + 8 + j + 1 + RING)
                    after(dve.tensor_copy(chunk(A_HI, 4 + j), chunk(XV, j)))
                    dve.tensor_tensor(chunk(A_LO, 4 + j), chunk(XV, j), chunk(A_HI, 4 + j).bitcast(F32),
                                      ALU.subtract).then_inc(mixed, 1)
                dve.wait_ge(sin_ready, 2)
                dve.wait_ge(mixed, 4)
                wq, wk = HEADW[:, 0:DN], HEADW[:, DN:2 * DN]
                wqr, wkr = HEADW[:, 2 * DN:2 * DN + DR], HEADW[:, 2 * DN + DR:]

                def over_heads(ap, heads=H):
                    return ap.unsqueeze(1).to_broadcast([P, heads, ap.shape[1]])

                def over_features(ap, n):
                    return ap.unsqueeze(2).to_broadcast([P, ap.shape[1], n])

                def scaled(x, inv, w):
                    after(dve.tensor_tensor(x, x, over_features(inv, x.shape[2]), ALU.mult))
                    after(dve.tensor_tensor(x, x, over_heads(w, x.shape[1]), ALU.mult))

                def rotated(x, t, tmp):
                    heads = x.shape[1]
                    cos, sin = (over_heads(chunk(z, t, DR // 2), heads) for z in (COS, SIN))
                    x1, x2 = x[:, :, 0:DR // 2], x[:, :, DR // 2:]
                    m = [tmp[:, i * heads * DR // 2:(i + 1) * heads * DR // 2].rearrange("p (h d) -> p h d", h=heads) for i in range(4)]
                    dve.tensor_tensor(m[0], x1, cos, ALU.mult)
                    dve.tensor_tensor(m[1], x2, sin, ALU.mult)
                    dve.tensor_tensor(m[2], x2, cos, ALU.mult)
                    after(dve.tensor_tensor(m[3], x1, sin, ALU.mult))
                    dve.tensor_tensor(x1, m[0], m[1], ALU.subtract)
                    after(dve.tensor_tensor(x2, m[2], m[3], ALU.add))

                with loop(dve, TT, (seq, 14), (hsq, 3), (hstd, 2)) as t:
                    q, k = heads(chunk(QTOK, t, H * DQ)), heads(chunk(KTOK, t, H * DQ))
                    kr = chunk(KRT, t, DR).unsqueeze(1)
                    split_next(U_GATE, t, 0)
                    dve.wait_ge(head_sq, hsq.add(3))
                    dve.tensor_reduce(STAT[:, 0:H], heads(TQ0[:, :])[:, :, 0:DN], AX.X, ALU.add)
                    dve.tensor_reduce(STAT[:, H:2 * H], TQ1[:, 0:H * DN].rearrange("p (h d) -> p h d", h=H), AX.X, ALU.add)
                    dve.tensor_reduce(STAT[:, 2 * H:3 * H], heads(TQ0[:, :])[:, :, DN:], AX.X, ALU.add)
                    dve.tensor_reduce(STAT[:, 3 * H:3 * H + 1], TQ1[:, H * DN:H * DN + DR], AX.X, ALU.add).then_inc(head_sum, 1)
                    split_next(U_GATE, t, 1)
                    dve.wait_ge(head_std, hstd.add(2))
                    after(dve.reciprocal(STAT[:, 32:32 + 3 * H + 1], STAT[:, 0:3 * H + 1]))
                    scaled(q[:, :, 0:DN], STAT[:, 32:32 + H], wq)
                    scaled(q[:, :, DN:], STAT[:, 32 + 2 * H:32 + 3 * H], wqr)
                    rotated(q[:, :, DN:], t, RINV[:, :])
                    split_next(U_GATE, t, 2)
                    scaled(k[:, :, 0:DN], STAT[:, 32 + H:32 + 2 * H], wk)
                    scaled(kr, STAT[:, 32 + 3 * H:32 + 3 * H + 1], wkr)
                    rotated(kr, t, UN[:, 800:])
                    after(dve.tensor_copy(k[:, :, DN:], kr.to_broadcast([P, H, DR])))
                    dve.sem_inc(k_ready, 1)
                    split_next(U_GATE, t, 3)
                for n in range(1, 2 * H + TT, 2):
                    dve.wait_ge(turned, n + 1)
                    if n < 2 * H:
                        ins = dve.tensor_copy(chunk(KT, n // 2), bank[4 + n % 4][0:DQ, :])
                    else:
                        ins = dve.tensor_copy(chunk(V, n - 2 * H), bank[4 + n % 4][:, :])
                    ins.then_inc(turn_dve, 1)
                def causal(n, scores):
                    last = scores[:, n % TT * P:(n % TT + 1) * P]
                    return dve.tensor_tensor(last, last, CAUSAL[:, :], ALU.add)

                attend(0, lambda n: (n % TT + 1) * P, causal, DQ ** -0.5, PROB,
                       lambda c, src: dve.tensor_tensor(chunk(A_LO, c), src, chunk(A_HI, c).bitcast(F32), ALU.subtract))
                with loop(dve, KC // RING, (seq, 2 * RING)) as it:
                    for j in range(RING):
                        b, un = (U_BRANCH + j) % RING, UN[:, j % 2 * S:(j % 2 + 1) * S]
                        split_next(U_BRANCH, it, j)
                        dve.wait_ge(strip_done, it * RING + (U_BRANCH + j + 1 + RING))
                        after(dve.tensor_tensor(un, bank[b][:, :], chunk(GATES, it * RING + j), ALU.mult))
                        after(dve.tensor_tensor(RINV[:, :], bank[4 + b][:, :], chunk(GATES, it * RING + (KC + j)), ALU.mult))
                        dve.sem_inc(bank_free, 1)
                        dve.tensor_tensor(un, un, RINV[:, :], ALU.add).then_inc(merged, 1)
                        dve.wait_ge(mhi_ready, it * RING + (j + 1))
                        dve.tensor_tensor(chunk(H_LO, it * RING + j), un, chunk(H_HI, it * RING + j).bitcast(F32),
                                          ALU.subtract).then_inc(mlo_ready, 1)
                down(U_OUT, MOD, 40)

            def mixer2():
                dve.wait_ge(gem_done, T_2)

                def context_strip(s):
                    split_next(U_CTX, 0, s)
                    dve.wait_ge(strip_done, U_CTX + s + 1 + RING)
                    dst = KT2[:, s * KEYS + S:(s + 1) * KEYS] if s < 4 else chunk(VTC, s - 4, CTX)
                    dve.tensor_copy(dst, bank[(U_CTX + s) % RING][:, 0:CTX]).then_inc(bank_free, 1)

                for s in range(4):
                    context_strip(s)
                mod_columns(M_2, M_CTX, M_2)
                factors(A_2, M_2 + KC, V_N1G)
                after(factors(A_2 + KC, M_2 + 4 * KC, V_N2G))
                norm(A_2, M_2, lambda i: context_strip(4 + i))
                cv = [CV[:, c * CPAD:(c + 1) * CPAD] for c in range(2)]
                for c in range(2):
                    dve.memset(cv[c][:, 0:PAD2], 0.0)
                    ins = dve.memset(cv[c][:, PAD2 + S:], 0.0)
                after(ins)
                taps = [(c, t) for c in range(2) for t in range(CK2)]

                def convolve(count):
                    for c, t in taps[:count]:
                        tap, v = COL3[:, 2 * t + c:2 * t + c + 1], cv[c][:, t:t + S]
                        if t == 0:
                            ins = dve.tensor_scalar(chunk(ACC, c), v, tap, COL1[:, V_DWB + c:V_DWB + c + 1], ALU.mult, ALU.add)
                        else:
                            ins = dve.scalar_tensor_tensor(out=chunk(ACC, c), in0=v, scalar=tap, in1=chunk(ACC, c),
                                                           op0=ALU.mult, op1=ALU.add)
                        after(ins)
                        if t == CK2 - 1:
                            dve.sem_inc(conv_ready, 1)
                    del taps[:count]

                def turned_values(n):
                    dve.wait_ge(vw_turned, n + 1)
                    dve.tensor_copy(window_values(n), window_bank(n)).then_inc(vw_dve, 1)

                for s in range(len(IN2_COLS)):
                    u = U_IN2 + s
                    split_next(U_IN2, 0, s)
                    if s < 2:
                        dve.wait_ge(strip_done, u + 1 + RING)
                        dve.tensor_copy(chunk(UT, s), bank[u % RING][:, :]).then_inc(bank_free, 1)
                    elif s in (3, 5):
                        c = s // 2 - 1
                        dve.wait_ge(strip_done, u + 1 + RING)
                        dve.wait_ge(sig_ready, c + 1)
                        ins = dve.tensor_tensor(cv[c][:, PAD2:PAD2 + S], bank[u % RING][:, :], SQ[:, c * S:(c + 1) * S], ALU.mult)
                        ins.then_inc(bank_free, 2)
                        dve.wait_ge(bank_free, u + 1 + RING)
                    if s >= 3:
                        convolve(5)
                    if s >= 15:
                        turned_values(2 * (s - 15) + 1)
                for t in (1, 3):
                    dve.wait_ge(uc_done, t + 1)
                    dve.tensor_copy(chunk(UC, t), bank[t][:, :]).then_inc(uc_dve, 1)
                for n in (7, 9):
                    turned_values(n)
                dve.wait_ge(ln_sum, 1)
                for c in range(2):
                    dve.scalar_tensor_tensor(out=chunk(ACC, c), in0=bank[4][:, :], scalar=-1.0 / CW2, in1=chunk(ACC, c),
                                             op0=ALU.mult, op1=ALU.add).then_inc(dev_ready, 1)
                dve.wait_ge(ft_done, 2)
                dve.tensor_copy(chunk(FT, 1), bank[1][:, :]).then_inc(ft_dve, 1)
                dve.wait_ge(ln_std, 1)
                after(dve.reciprocal(bank[4][:, :], bank[4][:, :]))
                for c in range(2):
                    dve.tensor_tensor(chunk(ACC, c), chunk(ACC, c), bank[4][:, :], ALU.mult).then_inc(z_ready, 1)
                for h in range(H):
                    dve.wait_ge(rpb_turned, h + 1)
                    span = bank[5 + h % 3][:, 0:SPAN]
                    for v in range(3):
                        first = WIN - v * WIN // 2
                        ins = dve.tensor_tensor(chunk(BIAS, v * H + h, ROWS * KW).rearrange("p (k c) -> p k c", k=ROWS),
                                                bass.AP(span.tensor, span.offset + first, [span.ap[0], [RPB_C, ROWS], [1, KW]]),
                                                MASK[:, v * KW:(v + 1) * KW].unsqueeze(1).to_broadcast([P, ROWS, KW]), ALU.add)
                    ins.then_inc(bias_ready, 1)
                for m in range(4):
                    dve.wait_ge(mix_hi, m + 1)
                    lo, hi = chunk(A_LO, m), chunk(A_HI, m).bitcast(F32)
                    if m < 2:
                        ins = dve.tensor_tensor(lo, bank[2 + m][:, :], hi, ALU.subtract)
                    else:
                        ins = dve.scalar_tensor_tensor(out=lo, in0=bank[m - 2][:, :], scalar=COL1[:, V_PWB + m - 2:V_PWB + m - 1],
                                                       in1=hi, op0=ALU.add, op1=ALU.subtract)
                    ins.then_inc(mixed, 1)

                def biased(n, scores):
                    h, j = n // TT, n % TT
                    return dve.tensor_tensor(scores[:, 0:ROWS * KW], scores[:, 0:ROWS * KW],
                                             chunk(BIAS, VARIANT[j] * H + h, ROWS * KW), ALU.add)

                attend(TT * H, lambda n: S, biased, 1.0, PROB2,
                       lambda c, src: dve.tensor_tensor(by_rows(chunk(A_LO, 4 + c)), by_tiles(src),
                                                        by_rows(chunk(A_HI, 4 + c).bitcast(F32)), ALU.subtract))
                down(U_OUT2, MOD, M_2 + 2 * KC)

            def mlp():
                norm(A_2 + KC, M_2 + 3 * KC)
                for part in range(MLP_PARTS):
                    u = U_MLP + 2 * KC * part
                    with loop(dve, KC // RING, (silu, RING), (ahi, RING), (alo_own, RING)) as it:
                        for j in range(RING):
                            hf = HF[:, j % 2 * S:(j % 2 + 1) * S]
                            split_next(u, it, j)
                            dve.wait_ge(alo_ready, alo_own.add(0))
                            alo_own.add()
                            dve.wait_ge(silu_ready, silu.add())
                            dve.tensor_tensor(hf, SG[:, j % 2 * S:(j % 2 + 1) * S], bank[(u + j) % RING][:, :],
                                              ALU.mult).then_inc(bank_free, 1)
                            dve.wait_ge(ahi_ready, ahi.add())
                            dve.tensor_tensor(chunk(A_LO, it * RING + j), hf, chunk(A_HI, it * RING + j).bitcast(F32),
                                              ALU.subtract).then_inc(alo_ready, 1)
                    down(u + KC, MOD, M_2 + 5 * KC)

            dve.sem_inc(lo_ready, RING)
            dve.sem_inc(h_ready, 2)
            dve.sem_inc(alo_ready, 2)
            for i, (dst, b) in enumerate(((COL1[:, 0:V_ROWS], 4), (COL2[:, :], 5), (COL3[:, :], 6))):
                dve.wait_ge(cols_turned, i + 1)
                dve.tensor_copy(dst, bank[b][:, 0:dst.shape[1]]).then_inc(cols_ready, 1)
            dve.wait_ge(ident_ready, 1)
            after(dve.tensor_tensor(SUM32[:, :], IDENT[:, 0:32], IDENT[:, 32:64], ALU.add))
            after(dve.tensor_tensor(SUM32[:, :], SUM32[:, :], IDENT[:, 64:96], ALU.add))
            dve.tensor_tensor(SUM32[:, :], SUM32[:, :], IDENT[:, 96:128], ALU.add).then_inc(cols_ready, 1)
            dve.wait_ge(cond_ready, 1)
            gem_step(0, V_C, 0)
            for k in range(KC):
                dve.wait_ge(x_turned, k + 1)
                dve.tensor_copy(chunk(X, k), bank[k % 2][:, :]).then_inc(x_ready, 1)
            dve.sem_inc(bank_free, RING)
            for t in range(1, 8):
                gem_step(t % 3, V_C, t)
            for u in range(LEAD):
                split_lo(u, u)
            mod_columns(0, 16, 0)
            factors(A_1, 8, V_NORM).then_inc(mod_ready, 1)
            dve.wait_ge(mod_ready, 1)
            norm(A_1, 0)
            u, t = U_FFN0, 8
            for i, (_, chunks) in enumerate(FFN_PARTS):
                ffn_up(u, chunks, V_C, t)
                u, t = u + 2 * chunks, t + chunks
                if i == 0:
                    mod_columns(16, 24, 16)
                    after(half_gate(0))
                down(u, GHALF, 0, V_C, t)
                u, t = u + KC, t + 2
            mixer1()
            norm(A_1 + 2 * KC, 48)
            u, t = U_FFN1, T_ADA
            for i, (_, chunks) in enumerate(FFN_PARTS):
                ffn_up(u, chunks, V_C2, t, V_CCTX if i == 0 else None)
                u, t = u + 2 * chunks, t + chunks
                if i == 0:
                    dve.wait_ge(ctx_std, 1)
                    after(dve.reciprocal(STAT[:, 204:206], STAT[:, 200:202]))
                    for j in range(2):
                        dve.tensor_scalar(CTOK[:, j * D:(j + 1) * D], CTOK[:, j * D:(j + 1) * D], STAT[:, 204 + j:205 + j], None,
                                          ALU.mult).then_inc(ctx_ready, 1)
                down(u, GHALF, 2 * KC, V_C2 if i == 0 else None, t)
                u, t = u + KC, t + (2 if i == 0 else 0)
                if i == 0:
                    mod_columns(M_CTX, M_COLS, M_2)
                    dve.sem_inc(ctx_mod, 1)
                    after(factors(A_CTX, M_CTX + KC, V_N1G))
                    for k in range(KC + 1):
                        if k < KC:
                            dve.wait_ge(ctx_turned, k // 2 + 1)
                            if k >= 4:
                                dve.wait_ge(clo_ready, k - 3)
                            dve.tensor_scalar(chunk(HF, k % 4, CTX), bank[(4, 6, 7, 5)[k // 2]][:, k % 2 * CTX:(k % 2 + 1) * CTX],
                                              AMOD[:, A_CTX + k:A_CTX + k + 1], MOD[:, M_CTX + k:M_CTX + k + 1],
                                              ALU.mult, ALU.add).then_inc(ctx_full, 1)
                        if k >= 1:
                            dve.wait_ge(chi_ready, k)
                            dve.tensor_tensor(chunk(C_LO, k - 1, CTX), chunk(HF, (k - 1) % 4, CTX),
                                              chunk(C_HI, k - 1, CTX).bitcast(F32), ALU.subtract).then_inc(clo_ready, 1)
            mixer2()
            mlp()
            dve.wait_ge(std_ready, std.add())
            after(dve.reciprocal(RINV[:, :], RINV[:, :]))
            for k in range(KC):
                dve.scalar_tensor_tensor(out=chunk(YT, k), in0=chunk(X, k), scalar=COL1[:, V_FIN + k:V_FIN + k + 1],
                                         in1=RINV[:, :], op0=ALU.mult, op1=ALU.mult).then_inc(y_ready, 1)
            for t in range(TT):
                dve.wait_ge(y_turned, 2 * t + 2)
                dve.tensor_copy(YTOK[:, t * D + S:(t + 1) * D], bank[7][:, :]).then_inc(ytok_ready, 1)


_INS = ["x", "c", "positions", "w_ada", "b_ada", "norm_w", "ffn_w13", "ffn_w2", "w_in", "q_a_norm", "w_uq", "kv_a_norm",
        "w_ukv", "q_norm_nope", "k_norm_nope", "q_norm_rope", "k_norm_rope", "conv_w", "w_branch", "w_out", "c_2",
        "ctx_2", "c_ctx_2", "ada_w_2", "ada_b_2", "norm1_g_2", "norm2_g_2", "w_in_2", "w_fourier_2", "conv_dw_w_2",
        "conv_dw_b_2", "conv_norm_g_2", "conv_norm_b_2", "conv_pw_w_2", "conv_pw_b_2", "na_rpb_2", "w_out_2",
        "mlp_w1_2", "mlp_w2_2", "final_norm_g_2"]


def constants():
    f = 1.0 / np.float32(10000) ** (np.arange(0, DR, 2, dtype=np.float32) / np.float32(DR))
    feat = np.arange(DH)
    turn = 2 * np.pi * np.outer(feat, feat) / DH
    two = np.kron(np.eye(2), np.cos(turn)), np.kron(np.eye(2), np.sin(turn))
    tok = np.arange(S)
    turn = 2 * np.pi * (np.outer(tok, tok) % S) / S
    scale = 1.0 / np.sqrt(S * DH)
    q, k = np.arange(P)[:, None], np.arange(P)[None, :]
    near = np.zeros((P, 3, KW), np.float32)
    for v, (tile, w) in enumerate(((0, 0), (1, 8), (3, 32))):
        col, key = QC * tile + np.arange(P)[:, None] % QC, w + np.arange(KW)[None, :]
        first = np.clip(col - WIN // 2, 0, COLS - WIN)
        near[:, v] = np.where((key >= first) & (key < first + WIN), 0.0, NEG)
    return {
        "rope_freq": np.tile(f.astype(np.float32), (P, 1)),
        "dft_feat": np.concatenate(two, axis=1).astype(np.float32),
        "dft_tok": np.stack([np.cos(turn) * scale, -np.sin(turn) * scale]).astype(np.float32),
        "causal": np.where(k <= q, 0.0, NEG).astype(np.float32),
        "near": near,
    }


def kernel(**inputs):
    import concourse.bacc as bacc
    from concourse.bass_utils import run_bass_kernel_spmd as run

    nc = bacc.Bacc("TRN2", target_bir_lowering=False, num_devices=1)
    arrays, aps = {}, {}
    given = {n: np.ascontiguousarray(inputs[n]) for n in _INS}
    for name, v in {**given, **constants()}.items():
        arrays[f"in_{name}"] = v
        aps[name] = nc.dram_tensor(f"in_{name}", v.shape, mybir.dt.from_np(v.dtype), kind="ExternalInput").ap()
    out = nc.dram_tensor("out_0", (1, S, D), F32, kind="ExternalOutput").ap()
    block_pair_kernel(nc, aps, out)
    r = run(nc, [arrays], core_ids=[0])
    return r.results[0]["out_0"]
```

```python
import numpy as np
import concourse.bass as bass
from concourse import mybir
from contextlib import ExitStack, contextmanager

F32 = mybir.dt.float32
F32R = mybir.dt.float32r
I32 = mybir.dt.int32
ALU = mybir.AluOpType
ACT = mybir.ActivationFunctionType
AX = mybir.AxisListType

P = 128
D = 1024
KC = D // P
S = 512
TT = S // P
CTX = 256
FF = 2816
EPS, LN_EPS = 1e-6, 1e-5
H = 8
DN, DR, DV = 64, 32, 64
DQ = DN + DR
QR, KR = 256, 128
CW, CK = 512, 3
COLS, ROWS = 64, 8
WIN = 16
QC = 16
KW = 32
NEAR = (0, QC // 2, QC // 2 + WIN, 2 * WIN)
VARIANT = (0, 1, 1, 2)
RPB_R, RPB_C = 2 * ROWS - 1, 2 * WIN - 1
SPAN = (ROWS - 1) * RPB_C + KW + WIN
SPAN_IN = SPAN - SPAN % 16
CW2, CK2 = 256, 31
PAD2 = CK2 // 2
DH = 64
NEG = -1e30
ROUND = 1.5 * 2.0 ** 23
HALF_TURN = float(np.float32(np.pi)) - 2.0 ** -22
TURN = (6.28125, 0.0019354820251464844, -1.7484555314695172e-07)

RING = 4
LEAD = 3
STRIP = KC * P
GEM = 256
GEM_RING = 4
FOLD = GEM // 32

FFN_PARTS = [(0, 8), (8, 8), (16, 6)]
FFN_STRIPS = sum(2 * n + KC for _, n in FFN_PARTS)
U_FFN0 = 0
U_LATENT = U_FFN0 + FFN_STRIPS
U_CONV = U_LATENT + 4
U_GATE = U_CONV + 12
U_BRANCH = U_GATE + 16
U_OUT = U_BRANCH + KC
U_FFN1 = U_OUT + KC
U_CTX = U_FFN1 + FFN_STRIPS
U_IN2 = U_CTX + 8
U_OUT2 = U_IN2 + 18
U_MLP = U_OUT2 + KC
MLP_PARTS = 4
STRIPS = U_MLP + MLP_PARTS * 2 * KC

V_NORM, V_N1G, V_N2G, V_FIN = 0, 24, 32, 40
V_QA, V_KVA, V_DWB, V_LNG, V_LNB, V_PWB, V_CONV, V_ROWS = 48, 50, 51, 53, 55, 57, 59, 71
C_1, C_2, C_CTX = 0, 8, 16
M_2, M_CTX, M_COLS = 72, 120, 136
A_1, A_2, A_CTX, A_COLS = 0, 24, 40, 48


class Tally:

    def __init__(self, sem):
        self.sem, self.n, self.it, self.per, self.start = sem, 0, None, 0, 0

    def enter(self, it, per):
        self.it, self.per, self.start = it, per, self.n

    def leave(self, times):
        assert self.n == self.start + self.per, (self.sem, self.n, self.start, self.per)
        self.n, self.it = self.start + self.per * times, None

    def add(self, k=1):
        self.n += k
        return self.n if self.it is None else self.it * self.per + self.n


@contextmanager
def loop(eng, times, *tallies):
    if times == 1:
        yield 0
        return
    with eng.Fori(0, times) as it:
        for t, per in tallies:
            t.enter(it, per)
        yield it
        for t, per in tallies:
            t.leave(times)


def block_pair_kernel(nc, a, out):
    with ExitStack() as ctx:
        place = [(nc.sbuf_base + 63) // 64 * 64]

        def sb(name, shape, dt=F32, over=None):
            size = int(np.prod(shape[1:])) * 4
            offset = place[0] if over is None else over
            if over is None:
                place[0] += (size + 63) // 64 * 64
            t = nc.alloc_sbuf_tensor_at(name, shape, dt, offset=offset)
            where[name] = offset
            return t

        where = {}
        X = sb("X", [P, KC * S])
        H_HI = sb("H_HI", [P, KC * S], F32R)
        H_LO = sb("H_LO", [P, KC * S], F32R)
        place[0] += 64
        A_HI = sb("A_HI", [P, KC * S], F32R)
        A_LO = sb("A_LO", [P, KC * S], F32R)
        RAW = sb("RAW", [P, RING * STRIP])
        W_HI = sb("W_HI", [P, RING * STRIP], F32R)
        W_LO = sb("W_LO", [P, RING * STRIP], F32R)
        COL1 = sb("COL1", [P, V_ROWS + 1])
        CRAW = sb("CRAW", [P, 3 * KC])
        COL2 = sb("COL2", [P, M_CTX])
        COL3 = sb("COL3", [P, 2 * CK2])
        CSIL = sb("CSIL", [P, 3 * KC])
        IDENT = sb("IDENT", [P, P])
        ONES = sb("ONES", [P, P])
        FLIP = sb("FLIP", [P, P])
        SUM32 = sb("SUM32", [P, 32])
        MOD = sb("MOD", [P, M_COLS])
        AMOD = sb("AMOD", [P, A_COLS])
        GHALF = sb("GHALF", [P, 3 * KC])
        CONST = sb("CONST", [P, 4])
        STAT = sb("STAT", [P, 256])
        FOLDED = sb("FOLDED", [P, M_COLS * 4])
        SQ = sb("SQ", [P, 2 * S])
        UN = sb("UN", [P, 2 * S])
        NRM = sb("NRM", [P, 4 * S], over=where["SQ"])
        RINV = sb("RINV", [P, S])
        SG = sb("SG", [P, 2 * S], over=where["SQ"])
        HF = sb("HF", [P, 2 * S], over=where["UN"])
        SSUM = sb("SSUM", [P, S])
        scratch = place[0]
        assert scratch + 60 * 1024 <= nc.sbuf_usable_end, (scratch, nc.sbuf_usable_end)
        GBUF = sb("GBUF", [P, GEM_RING * KC * GEM], over=scratch)
        GACC = sb("GACC", [P, GEM], over=scratch + GEM_RING * KC * GEM * 4)
        GTURN = sb("GTURN", [P, GEM], over=where["GACC"] + GEM * 4)
        GATES = sb("GATES", [P, 2 * KC * S], over=scratch)
        XV = sb("XV", [P, 4 * S], over=scratch)
        UPAD = S + CK - 1
        UB = sb("UB", [P, 4 * UPAD], over=scratch + 4 * S * 4)
        QTOK = sb("QTOK", [P, TT * H * DQ], over=scratch + 2 * KC * S * 4)
        KTOK = sb("KTOK", [P, TT * H * DQ], over=where["QTOK"] + TT * H * DQ * 4)
        KRF = sb("KRF", [DR, S], over=where["QTOK"])
        V = sb("V", [P, TT * H * DV], over=where["QTOK"])
        small = [where["KTOK"] + TT * H * DQ * 4]

        def small_sb(name, shape, dt=F32):
            t = sb(name, shape, dt, over=small[0])
            small[0] += (int(np.prod(shape[1:])) * 4 + 31) // 32 * 32
            assert small[0] <= nc.sbuf_usable_end
            return t

        POS = small_sb("POS", [P, TT], I32)
        FREQ = small_sb("FREQ", [P, DR // 2])
        HEADW = small_sb("HEADW", [P, 2 * DN + 2 * DR])
        KRT = small_sb("KRT", [P, TT * DR])
        CAUSAL = small_sb("CAUSAL", [P, P])
        ANGLE = small_sb("ANGLE", [P, 3 * TT * DR // 2])
        COS = small_sb("COS", [P, TT * DR // 2])
        SIN = small_sb("SIN", [P, TT * DR // 2])
        UQ = sb("UQ", [P, 2 * H * DQ], over=where["A_HI"])
        CKVT = sb("CKVT", [P, S], over=where["A_HI"] + 2 * H * DQ * 4)
        UKV = sb("UKV", [P, H * (DN + DV)], over=where["A_LO"])
        CQT = sb("CQT", [P, 2 * S], over=where["A_LO"] + H * (DN + DV) * 4)
        QT = sb("QT", [DQ, H * S], over=where["H_HI"])
        KT = sb("KT", [DQ, H * S], over=where["H_LO"])
        PROB = sb("PROB", [P, 4 * S], over=where["KTOK"])
        PT = sb("PT", [P, 2 * S], over=where["KTOK"] + 4 * S * 4)
        TQ0 = sb("TQ0", [P, H * DQ], over=where["SQ"])
        TQ1 = sb("TQ1", [P, H * DQ], over=where["UN"])
        CTOK = sb("CTOK", [P, 2 * D], over=scratch + 50 * 1024)
        C_HI = sb("C_HI", [P, KC * CTX], F32R, over=scratch + 34 * 1024)
        C_LO = sb("C_LO", [P, KC * CTX], F32R, over=scratch + 42 * 1024)
        KEYS = S + CTX
        KT2 = sb("KT2", [P, 4 * KEYS], over=scratch)
        QZ = sb("QZ", [P, 8 * S], over=scratch + 12 * 1024)
        VT = sb("VT", [P, 2 * TT * ROWS * KW], over=scratch + 28 * 1024)
        VW = sb("VW", [P, 8 * H * DH], over=scratch + 36 * 1024)
        VTC = sb("VTC", [P, 4 * CTX], over=scratch + 52 * 1024)
        VC = sb("VC", [P, 2 * H * DH], over=scratch + 56 * 1024)
        MASK = sb("MASK", [P, 3 * KW], over=scratch + 60 * 1024)
        assert scratch + 60 * 1024 + 3 * KW * 4 <= nc.sbuf_usable_end
        TCOS = sb("TCOS", [P, TT * S], over=where["A_HI"])
        TSIN = sb("TSIN", [P, TT * S], over=where["A_LO"])
        UT = sb("UT", [P, 2 * S], over=where["A_HI"] + 4 * S * 4)
        FT = sb("FT", [P, 2 * S], over=where["A_HI"] + 4 * S * 4)
        ACC = sb("ACC", [P, 2 * S], over=where["A_HI"] + 6 * S * 4)
        CPAD = S + CK2 - 1
        CV = sb("CV", [P, 2 * CPAD], over=where["A_LO"] + 4 * S * 4)
        DFEAT = sb("DFEAT", [P, 2 * P], over=where["CV"] + 2 * CPAD * 4 // 64 * 64 + 64)
        WF = sb("WF", [P, 2 * 2 * P], over=where["DFEAT"] + 2 * P * 4)
        assert where["WF"] + 4 * P * 4 <= where["A_LO"] + KC * S * 4
        PW = sb("PW", [P, 2 * CW2], over=where["RINV"])
        BIAS = sb("BIAS", [P, 3 * H * ROWS * KW], over=where["H_HI"])
        RPB = sb("RPB", [P, H * SPAN_IN + 16], over=where["H_LO"] + 4 * S * 4)
        assert where["RPB"] + H * SPAN_IN * 4 + 64 == where["A_HI"]
        CSQ = sb("CSQ", [P, 2 * S], over=where["CV"])
        UC = sb("UC", [P, TT * S], over=where["SQ"])
        PT2 = sb("PT2", [P, 2 * S], over=where["RPB"])
        PROB2 = sb("PROB2", [P, 4 * S], over=where["SQ"])
        XTOK = sb("XTOK", [P, TT * D], over=where["A_HI"])
        ROWS1 = sb("ROWS1", [V_ROWS, P], over=where["A_LO"])
        ROWS2 = sb("ROWS2", [M_CTX, P], over=where["A_LO"] + 512)
        ROWS3 = sb("ROWS3", [2 * CK2, P], over=where["A_LO"] + 1024)
        YT = sb("YT", [P, KC * S], over=where["A_HI"])
        YTOK = sb("YTOK", [P, TT * D], over=where["H_HI"])

        bank = [ctx.enter_context(nc.psum_tensor(f"bank{i}", [P, S], F32)) for i in range(8)]

        def sem(name):
            return ctx.enter_context(nc.semaphore(name))

        raw_in = [sem(f"raw_in{i}") for i in range(RING)]
        hi_ready = sem("hi_ready")
        lo_ready = sem("lo_ready")
        strip_done = sem("strip_done")
        bank_free = sem("bank_free")
        rows_in = sem("rows_in")
        x_in = sem("x_in")
        gem_in = [sem(f"gem_in{i}") for i in range(GEM_RING)]
        gem_done = sem("gem_done")
        ident_ready = sem("ident_ready")
        const_ready = sem("const_ready")
        cols_turned = sem("cols_turned")
        cols_ready = sem("cols_ready")
        cond_in = sem("cond_in")
        cond_ready = sem("cond_ready")
        x_turned = sem("x_turned")
        x_ready = sem("x_ready")
        mod_summed = sem("mod_summed")
        sq_ready = sem("sq_ready")
        sq_used = sem("sq_used")
        stat_ready = sem("stat_ready")
        std_ready = sem("std_ready")
        un_ready = sem("un_ready")
        nhi_ready = sem("nhi_ready")
        h_ready = sem("h_ready")
        silu_ready = sem("silu_ready")
        ahi_ready = sem("ahi_ready")
        alo_ready = sem("alo_ready")
        dve_seq = sem("dve_seq")
        pool_seq = sem("pool_seq")
        up_in = sem("up_in")
        head_in = sem("head_in")
        lat_sq = sem("lat_sq")
        lat_sum = sem("lat_sum")
        lat_std = sem("lat_std")
        lat_ready = sem("lat_ready")
        kr_turned = sem("kr_turned")
        angle_ready = sem("angle_ready")
        sin_ready = sem("sin_ready")
        up_done = sem("up_done")
        up_read = sem("up_read")
        head_sq = sem("head_sq")
        head_sum = sem("head_sum")
        head_std = sem("head_std")
        k_ready = sem("k_ready")
        turned = sem("turned")
        turn_act = sem("turn_act")
        turn_dve = sem("turn_dve")
        score_done = sem("score_done")
        neg_ready = sem("neg_ready")
        exp_done = sem("exp_done")
        prob_ready = sem("prob_ready")
        prob_turned = sem("prob_turned")
        pt_ready = sem("pt_ready")
        pv_done = sem("pv_done")
        ohi_ready = sem("ohi_ready")
        olo_ready = sem("olo_ready")
        mixed = sem("mixed")
        merged = sem("merged")
        mhi_ready = sem("mhi_ready")
        mlo_ready = sem("mlo_ready")
        ctx_in = sem("ctx_in")
        ctx_sq = sem("ctx_sq")
        ctx_std = sem("ctx_std")
        ctx_ready = sem("ctx_ready")
        ctx_mod = sem("ctx_mod")
        ctx_turned = sem("ctx_turned")
        ctx_full = sem("ctx_full")
        chi_ready = sem("chi_ready")
        clo_ready = sem("clo_ready")
        flip_ready = sem("flip_ready")
        rpb_in = sem("rpb_in")
        table_in = sem("table_in")
        zeros_ready = sem("zeros_ready")
        sig_ready = sem("sig_ready")
        conv_ready = sem("conv_ready")
        ln_sum = sem("ln_sum")
        dev_ready = sem("dev_ready")
        ln_sq = sem("ln_sq")
        ln_std = sem("ln_std")
        z_ready = sem("z_ready")
        act_ready = sem("act_ready")
        uc_done = sem("uc_done")
        uc_act = sem("uc_act")
        uc_dve = sem("uc_dve")
        ft_done = sem("ft_done")
        ft_act = sem("ft_act")
        ft_dve = sem("ft_dve")
        rpb_turned = sem("rpb_turned")
        bias_ready = sem("bias_ready")
        vw_turned = sem("vw_turned")
        vw_act = sem("vw_act")
        vw_dve = sem("vw_dve")
        mix_done = sem("mix_done")
        mix_hi = sem("mix_hi")
        y_ready = sem("y_ready")
        y_turned = sem("y_turned")
        ytok_ready = sem("ytok_ready")
        out_done = sem("out_done")

        def chunk(t, k, n=S):
            return t[:, bass.ds(k * n, n)]

        def heads(t):
            return t.rearrange("p (h d) -> p h d", h=H)

        def soft(n, i):
            return STAT[:, 128 + n % 4 * 4 + i:128 + n % 4 * 4 + i + 1]

        def by_rows(t):
            return t.rearrange("p (r j c) -> p j r c", r=ROWS, j=TT)

        def by_tiles(t):
            return t.rearrange("p (j r c) -> p j r c", j=TT, r=ROWS)

        def window_values(n):
            if n >= 8:
                return chunk(VC, n - 8)
            c, half = n // 2, n % 2
            return VW[:, half * 4 * S:(half + 1) * 4 * S].rearrange("p (t f) -> p t f", t=4)[:, :, c * P:(c + 1) * P]

        def window_bank(n):
            b = bank[4 + n % 4][:, :]
            return b if n >= 8 else b.rearrange("p (t f) -> p t f", t=4)

        def strip_of(t, slot):
            return t[:, slot * STRIP:(slot + 1) * STRIP]

        def rows_of(w):
            return w.rearrange("(k p) n -> p k n", p=P)

        w13 = [rows_of(a["ffn_w13"][0, f]) for f in range(2)]
        w2 = [rows_of(a["ffn_w2"][0, f]) for f in range(2)]
        w_in, w_out = rows_of(a["w_in"][0]), rows_of(a["w_out"][0])
        w_branch = rows_of(a["w_branch"][0].rearrange("g k d -> (g k) d"))
        w_ada, ada_2 = rows_of(a["w_ada"][0]), rows_of(a["ada_w_2"][0])
        w_in2, w_out2 = rows_of(a["w_in_2"][0]), rows_of(a["w_out_2"][0])
        w_mlp1, w_mlp2 = rows_of(a["mlp_w1_2"][0]), rows_of(a["mlp_w2_2"][0])

        def gem_ffn0(seq):
            return lambda it, g: it * GEM_RING + (seq + g)

        def gem_up1(part):
            def tile(it, g):
                return it * 2 + (T_ADA + g // 2 + (8 + 8 * part if g % 2 else 4 * part))
            return tile

        def gem_down1(part):
            return lambda it, g: T_ADA + 12 + 8 * part + g

        GEM_PLAN = [[(8, gem_ffn0(8), 4, gem_ffn0(16)), (8, gem_ffn0(20), 4, gem_ffn0(28)), (0, None, 4, gem_ffn0(32))],
                    [(8, gem_up1(0), 4, gem_down1(0)), (8, gem_up1(1), 4, gem_down1(1)), (0, None, 0, None)]]

        def gem_after(part):
            return (0, 1, 2, 3) if part == len(FFN_PARTS) - 1 else (0, 2, 4, 6)

        T_ADA = 9 * D // GEM
        T_2 = T_ADA + 6 * D // GEM

        rpb = nc.dram_tensor("rpb_padded", (2 * WIN + H * RPB_R * RPB_C,), F32, kind="Internal").ap()
        IN2_COLS = [c * P for c in (0, 1, 4, 2, 5, 3)] + [c * P for c in range(6, 18)]

        block = ctx.enter_context(nc.Block())

        @block.sync
        def _(sp):
            def load_strip(u, slot, src):
                dst = strip_of(RAW, slot)[:, 0:src.shape[1] * src.shape[2]]
                sp.wait_ge(lo_ready, u + 1)
                sp.dma_start(dst.rearrange("p (k n) -> p k n", k=src.shape[1]), src).then_inc(raw_in[slot], 16)

            def load_gem(slot, src):
                dst = GBUF[:, slot * KC * GEM:(slot + 1) * KC * GEM].rearrange("p (k n) -> p k n", k=KC)
                sp.dma_start(dst, src).then_inc(gem_in[slot], 16)

            def load_strips(u0, count, src):
                with loop(sp, count // RING) as it:
                    for j in range(RING):
                        load_strip(it * RING + (u0 + j), (u0 + j) % RING, src(it * RING + j))

            def load_gem_after(slot, seq, src):
                sp.wait_ge(gem_done, seq - (GEM_RING - 1))
                load_gem(slot, src)

            def load_ffn(u, f, seq, w13, w2, src):
                for part, (c0, chunks) in enumerate(FFN_PARTS):
                    ups, tile_up, downs, tile_down = GEM_PLAN[f][part]
                    per = GEM_RING if ups else 2
                    with loop(sp, chunks // per) as it:
                        for j in range(2 * per):
                            col = (it * per + (j // 2 + c0)) * P + (j % 2) * FF
                            load_strip(it * 2 * per + (u + j), (u + j) % RING, w13[:, :, bass.ds(col, P)])
                            if ups and j % 2:
                                load_gem_after(j // 2, it * GEM_RING + (seq + j // 2), src(tile_up(it, j // 2)))
                    u, seq = u + 2 * chunks, seq + ups
                    for m in range(KC):
                        load_strip(u + m, (u + m) % RING, w2[:, c0:c0 + chunks, m * P:(m + 1) * P])
                        if downs and m in gem_after(part):
                            g = gem_after(part).index(m)
                            load_gem_after(g, seq + g, src(tile_down(0, g)))
                    u, seq = u + KC, seq + downs

            def rows(dst, names):
                at = 0
                for name in names:
                    v = a[name]
                    flat = v.rearrange(" ".join("abc"[:len(v.shape)]) + " -> (" + " ".join("abc"[:len(v.shape)]) + ")") if len(v.shape) > 1 else v
                    n = int(np.prod(v.shape)) // P
                    sp.dma_start(dst[at:at + n, :], flat.rearrange("(r p) -> r p", p=P)).then_inc(rows_in, 16)
                    at += n

            def ada(t):
                return w_ada[:, :, bass.ds(t * GEM, GEM)]

            def ada2(t):
                return ada_2[:, :, bass.ds((t - T_ADA) * GEM, GEM)]

            with nc.allow_non_contiguous_dma(reason="1024 numbers, 8 to a partition"):
                for i, name in enumerate(("c", "c_2", "c_ctx_2")):
                    v = a[name] if len(a[name].shape) > 1 else a[name].unsqueeze(0)
                    sp.dma_start(CRAW[:, i * KC:(i + 1) * KC], v.rearrange("a (k p) -> p (a k)", p=P)).then_inc(cond_in, 16)
            for t in range(GEM_RING):
                load_gem(t, ada(t))
            for t in range(TT):
                sp.dma_start(XTOK[:, t * D:(t + 1) * D], a["x"][0, t * P:(t + 1) * P, :]).then_inc(x_in, 16)
            rows(ROWS1, ["norm_w", "norm1_g_2", "norm2_g_2", "final_norm_g_2", "q_a_norm", "kv_a_norm", "conv_dw_b_2",
                         "conv_norm_g_2", "conv_norm_b_2", "conv_pw_b_2", "conv_w"])
            rows(ROWS2, ["b_ada", "ada_b_2"])
            rows(ROWS3, ["conv_dw_w_2"])
            for t in range(GEM_RING, 8):
                load_gem_after(t % GEM_RING, t, ada(t))
            load_ffn(U_FFN0, 0, 8, w13[0], w2[0], ada)
            with nc.allow_non_contiguous_dma(reason="512 positions, one to a partition"):
                sp.dma_start(POS[:, :], a["positions"].rearrange("a (t p) -> p (a t)", p=P)).then_inc(head_in, 16)
            sp.dma_start(FREQ[:, :], a["rope_freq"]).then_inc(head_in, 16)
            sp.dma_start(CAUSAL[:, :], a["causal"]).then_inc(head_in, 16)
            flat = a["na_rpb_2"].rearrange("a h r c -> (a h r c)")
            n, pad = H * RPB_R * RPB_C, WIN
            for to, frm, size in ((pad, 0, n), (0, 0, pad), (pad + n, n - pad, pad)):
                sp.dma_start(rpb[to:to + size], flat[frm:frm + size]).then_inc(rpb_in, 16)
            at = 0
            for name, n in (("q_norm_nope", DN), ("k_norm_nope", DN), ("q_norm_rope", DR), ("k_norm_rope", DR)):
                sp.dma_start(HEADW[:, at:at + n], a[name].to_broadcast([P, n])).then_inc(head_in, 16)
                at += n
            for j, cols in enumerate((P, P, P, DR)):
                load_strip(U_LATENT + j, (U_LATENT + j) % RING, w_in[:, :, j * P:j * P + cols])
            i3 = QR + KR + DR
            for part in (0, 2, 1):
                u = U_CONV + 4 * (0, 2, 1)[part]
                load_strips(u, 4, lambda m: w_in[:, :, i3 + part * CW + m * P:i3 + part * CW + (m + 1) * P])
                if part == 0:
                    sp.wait_ge(strip_done, U_LATENT + RING)
                    sp.dma_start(UQ[:, :].rearrange("p (k n) -> p k n", k=2), rows_of(a["w_uq"][0])).then_inc(up_in, 16)
                    sp.dma_start(UKV[:, :], a["w_ukv"][0]).then_inc(up_in, 16)
            load_strips(U_GATE, 2 * KC, lambda m: w_in[:, :, bass.ds(m * P + (i3 + 3 * CW), P)])
            load_strips(U_BRANCH, KC, lambda m: w_branch[:, :, bass.ds(m * P, P)])
            load_strips(U_OUT, KC, lambda m: w_out[:, :, bass.ds(m * P, P)])
            sp.wait_ge(mlo_ready, KC)
            sp.dma_start(CTOK[:, :].rearrange("p (t d) -> p t d", t=2),
                         a["ctx_2"][0].rearrange("(t p) d -> p t d", p=P)).then_inc(ctx_in, 16)
            load_ffn(U_FFN1, 1, T_ADA, w13[1], w2[1], ada2)
            load_strips(U_CTX, 8, lambda m: w_in2[:, :, bass.ds(m * P + 10 * P, P)])
            for s, col in enumerate(IN2_COLS):
                load_strip(U_IN2 + s, (U_IN2 + s) % RING, w_in2[:, :, col:col + P])
                if s == 8:
                    sp.wait_ge(strip_done, U_IN2 + 1 + RING)
                    for dst, i in ((TCOS, 0), (TSIN, 1)):
                        sp.dma_start(dst[:, :].rearrange("p (t s) -> p t s", t=TT),
                                     a["dft_tok"][i].rearrange("(t p) s -> p t s", p=P)).then_inc(table_in, 16)
                    sp.dma_start(DFEAT[:, :], a["dft_feat"]).then_inc(table_in, 16)
                    sp.dma_start(MASK[:, :], a["near"].rearrange("p v k -> p (v k)")).then_inc(table_in, 16)
                    sp.dma_start(WF[:, :].rearrange("p (k n) -> p k n", k=2), rows_of(a["w_fourier_2"][0])).then_inc(table_in, 16)
                    sp.dma_start(PW[:, :].rearrange("p (k n) -> p k n", k=2), rows_of(a["conv_pw_w_2"][0])).then_inc(table_in, 16)
            load_strips(U_OUT2, RING, lambda m: w_out2[:, :, bass.ds(m * P, P)])
            sp.wait_ge(strip_done, U_OUT2 + RING)
            sp.wait_ge(rpb_in, 16 * 3)
            for r in range(ROWS):
                src = bass.AP(rpb.tensor, r * RPB_C, [[1, QC], [RPB_R * RPB_C, H], [1, SPAN_IN]])
                sp.dma_start(RPB[r * QC:(r + 1) * QC, 0:H * SPAN_IN].rearrange("p (h c) -> p h c", h=H), src).then_inc(table_in, 16)
            load_strips(U_OUT2 + RING, RING, lambda m: w_out2[:, :, bass.ds((m + RING) * P, P)])
            for part in range(MLP_PARTS):
                u = U_MLP + 2 * KC * part
                load_strips(u, KC, lambda m: w_mlp1[:, :, bass.ds(m * P + part * D, P)])
                load_strips(u + KC, KC, lambda m: w_mlp2[:, part * KC:(part + 1) * KC, bass.ds(m * P, P)])
            for t in range(TT):
                sp.wait_ge(ytok_ready, 2 * t + 2)
                sp.dma_start(out[0, t * P:(t + 1) * P, :], YTOK[:, t * D:(t + 1) * D]).then_inc(out_done, 16)
            sp.wait_ge(out_done, 16 * TT)

        @block.gpsimd
        def _(pool):
            pool.memset(IDENT[:, :], 0.0).then_inc(pool_seq, 1)
            pool.memset(ONES[:, :], 1.0).then_inc(const_ready, 1)
            pool.memset(CONST[:, 0:1], EPS).then_inc(const_ready, 1)
            pool.memset(CONST[:, 1:2], LN_EPS).then_inc(const_ready, 1)
            pool.memset(RPB[:, H * SPAN_IN:], 0.0)
            pool.memset(SSUM[:, :], 0.0).then_inc(pool_seq, 1)
            pool.wait_ge(pool_seq, 1)
            pool.affine_select(out=IDENT[:, :], in_=IDENT[:, :], compare_op=ALU.not_equal, fill=1.0, base=0,
                               pattern=[[-1, P]], channel_multiplier=1).then_inc(ident_ready, 1)
            pool.wait_ge(ident_ready, 1)
            pool.tensor_tensor(SUM32[:, :], IDENT[:, 0:32], IDENT[:, 32:64], ALU.add).then_inc(pool_seq, 1)
            for i in (2, 3):
                pool.wait_ge(pool_seq, i + 1)
                pool.tensor_tensor(SUM32[:, :], SUM32[:, :], IDENT[:, 32 * i:32 * i + 32], ALU.add).then_inc(pool_seq, 1)
            pool.wait_ge(pool_seq, 5)
            pool.sem_inc(const_ready, 1)
            pool.memset(FLIP[:, :], 0.0).then_inc(pool_seq, 1)
            pool.wait_ge(pool_seq, 6)
            pool.affine_select(out=FLIP[:, :], in_=FLIP[:, :], compare_op=ALU.not_equal, fill=1.0, base=1 - P,
                               pattern=[[1, P]], channel_multiplier=1).then_inc(flip_ready, 1)
            sq, seq = Tally(sq_ready), Tally(pool_seq)
            seq.n = 6

            def sum_squares(clear):
                if clear:
                    pool.wait_ge(stat_ready, clear)
                    pool.memset(SSUM[:, :], 0.0).then_inc(pool_seq, 1)
                    seq.add()
                pool.wait_ge(pool_seq, seq.n)
                for k in range(KC - 1):
                    pool.wait_ge(sq_ready, sq.add())
                    pool.tensor_tensor(SSUM[:, :], SSUM[:, :], SQ[:, k % 2 * S:(k % 2 + 1) * S], ALU.add).then_inc(pool_seq, 1)
                    pool.wait_ge(pool_seq, seq.add())
                    pool.sem_inc(sq_used, 1)
                sq.add()

            sum_squares(0)
            for norms in range(1, 4):
                sum_squares(norms)
            pool.wait_ge(stat_ready, 4)
            pool.memset(QZ[:, :], 0.0).then_inc(zeros_ready, 1)
            for norms in range(4, 6):
                sum_squares(norms)
        @block.tensor
        def _(pe):
            def wait_strip(u):
                pe.wait_ge(lo_ready, u + (1 + RING))
                pe.wait_ge(bank_free, u + 1)

            def products(dst, slot, blocks, hi, lo, n, cols=P, first=True, last=True):
                for i, (b, k) in enumerate(blocks):
                    w_hi = W_HI[:, slot * STRIP + b * cols:slot * STRIP + (b + 1) * cols]
                    w_lo = W_LO[:, slot * STRIP + b * cols:slot * STRIP + (b + 1) * cols]
                    x_hi, x_lo = hi[:, k * n:(k + 1) * n], lo[:, k * n:(k + 1) * n]
                    pe.matmul(dst, w_hi, x_hi, start=first and i == 0, stop=False)
                    pe.matmul(dst, w_hi, x_lo, start=False, stop=False)
                    mm = pe.matmul(dst, w_lo, x_hi, start=False, stop=last and i == len(blocks) - 1)
                return mm

            def strip(u, slot, hi, lo, chunks=KC, n=S, cols=P, each=None):
                wait_strip(u)
                for k in range(chunks):
                    if each is not None:
                        pe.wait_ge(each[0], each[1] + k + 1)
                    mm = products(bank[slot][0:cols, 0:n], slot, [(k, k)], hi, lo, n, cols,
                                  first=k == 0, last=k == chunks - 1)
                mm.then_inc(strip_done, 1)

            def strips(u0, count, hi, lo, chunks=KC, n=S, each=None):
                with loop(pe, count // RING) as it:
                    for j in range(RING):
                        strip(it * RING + (u0 + j), (u0 + j) % RING, hi, lo, chunks, n, each=each if j == 0 else None)

            def first_strips(u0, hi, lo, each):
                for j in range(LEAD):
                    wait_strip(u0 + j)
                for k in range(KC):
                    pe.wait_ge(each[0], each[1] + k + 1)
                    for j in range(LEAD):
                        slot = (u0 + j) % RING
                        mm = products(bank[slot][:, :], slot, [(k, k)], hi, lo, S, first=k == 0, last=k == KC - 1)
                        if k == KC - 1:
                            mm.then_inc(strip_done, 1)

            def new_strips(u0, count, hi, lo, each):
                first_strips(u0, hi, lo, each)
                strip(u0 + LEAD, (u0 + LEAD) % RING, hi, lo)
                strips(u0 + RING, count - RING, hi, lo)

            sq, sq_last = Tally(sq_used), Tally(sq_ready)
            h, alo = Tally(h_ready), Tally(alo_ready)
            h.n = alo.n = 2
            pe.sem_inc(strip_done, RING)

            def stat():
                pe.wait_ge(sq_used, sq.add(KC - 1))
                pe.matmul(bank[4][:, :], ONES[:, :], SSUM[:, :], start=True, stop=False)
                pe.wait_ge(sq_ready, sq_last.add(KC))
                pe.matmul(bank[4][:, :], ONES[:, :], SQ[:, S:2 * S], start=False, stop=True).then_inc(stat_ready, 1)

            def fold(c0, c1, tiles):
                pe.wait_ge(gem_done, tiles)
                for r in range(4):
                    mm = pe.matmul(bank[5][32 * r:32 * r + 32, c0:c1], SUM32[:, :],
                                   FOLDED[:, 4 * c0 + r:4 * c1:4], start=True, stop=True)
                mm.then_inc(mod_summed, 1)

            def normed():
                return h_ready, h.add(KC) - KC

            def widened(chunks):
                return alo_ready, alo.add(chunks) - chunks

            def ffn(u, after_up, after_down):
                for i, (_, chunks) in enumerate(FFN_PARTS):
                    if i == 0:
                        new_strips(u, 2 * chunks, H_HI, H_LO, normed())
                    else:
                        strips(u, 2 * chunks, H_HI, H_LO)
                    u += 2 * chunks
                    after_up[i]()
                    strips(u, KC, A_HI, A_LO, chunks, each=widened(chunks))
                    u += KC
                    after_down[i]()

            def attend(n0, scores, keys, prob, pt, values):
                for n in range(TT * H + 3):
                    if n < TT * H:
                        if n >= 4:
                            pe.wait_ge(exp_done, n0 + n - 3)
                        for dst, q, k in scores(n, bank[n % 4]):
                            mm = pe.matmul(dst, q, k, start=True, stop=True)
                        mm.then_inc(score_done, 1)
                    if 0 <= n - 2 < TT * H:
                        m = n - 2
                        pe.wait_ge(prob_ready, n0 + m + 1)
                        if m >= 2:
                            pe.wait_ge(pt_ready, n0 + m - 1)
                        for k in range(keys(m)):
                            mm = pe.transpose(bank[4 + m % 2][:, k * P:(k + 1) * P],
                                              prob[:, m % 4 * S + k * P:m % 4 * S + (k + 1) * P], IDENT[:, :])
                        mm.then_inc(prob_turned, 1)
                    if n >= 3:
                        m = n - 3
                        h, i = m // TT, m % TT
                        pe.wait_ge(pt_ready, n0 + m + 1)
                        if h >= 4 and h % 2 == 0 and i == 0:
                            pe.wait_ge(olo_ready, (n0 // TT + h) // 2 - 1)
                        for k in range(keys(m)):
                            mm = pe.matmul(bank[6 + h // 2 % 2][DV * (h % 2):DV * (h % 2) + DV, i * P:(i + 1) * P],
                                           values(m, k), pt[:, m % 2 * S + k * P:m % 2 * S + (k + 1) * P],
                                           start=k == 0, stop=k == keys(m) - 1)
                        mm.then_inc(pv_done, 1)
                pe.wait_ge(exp_done, n0 + TT * H)
                pe.wait_ge(olo_ready, (n0 // TT + H) // 2)

            def mixer1():
                stat()
                first_strips(U_LATENT, H_HI, H_LO, normed())
                strip(U_LATENT + 3, (U_LATENT + 3) % RING, H_HI, H_LO, cols=DR)
                strips(U_CONV, 4, H_HI, H_LO)
                pe.wait_ge(lat_sq, 3)
                pe.matmul(bank[4][:, :], ONES[:, :], SQ[:, 0:S], start=True, stop=False)
                pe.matmul(bank[4][:, :], ONES[:, :], SQ[:, S:2 * S], start=False, stop=True)
                pe.matmul(bank[5][:, :], ONES[:, :], UN[:, 0:S], start=True, stop=True).then_inc(lat_sum, 1)
                pe.wait_ge(bank_free, U_CONV + RING)
                for t in range(TT):
                    mm = pe.transpose(bank[6][:, t * DR:(t + 1) * DR], KRF[:, t * P:(t + 1) * P], IDENT[0:DR, 0:DR])
                mm.then_inc(kr_turned, 1)
                strips(U_CONV + 4, 8, H_HI, H_LO)
                pe.wait_ge(up_in, 32)
                pe.wait_ge(lat_ready, 1)
                half = H * DQ // 2
                for n in range(3 * TT):
                    b = bank[4 + n % 4]
                    if n >= 4:
                        pe.wait_ge(up_read, n - 3)
                    if n < 2 * TT:
                        t, c = n // 2, n % 2 * half
                        for k in range(2):
                            mm = pe.matmul(b[:, 0:half], CQT[:, k * S + t * P:k * S + (t + 1) * P],
                                           UQ[:, k * H * DQ + c:k * H * DQ + c + half], start=k == 0, stop=k == 1)
                    else:
                        t = n - 2 * TT
                        mm = pe.matmul(b[:, :], CKVT[:, t * P:(t + 1) * P],
                                       UKV[:, :].rearrange("p (h d) -> p h d", h=H)[:, :, 0:DN], start=True, stop=True)
                    mm.then_inc(up_done, 1)
                strips(U_GATE, 2 * KC, H_HI, H_LO)
                pe.wait_ge(k_ready, TT)
                for n in range(2 * H + TT):
                    b = bank[4 + n % 4]
                    if n >= 4:
                        pe.wait_ge((turn_act, turn_dve)[n % 2], n // 2 - 1)
                    if n < 2 * H:
                        for t in range(TT):
                            at = (t * H + n // 2) * DQ
                            mm = pe.transpose(b[0:DQ, t * P:(t + 1) * P], (QTOK, KTOK)[n % 2][:, at:at + DQ], IDENT[:, :])
                    else:
                        t = n - 2 * H
                        mm = pe.matmul(b[:, :], CKVT[:, t * P:(t + 1) * P],
                                       UKV[:, :].rearrange("p (h d) -> p h d", h=H)[:, :, DN:], start=True, stop=True)
                    mm.then_inc(turned, 1)
                pe.wait_ge(turn_act, H + TT // 2)
                pe.wait_ge(turn_dve, H + TT // 2)
                pe.wait_ge(bank_free, U_BRANCH + RING)
                attend(0, lambda n, dst: [(dst[:, 0:(n % TT + 1) * P],
                                           QT[:, n // TT * S + n % TT * P:n // TT * S + (n % TT + 1) * P],
                                           KT[:, n // TT * S:n // TT * S + (n % TT + 1) * P])],
                       lambda n: n % TT + 1, PROB, PT,
                       lambda n, k: V[:, (k * H + n // TT) * DV:(k * H + n // TT + 1) * DV])
                with loop(pe, KC // RING) as it:
                    for j in range(RING):
                        u = it * RING + (U_BRANCH + j)
                        slot = (U_BRANCH + j) % RING
                        wait_strip(u)
                        products(bank[slot][:, :], slot, [(k, k) for k in range(4)], A_HI, A_LO, S)
                        products(bank[4 + slot][:, :], slot, [(k, k) for k in range(4, KC)], A_HI, A_LO, S).then_inc(strip_done, 1)
                new_strips(U_OUT, KC, H_HI, H_LO, (mlo_ready, 0))

            def context():
                fold(M_CTX, M_COLS, T_2)
                pe.wait_ge(ctx_ready, 2)
                for i, b in enumerate((4, 6, 7, 5)):
                    if b == 5:
                        pe.wait_ge(ctx_mod, 1)
                    for k in (2 * i, 2 * i + 1):
                        for t in range(2):
                            mm = pe.transpose(bank[b][:, k % 2 * CTX + t * P:k % 2 * CTX + (t + 1) * P],
                                              CTOK[:, t * D + k * P:t * D + (k + 1) * P], IDENT[:, :])
                    mm.then_inc(ctx_turned, 1)

            def mixer2():
                pe.wait_ge(clo_ready, KC)
                strips(U_CTX, 4, C_HI, C_LO, n=CTX)
                stat()
                strips(U_CTX + 4, 4, C_HI, C_LO, n=CTX)

                def turn_values(c):
                    for n in (2 * c, 2 * c + 1):
                        if n >= 4:
                            pe.wait_ge((vw_act, vw_dve)[n % 2], n // 2 - 1)
                        for i in range(4):
                            tile = n % 2 * 4 + i
                            mm = pe.transpose(bank[4 + n % 4][:, i * P:(i + 1) * P],
                                              VT[:, (c % 2 * 8 + tile) * P:(c % 2 * 8 + tile + 1) * P], IDENT[:, :])
                        mm.then_inc(vw_turned, 1)

                first_strips(U_IN2, H_HI, H_LO, normed())
                for s in range(LEAD, len(IN2_COLS)):
                    strip(U_IN2 + s, (U_IN2 + s) % RING, H_HI, H_LO)
                    if s >= 15:
                        pe.wait_ge(bank_free, U_IN2 + s + RING)
                        turn_values(s - 15)
                pe.wait_ge(table_in, 16 * 6)
                pe.wait_ge(bank_free, U_OUT2 + RING)
                for t in range(TT):
                    for c in range(2):
                        mm = pe.matmul(bank[t][:, c * 2 * P:(c + 1) * 2 * P], UT[:, c * S + t * P:c * S + (t + 1) * P],
                                       DFEAT[:, :], start=True, stop=True)
                    mm.then_inc(uc_done, 1)
                turn_values(3)
                for t in range(2):
                    pe.wait_ge((vw_act, vw_dve)[t], 3)
                    for c in range(4):
                        mm = pe.transpose(bank[4 + t][:, c * P:(c + 1) * P], VTC[:, c * CTX + t * P:c * CTX + (t + 1) * P],
                                          IDENT[:, :])
                    mm.then_inc(vw_turned, 1)
                pe.wait_ge(vw_act, 5)
                pe.wait_ge(vw_dve, 5)
                pe.wait_ge(conv_ready, 2)
                for c in range(2):
                    mm = pe.matmul(bank[4][:, :], ONES[:, :], chunk(ACC, c), start=c == 0, stop=c == 1)
                mm.then_inc(ln_sum, 1)
                pe.wait_ge(uc_act, 2)
                pe.wait_ge(uc_dve, 2)
                for c in range(2):
                    for t in range(TT):
                        for i, table in enumerate((TCOS, TSIN)):
                            at = t * S + (2 * c + i) * P
                            mm = pe.matmul(bank[c][:, :], UC[:, at:at + P], chunk(table, t),
                                           start=t + i == 0, stop=t + i == TT)
                    mm.then_inc(ft_done, 1)
                pe.wait_ge(ln_sq, 2)
                for c in range(2):
                    mm = pe.matmul(bank[4][:, :], ONES[:, :], chunk(CSQ, c), start=c == 0, stop=c == 1)
                mm.then_inc(ln_sum, 1)
                pe.wait_ge(flip_ready, 1)
                pe.wait_ge(table_in, 16 * (6 + ROWS))
                for h in range(H):
                    if h >= 3:
                        pe.wait_ge(bias_ready, h - 2)
                    pe.matmul(bank[5 + h % 3][:, 0:SPAN], FLIP[:, :], RPB[:, h * SPAN_IN:h * SPAN_IN + SPAN],
                              start=True, stop=True).then_inc(rpb_turned, 1)
                pe.wait_ge(ft_act, 1)
                pe.wait_ge(ft_dve, 1)
                for m in range(2):
                    for c in range(2):
                        mm = pe.matmul(bank[2 + m][:, :], WF[:, (2 * c + m) * P:(2 * c + m + 1) * P], chunk(FT, c),
                                       start=c == 0, stop=c == 1)
                    mm.then_inc(mix_done, 1)
                pe.wait_ge(act_ready, 2)
                for m in range(2):
                    for c in range(2):
                        mm = pe.matmul(bank[m][:, :], PW[:, (2 * c + m) * P:(2 * c + m + 1) * P], chunk(ACC, c),
                                       start=c == 0, stop=c == 1)
                    mm.then_inc(mix_done, 1)
                pe.wait_ge(bias_ready, H)
                pe.wait_ge(mixed, 8)

                def scores(n, dst):
                    h, j = n // TT, n % TT
                    c = h // 2
                    q = QZ[:, h * S + j * P:h * S + (j + 1) * P]
                    near = KT2[:, c * KEYS:c * KEYS + S].rearrange("p (r c) -> p r c", r=ROWS)[:, :, NEAR[j]:NEAR[j] + KW]
                    return [(dst[:, 0:CTX], q, near), (dst[:, CTX:], q, KT2[:, c * KEYS + S:(c + 1) * KEYS])]

                def values(n, k):
                    h, j = n // TT, n % TT
                    if k < 2:
                        return VW[:, ((2 * j + k) * H + h) * DH:((2 * j + k) * H + h + 1) * DH]
                    return VC[:, ((k - 2) * H + h) * DH:((k - 2) * H + h + 1) * DH]

                attend(TT * H, scores, lambda n: 4, PROB2, PT2, values)
                strips(U_OUT2, KC, A_HI, A_LO)

            def mlp():
                stat()
                for part in range(MLP_PARTS):
                    u = U_MLP + 2 * KC * part
                    if part == 0:
                        new_strips(u, KC, H_HI, H_LO, normed())
                    else:
                        strips(u, KC, H_HI, H_LO)
                    strips(u + KC, KC, A_HI, A_LO, each=widened(KC))

            def nothing():
                pass

            pe.wait_ge(ident_ready, 1)
            pe.wait_ge(x_in, 16 * TT)
            for k in range(KC):
                if k >= RING:
                    pe.wait_ge(x_ready, k - RING + 1)
                for t in range(TT):
                    mm = pe.transpose(bank[k % RING][:, t * P:(t + 1) * P], XTOK[:, t * D + k * P:t * D + (k + 1) * P],
                                      IDENT[:, :])
                mm.then_inc(x_turned, 1)
            pe.wait_ge(rows_in, 16 * 14)
            for b, rows, dst in ((5, ROWS1, V_ROWS), (6, ROWS2, M_CTX), (7, ROWS3, 2 * CK2)):
                pe.transpose(bank[b][:, 0:dst], rows[:, :], IDENT[0:dst, 0:dst]).then_inc(cols_turned, 1)
            pe.wait_ge(const_ready, 4)
            stat()
            pe.wait_ge(cols_ready, 3)
            fold(0, 16, 8)
            ffn(U_FFN0, [lambda: fold(16, 24, 12),
                         nothing, lambda: fold(24, 64, 32)], [nothing] * 3)
            mixer1()
            stat()
            ffn(U_FFN1, [lambda: fold(64, M_2, T_ADA),
                         nothing, lambda: fold(M_2, M_CTX, T_2)], [nothing, context, nothing])
            mixer2()
            mlp()
            stat()
            for t in range(TT):
                for half in range(2):
                    if t:
                        pe.wait_ge(ytok_ready, 2 * t)
                    for i in range(4):
                        k = 4 * half + i
                        if t == 0:
                            pe.wait_ge(y_ready, k + 1)
                        mm = pe.transpose(bank[6 + half][:, i * P:(i + 1) * P],
                                          YT[:, k * S + t * P:k * S + (t + 1) * P], IDENT[:, :])
                    mm.then_inc(y_turned, 1)

        @block.scalar
        def _(act):
            def split_hi(u, slot, turn):
                act.wait_ge(raw_in[slot], turn * 16 + 16)
                act.wait_ge(strip_done, u + 1)
                act.activation(strip_of(W_HI, slot), strip_of(RAW, slot), ACT.Copy).then_inc(hi_ready, 1)

            def split_next(u0, it, j):
                u = u0 + j + LEAD
                if not isinstance(it, int) or it * RING + u < STRIPS:
                    split_hi(it * RING + u, u % RING, it + u // RING)

            silu, ahi, un = Tally(silu_ready), Tally(ahi_ready), Tally(un_ready)
            std, nhi, hsum = Tally(stat_ready), Tally(nhi_ready), Tally(head_sum)

            def square(k, j):
                act.activation(SQ[:, j * S:(j + 1) * S], chunk(X, k), ACT.Square).then_inc(sq_ready, 1)

            def norm(shift, between=None):
                act.wait_ge(stat_ready, std.add())
                act.activation(RINV[:, :], bank[4][:, :], ACT.Sqrt, bias=CONST[:, 0:1], scale=1.0 / D).then_inc(std_ready, 1)

                for k in range(KC):
                    act.wait_ge(un_ready, un.add())
                    act.activation(chunk(H_HI, k), chunk(NRM, k % 4), ACT.Identity,
                                   bias=MOD[:, shift + k:shift + k + 1]).then_inc(nhi_ready, 1)
                    if between is not None and k % 2:
                        between(k // 2)

            def ffn_up(u0, chunks):
                with loop(act, chunks // 2) as it:
                    for p in range(2):
                        split_next(u0, it, 2 * p)
                        split_next(u0, it, 2 * p + 1)
                        g = u0 + 2 * p
                        act.wait_ge(strip_done, it * RING + (g + 1 + RING))
                        act.activation(SG[:, p * S:(p + 1) * S], bank[g % RING][:, :], ACT.Silu).then_inc(silu_ready, 1)
                        act.wait_ge(bank_free, it * RING + (g + 2 + RING))
                        act.activation(chunk(A_HI, it * 2 + p), HF[:, p * S:(p + 1) * S], ACT.Copy).then_inc(ahi_ready, 1)

            def down(u0, squares):
                def turn(it):
                    for j in range(RING):
                        split_next(u0, it, j)
                        if squares:
                            act.wait_ge(bank_free, it * RING + (u0 + j + 1 + RING))
                            act.wait_ge(sq_used, squares + (it * RING + j) - 1)
                            square(it * RING + j, j % 2)

                if u0 + KC == STRIPS:
                    for it in range(KC // RING):
                        turn(it)
                    return
                with loop(act, KC // RING) as it:
                    turn(it)

            def attend(n0, keys, scale, prob, pt, output):
                for n in range(TT * H + 4):
                    if n < TT * H:
                        act.wait_ge(neg_ready, n0 + n + 1)
                        if n >= 4:
                            act.wait_ge(prob_turned, n0 + n - 3)
                        act.activation(prob[:, n % 4 * S:n % 4 * S + keys(n)], bank[n % 4][:, 0:keys(n)], ACT.Exp,
                                       bias=soft(n, 1), scale=scale, accum_out=soft(n, 2)).then_inc(exp_done, 1)
                    if 0 <= n - 2 < TT * H:
                        m = n - 2
                        act.wait_ge(prob_turned, n0 + m + 1)
                        if m >= 2:
                            act.wait_ge(pv_done, n0 + m - 1)
                        act.activation(pt[:, m % 2 * S:m % 2 * S + keys(m)], bank[4 + m % 2][:, 0:keys(m)],
                                       ACT.Copy).then_inc(pt_ready, 1)
                    if n >= 4 and (n - 3) % (2 * TT) == 0:
                        c = (n - 3) // (2 * TT) - 1
                        act.wait_ge(pv_done, n0 + (c + 1) * 2 * TT)
                        output(c, bank[6 + c % 2][:, :]).then_inc(ohi_ready, 1)

            def mixer1():
                norm(24)
                for j in range(4):
                    split_next(U_LATENT, 0, j)
                    if j < 3:
                        act.wait_ge(bank_free, U_LATENT + j + 1 + RING)
                        act.activation((SQ[:, 0:S], SQ[:, S:2 * S], UN[:, 0:S])[j],
                                       (CQT[:, 0:S], CQT[:, S:2 * S], CKVT[:, :])[j], ACT.Square).then_inc(lat_sq, 1)
                for j in range(4):
                    split_next(U_CONV, 0, j)
                act.wait_ge(lat_sum, 1)
                act.activation(UN[:, S:2 * S], bank[4][:, :], ACT.Sqrt, bias=CONST[:, 0:1], scale=1.0 / QR).then_inc(lat_std, 1)
                act.activation(RINV[:, :], bank[5][:, :], ACT.Sqrt, bias=CONST[:, 0:1], scale=1.0 / KR).then_inc(lat_std, 1)
                with loop(act, 2) as it:
                    for j in range(4):
                        split_next(U_CONV + 4, it, j)
                act.wait_ge(angle_ready, 1)
                act.activation(SIN[:, :], ANGLE[:, TT * DR // 2:TT * DR], ACT.Sin).then_inc(sin_ready, 1)
                act.activation(COS[:, :], ANGLE[:, TT * DR:], ACT.Sin).then_inc(sin_ready, 1)
                half = H * DQ // 2
                for n in range(3 * TT):
                    act.wait_ge(up_done, n + 1)
                    if n < 2 * TT:
                        act.activation(chunk(QTOK, n, half), bank[4 + n % 4][:, 0:half], ACT.Copy).then_inc(up_read, 1)
                    else:
                        act.activation(heads(chunk(KTOK, n - 2 * TT, H * DQ))[:, :, 0:DN],
                                       bank[4 + n % 4][:, :].rearrange("p (h d) -> p h d", h=H), ACT.Copy).then_inc(up_read, 1)
                act.wait_ge(bank_free, U_GATE + RING)
                act.wait_ge(mixed, 4)
                act.wait_ge(up_read, 3 * TT)
                with loop(act, TT, (hsum, 1)) as t:
                    act.activation(TQ0[:, :], chunk(QTOK, t, H * DQ), ACT.Square).then_inc(head_sq, 1)
                    act.activation(TQ1[:, 0:H * DN], heads(chunk(KTOK, t, H * DQ))[:, :, 0:DN], ACT.Square).then_inc(head_sq, 1)
                    act.activation(TQ1[:, H * DN:H * DN + DR], chunk(KRT, t, DR), ACT.Square).then_inc(head_sq, 1)
                    for j in range(RING):
                        split_next(U_GATE, t, j)
                        act.wait_ge(strip_done, t * RING + (U_GATE + j + 1 + RING))
                        act.activation(chunk(GATES, t * RING + j), bank[(U_GATE + j) % RING][:, :],
                                       ACT.Sigmoid).then_inc(bank_free, 1)
                        if j == 0:
                            act.wait_ge(head_sum, hsum.add())
                            act.activation(STAT[:, 0:2 * H], STAT[:, 0:2 * H], ACT.Sqrt, bias=CONST[:, 0:1],
                                           scale=1.0 / DN).then_inc(head_std, 1)
                            act.activation(STAT[:, 2 * H:3 * H + 1], STAT[:, 2 * H:3 * H + 1], ACT.Sqrt, bias=CONST[:, 0:1],
                                           scale=1.0 / DR).then_inc(head_std, 1)
                for n in range(0, 2 * H + TT, 2):
                    act.wait_ge(turned, n + 1)
                    if n < 2 * H:
                        ins = act.activation(chunk(QT, n // 2), bank[4 + n % 4][0:DQ, :], ACT.Copy)
                    else:
                        ins = act.activation(chunk(V, n - 2 * H), bank[4 + n % 4][:, :], ACT.Copy)
                    ins.then_inc(turn_act, 1)
                attend(0, lambda n: (n % TT + 1) * P, DQ ** -0.5, PROB, PT,
                       lambda c, src: act.activation(chunk(A_HI, c), src, ACT.Copy))
                with loop(act, KC // RING) as it:
                    for j in range(RING):
                        split_next(U_BRANCH, it, j)
                        act.wait_ge(merged, it * RING + (j + 1))
                        act.activation(chunk(H_HI, it * RING + j), UN[:, j % 2 * S:(j % 2 + 1) * S], ACT.Copy).then_inc(mhi_ready, 1)
                down(U_OUT, 2 * (KC - 1))

            def mixer2():
                for j in range(4):
                    split_next(U_CTX, 0, j)
                norm(M_2, lambda i: split_next(U_CTX + 4, 0, i))

                def turned_values(n):
                    act.wait_ge(vw_turned, n + 1)
                    act.activation(window_values(n), window_bank(n), ACT.Copy).then_inc(vw_act, 1)

                for s in range(len(IN2_COLS)):
                    u = U_IN2 + s
                    split_next(U_IN2, 0, s)
                    src = bank[u % RING]
                    if s in (2, 4):
                        act.wait_ge(strip_done, u + 1 + RING)
                        p = s // 2 - 1
                        act.activation(SQ[:, p * S:(p + 1) * S], src[:, :], ACT.Sigmoid).then_inc(sig_ready, 1)
                    if s == 6:
                        act.wait_ge(bank_free, u + RING)
                        act.wait_ge(zeros_ready, 1)
                    if s >= 6:
                        act.wait_ge(strip_done, u + 1 + RING)
                        part, c = (s - 6) // 4, (s - 6) % 4
                        if part == 0:
                            for i in range(2):
                                rows = slice(DH * i, DH * i + DH)
                                ins = act.activation(
                                    by_tiles(chunk(QZ, 2 * c + i)[rows, :]), by_rows(src[rows, :]), ACT.Copy, scale=DH ** -0.5)
                        elif part == 1:
                            ins = act.activation(KT2[:, c * KEYS:c * KEYS + S], src[:, :], ACT.Copy)
                        else:
                            if c >= 2:
                                act.wait_ge(vw_turned, 2 * c - 2)
                            for j in range(TT):
                                ins = act.activation(
                                    chunk(VT, c % 2 * TT + j, ROWS * KW).rearrange("p (r c) -> p r c", r=ROWS),
                                    src[:, :].rearrange("p (r c) -> p r c", r=ROWS)[:, :, NEAR[j]:NEAR[j] + KW], ACT.Copy)
                        ins.then_inc(bank_free, 1)
                        if s >= 15:
                            turned_values(2 * (s - 15))
                for t in (0, 2):
                    act.wait_ge(uc_done, t + 1)
                    act.activation(chunk(UC, t), bank[t][:, :], ACT.Copy).then_inc(uc_act, 1)
                for n in (6, 8):
                    turned_values(n)
                for c in range(2):
                    act.wait_ge(dev_ready, c + 1)
                    act.activation(chunk(CSQ, c), chunk(ACC, c), ACT.Square).then_inc(ln_sq, 1)
                act.wait_ge(ft_done, 2)
                act.activation(chunk(FT, 0), bank[0][:, :], ACT.Copy).then_inc(ft_act, 1)
                act.wait_ge(ln_sum, 2)
                act.activation(bank[4][:, :], bank[4][:, :], ACT.Sqrt, bias=CONST[:, 1:2], scale=1.0 / CW2).then_inc(ln_std, 1)
                for c in range(2):
                    act.wait_ge(z_ready, c + 1)
                    act.activation(chunk(ACC, c), chunk(ACC, c), ACT.Silu, bias=COL1[:, V_LNB + c:V_LNB + c + 1],
                                   scale=COL1[:, V_LNG + c:V_LNG + c + 1]).then_inc(act_ready, 1)
                for m in range(4):
                    act.wait_ge(mix_done, m + 1)
                    if m < 2:
                        ins = act.activation(chunk(A_HI, m), bank[2 + m][:, :], ACT.Copy)
                    else:
                        ins = act.activation(chunk(A_HI, m), bank[m - 2][:, :], ACT.Identity,
                                             bias=COL1[:, V_PWB + m - 2:V_PWB + m - 1])
                    ins.then_inc(mix_hi, 1)
                attend(TT * H, lambda n: S, 1.0, PROB2, PT2,
                       lambda c, src: act.activation(by_rows(chunk(A_HI, 4 + c)), by_tiles(src), ACT.Copy))
                down(U_OUT2, 4 * (KC - 1))

            def mlp():
                norm(M_2 + 3 * KC)
                for part in range(MLP_PARTS):
                    u = U_MLP + 2 * KC * part
                    with loop(act, KC // RING) as it:
                        for j in range(RING):
                            split_next(u, it, j)
                            act.wait_ge(strip_done, it * RING + (u + j + 1 + RING))
                            act.activation(SG[:, j % 2 * S:(j % 2 + 1) * S], bank[(u + j) % RING][:, :],
                                           ACT.Relu).then_inc(silu_ready, 1)
                            act.wait_ge(bank_free, it * RING + (u + j + 1 + RING))
                            act.activation(chunk(A_HI, it * RING + j), HF[:, j % 2 * S:(j % 2 + 1) * S],
                                           ACT.Copy).then_inc(ahi_ready, 1)
                    down(u + KC, 5 * (KC - 1) if part == MLP_PARTS - 1 else 0)

            act.wait_ge(cond_in, 16 * 3)
            act.activation(CSIL[:, :], CRAW[:, :], ACT.Silu).then_inc(cond_ready, 1)
            for k in range(KC):
                act.wait_ge(x_turned, k + 1)
                act.activation(chunk(X, k), bank[k % RING][:, :], ACT.Copy).then_inc(x_ready, 1)
                act.wait_ge(x_ready, k + 1)
                if k >= 2:
                    act.wait_ge(sq_used, k - 1)
                square(k, k % 2)
            act.sem_inc(bank_free, RING)
            for i, (dst, b) in enumerate(((COL1[:, 0:V_ROWS], 5), (COL2[:, :], 6), (COL3[:, :], 7))):
                act.wait_ge(cols_turned, i + 1)
                act.activation(dst, bank[b][:, 0:dst.shape[1]], ACT.Copy).then_inc(cols_ready, 1)
            for u in range(LEAD):
                act.wait_ge(raw_in[u], 16)
                act.activation(strip_of(W_HI, u), strip_of(RAW, u), ACT.Copy).then_inc(hi_ready, 1)
            norm(0)
            u = U_FFN0
            for i, (_, chunks) in enumerate(FFN_PARTS):
                ffn_up(u, chunks)
                u += 2 * chunks
                down(u, KC - 1 if i == 2 else 0)
                u += KC
            mixer1()
            norm(48)
            u = U_FFN1
            for i, (_, chunks) in enumerate(FFN_PARTS):
                ffn_up(u, chunks)
                u += 2 * chunks
                if i == 1:
                    act.wait_ge(ctx_in, 16)
                    for t in range(2):
                        act.activation(SQ[:, :], CTOK[:, t * D:(t + 1) * D], ACT.Square,
                                       accum_out=STAT[:, 200 + t:201 + t]).then_inc(ctx_sq, 1)
                        act.wait_ge(ctx_sq, t + 1)
                    act.activation(STAT[:, 200:202], STAT[:, 200:202], ACT.Sqrt, bias=CONST[:, 0:1],
                                   scale=1.0 / D).then_inc(ctx_std, 1)
                down(u, 3 * (KC - 1) if i == 2 else 0)
                u += KC
                if i == 1:
                    for k in range(KC):
                        act.wait_ge(ctx_full, k + 1)
                        act.activation(chunk(C_HI, k, CTX), chunk(HF, k % 4, CTX), ACT.Copy).then_inc(chi_ready, 1)
            mixer2()
            mlp()
            act.wait_ge(stat_ready, std.add())
            act.activation(RINV[:, :], bank[4][:, :], ACT.Sqrt, bias=CONST[:, 0:1], scale=1.0 / D).then_inc(std_ready, 1)
            for t in range(TT):
                act.wait_ge(y_turned, 2 * t + 1)
                act.activation(YTOK[:, t * D:t * D + S], bank[6][:, :], ACT.Copy).then_inc(ytok_ready, 1)

        @block.vector
        def _(dve):
            seq = Tally(dve_seq)

            def after(ins):
                ins.then_inc(dve_seq, 1)
                dve.wait_ge(dve_seq, seq.add())

            def split_lo(u, slot):
                dve.wait_ge(hi_ready, u + 1)
                dve.tensor_tensor(strip_of(W_LO, slot), strip_of(RAW, slot), strip_of(W_HI, slot).bitcast(F32),
                                  ALU.subtract).then_inc(lo_ready, 1)

            def split_next(u0, it, j, per=RING):
                u = u0 + j + LEAD
                if not isinstance(it, int) or it * per + u < STRIPS:
                    split_lo(it * per + u, u % RING)

            silu, ahi, nhi, std = Tally(silu_ready), Tally(ahi_ready), Tally(nhi_ready), Tally(std_ready)
            hsq, hstd = Tally(head_sq), Tally(head_std)
            gem_seq = KC + 1
            h_own, alo_own = Tally(h_ready), Tally(alo_ready)
            h_own.n = alo_own.n = 2
            gem_of = [Tally(gem_in[i]) for i in range(GEM_RING)]

            def gem_tile(slot, vec, at):
                g = GBUF[:, slot * KC * GEM:(slot + 1) * KC * GEM]
                after(dve.tensor_scalar(GACC[:, :], g[:, 0:GEM], CSIL[:, vec:vec + 1], None, ALU.mult))
                for k in range(1, KC):
                    after(dve.scalar_tensor_tensor(out=GACC[:, :], in0=g[:, k * GEM:(k + 1) * GEM],
                                                   scalar=CSIL[:, vec + k:vec + k + 1], in1=GACC[:, :],
                                                   op0=ALU.mult, op1=ALU.add))
                after(dve.transpose(GTURN[:, :], GACC[:, :]))
                return dve.tensor_reduce(FOLDED[:, bass.ds(at * FOLD, FOLD)],
                                         GTURN[:, :].rearrange("p (b i) -> p b i", i=32), AX.X, ALU.add)

            def gem_step(slot, seq_no, vec, at, also=None):
                dve.wait_ge(gem_in[slot], gem_of[slot].add(16))
                if not isinstance(seq_no, int) or seq_no:
                    dve.wait_ge(gem_done, seq_no)
                if also is not None:
                    after(gem_tile(slot, also, at + (T_2 - T_ADA)))
                gem_tile(slot, vec, at).then_inc(gem_done, 1)

            summed = [0]

            def mod_columns(c0, c1, bias):
                summed[0] += 1
                dve.wait_ge(mod_summed, summed[0])
                after(dve.tensor_tensor(MOD[:, c0:c1], bank[5][:, c0:c1], COL2[:, bias:bias + c1 - c0], ALU.add))

            def factors(dst, scale, weight):
                return dve.scalar_tensor_tensor(out=AMOD[:, dst:dst + KC], in0=MOD[:, scale:scale + KC], scalar=1.0,
                                                in1=COL1[:, weight:weight + KC], op0=ALU.add, op1=ALU.mult)

            def half_gate(i):
                return dve.tensor_scalar(GHALF[:, i * KC:(i + 1) * KC], MOD[:, i * 24 + 16:i * 24 + 24], 0.5, None, ALU.mult)

            def norm(factor, shift, between=None):
                dve.wait_ge(std_ready, std.add())
                after(dve.reciprocal(RINV[:, :], RINV[:, :]))
                start = h_own.n

                def normed(k):
                    if k >= 4:
                        dve.wait_ge(h_ready, start + k - 3)
                    dve.scalar_tensor_tensor(out=chunk(NRM, k % 4), in0=chunk(X, k), scalar=AMOD[:, factor + k:factor + k + 1],
                                             in1=RINV[:, :], op0=ALU.mult, op1=ALU.mult).then_inc(un_ready, 1)

                normed(0)
                normed(1)
                for k in range(KC):
                    dve.wait_ge(nhi_ready, nhi.add())
                    dve.scalar_tensor_tensor(out=chunk(H_LO, k), in0=chunk(NRM, k % 4), scalar=MOD[:, shift + k:shift + k + 1],
                                             in1=chunk(H_HI, k).bitcast(F32), op0=ALU.add, op1=ALU.subtract).then_inc(h_ready, 1)
                    h_own.add()
                    if k + 2 < KC:
                        normed(k + 2)
                    if between is not None and k % 2:
                        between(k // 2)

            def ffn_up(u0, chunks, seq_no=0, vec=None, tile=None, also=None):
                per = GEM_RING if vec is not None else 2
                gem = []
                if vec is not None:
                    gem = [(t, 16) for t in gem_of] + [(seq, 4 * gem_seq + (2 * (gem_seq + 1) if also is not None else 0))]
                with loop(dve, chunks // per, (silu, per), (ahi, per), (alo_own, per), *gem) as it:
                    for c in range(per):
                        p, g = c % 2, u0 + 2 * c
                        split_next(u0, it, 2 * c, 2 * per)
                        dve.wait_ge(alo_ready, alo_own.add(0) - 1)
                        alo_own.add()
                        dve.wait_ge(silu_ready, silu.add())
                        dve.wait_ge(strip_done, it * 2 * per + (g + 2 + RING))
                        dve.tensor_tensor(HF[:, p * S:(p + 1) * S], SG[:, p * S:(p + 1) * S], bank[(g + 1) % RING][:, :],
                                          ALU.mult).then_inc(bank_free, 2)
                        split_next(u0, it, 2 * c + 1, 2 * per)
                        dve.wait_ge(ahi_ready, ahi.add())
                        dve.tensor_tensor(chunk(A_LO, it * per + c), HF[:, p * S:(p + 1) * S],
                                          chunk(A_HI, it * per + c).bitcast(F32), ALU.subtract).then_inc(alo_ready, 1)
                        if vec is not None:
                            gem_step(c, it * GEM_RING + (seq_no + c), vec, tile(it, c), also if c % 2 == 0 else None)

            def down(u0, gate, gate0, seq_no=0, vec=None, tile=None, gem_at=()):
                def turn(it, strips):
                    for j in strips:
                        split_next(u0, it, j)
                        dve.wait_ge(strip_done, it * RING + (u0 + j + 1 + RING))
                        dve.scalar_tensor_tensor(out=chunk(X, it * RING + j), in0=bank[(u0 + j) % RING][:, :],
                                                 scalar=gate[:, bass.ds(it * RING + (gate0 + j), 1)],
                                                 in1=chunk(X, it * RING + j), op0=ALU.mult, op1=ALU.add).then_inc(bank_free, 1)
                        if j in gem_at:
                            g = gem_at.index(j)
                            gem_step(g, seq_no + g, vec, tile(0, g))

                if gem_at or u0 + KC == STRIPS:
                    turn(0, range(KC))
                else:
                    with loop(dve, KC // RING) as it:
                        turn(it, range(RING))

            def ffn(u, f, seq_no, vec, gate0, also, after_up, after_down):
                for part, (_, chunks) in enumerate(FFN_PARTS):
                    ups, tile_up, downs, tile_down = GEM_PLAN[f][part]
                    ffn_up(u, chunks, seq_no, vec if ups else None, tile_up, also)
                    after_up[part]()
                    u, seq_no = u + 2 * chunks, seq_no + ups
                    down(u, GHALF, gate0, seq_no, vec, tile_down, gem_after(part) if downs else ())
                    after_down[part]()
                    u, seq_no = u + KC, seq_no + downs

            def attend(n0, keys, masked, scale, prob, output):
                for n in range(TT * H + 4):
                    if n < TT * H:
                        dve.wait_ge(score_done, n0 + n + 1)
                        after(masked(n, bank[n % 4]))
                        after(dve.tensor_reduce(soft(n, 0), bank[n % 4][:, 0:keys(n)], AX.X, ALU.max))
                        dve.tensor_scalar(soft(n, 1), soft(n, 0), -scale, None, ALU.mult).then_inc(neg_ready, 1)
                    if 0 <= n - 1 < TT * H:
                        m = n - 1
                        dve.wait_ge(exp_done, n0 + m + 1)
                        after(dve.reciprocal(soft(m, 3), soft(m, 2)))
                        p = prob[:, m % 4 * S:m % 4 * S + keys(m)]
                        dve.tensor_scalar(p, p, soft(m, 3), None, ALU.mult).then_inc(prob_ready, 1)
                    if n >= 4 and (n - 3) % (2 * TT) == 0:
                        c = (n - 3) // (2 * TT) - 1
                        dve.wait_ge(ohi_ready, n0 // (2 * TT) + c + 1)
                        output(c, bank[6 + c % 2][:, :]).then_inc(olo_ready, 1)

            def mixer1():
                norm(A_1 + KC, 24)
                for j in range(4):
                    split_next(U_LATENT, 0, j)
                    dve.wait_ge(strip_done, U_LATENT + j + 1 + RING)
                    cols = DR if j == 3 else P
                    dve.tensor_copy((CQT[:, 0:S], CQT[:, S:2 * S], CKVT[:, :], KRF[:, :])[j],
                                    bank[(U_LATENT + j) % RING][0:cols, :]).then_inc(bank_free, 1)
                ub = [UB[:, j * UPAD:(j + 1) * UPAD] for j in range(4)]
                for j in range(4):
                    ins = dve.memset(ub[j][:, 0:CK - 1], 0.0)
                after(ins)
                for j in range(4):
                    split_next(U_CONV, 0, j)
                    dve.wait_ge(strip_done, U_CONV + j + 1 + RING)
                    dve.tensor_copy(chunk(XV, j), bank[(U_CONV + j) % RING][:, :]).then_inc(bank_free, 1)
                dve.wait_ge(lat_std, 2)
                after(dve.reciprocal(UN[:, S:2 * S], UN[:, S:2 * S]))
                after(dve.reciprocal(RINV[:, :], RINV[:, :]))
                for k in range(2):
                    after(dve.scalar_tensor_tensor(out=chunk(CQT, k), in0=chunk(CQT, k), scalar=COL1[:, V_QA + k:V_QA + k + 1],
                                                   in1=UN[:, S:2 * S], op0=ALU.mult, op1=ALU.mult))
                after(dve.scalar_tensor_tensor(out=CKVT[:, :], in0=CKVT[:, :], scalar=COL1[:, V_KVA:V_KVA + 1],
                                               in1=RINV[:, :], op0=ALU.mult, op1=ALU.mult))
                dve.wait_ge(kr_turned, 1)
                after(dve.tensor_copy(KRT[:, :], bank[6][:, 0:TT * DR]))
                dve.sem_inc(lat_ready, 1)
                for j in range(4):
                    split_next(U_CONV + 4, 0, j)
                    dve.wait_ge(strip_done, U_CONV + 4 + j + 1 + RING)
                    ins = dve.tensor_tensor(ub[j][:, CK - 1:], bank[(U_CONV + j) % RING][:, :], chunk(XV, j), ALU.mult)
                    ins.then_inc(bank_free, 1)
                    dve.wait_ge(bank_free, U_CONV + 4 + j + 1 + RING)
                    taps = [COL1[:, V_CONV + t * 4 + j:V_CONV + t * 4 + j + 1] for t in range(CK)]
                    after(dve.tensor_scalar(chunk(XV, j), ub[j][:, 0:S], taps[0], None, ALU.mult))
                    for t in range(1, CK):
                        after(dve.scalar_tensor_tensor(out=chunk(XV, j), in0=ub[j][:, t:t + S], scalar=taps[t],
                                                       in1=chunk(XV, j), op0=ALU.mult, op1=ALU.add))
                dve.wait_ge(head_in, 16 * 7)
                n = TT * DR // 2
                ang, tmp = ANGLE[:, 0:n], SIN[:, :]
                after(dve.tensor_copy(STAT[:, 100:100 + TT], POS[:, :]))
                for t in range(TT):
                    ins = dve.tensor_scalar(ang[:, t * DR // 2:(t + 1) * DR // 2], FREQ[:, :], STAT[:, 100 + t:101 + t], None, ALU.mult)
                after(ins)
                for i, (quarter, add) in enumerate(((0.0, 0.0), (0.25, np.pi / 2))):
                    r = ANGLE[:, (i + 1) * n:(i + 2) * n]
                    after(dve.tensor_scalar(tmp, ang, 1 / (2 * np.pi), quarter, ALU.mult, ALU.add))
                    after(dve.tensor_scalar(tmp, tmp, ROUND, ROUND, ALU.add, ALU.subtract))
                    src = ang
                    for part in TURN:
                        after(dve.scalar_tensor_tensor(out=r, in0=tmp, scalar=-part, in1=src, op0=ALU.mult, op1=ALU.add))
                        src = r
                    after(dve.tensor_scalar(r, r, float(add), None, ALU.add))
                    after(dve.tensor_scalar(r, r, HALF_TURN, -HALF_TURN, ALU.min, ALU.max))
                dve.sem_inc(angle_ready, 1)
                for j in range(4):
                    split_next(U_CONV + 8, 0, j)
                    dve.wait_ge(strip_done, U_CONV + 8 + j + 1 + RING)
                    dve.tensor_tensor(chunk(XV, j), bank[(U_CONV + j) % RING][:, :], chunk(XV, j), ALU.mult).then_inc(bank_free, 1)
                    dve.wait_ge(bank_free, U_CONV + 8 + j + 1 + RING)
                    after(dve.tensor_copy(chunk(A_HI, 4 + j), chunk(XV, j)))
                    dve.tensor_tensor(chunk(A_LO, 4 + j), chunk(XV, j), chunk(A_HI, 4 + j).bitcast(F32),
                                      ALU.subtract).then_inc(mixed, 1)
                dve.wait_ge(sin_ready, 2)
                dve.wait_ge(mixed, 4)
                wq, wk = HEADW[:, 0:DN], HEADW[:, DN:2 * DN]
                wqr, wkr = HEADW[:, 2 * DN:2 * DN + DR], HEADW[:, 2 * DN + DR:]

                def over_heads(ap, heads=H):
                    return ap.unsqueeze(1).to_broadcast([P, heads, ap.shape[1]])

                def over_features(ap, n):
                    return ap.unsqueeze(2).to_broadcast([P, ap.shape[1], n])

                def scaled(x, inv, w):
                    after(dve.tensor_tensor(x, x, over_features(inv, x.shape[2]), ALU.mult))
                    after(dve.tensor_tensor(x, x, over_heads(w, x.shape[1]), ALU.mult))

                def rotated(x, t, tmp):
                    heads = x.shape[1]
                    cos, sin = (over_heads(chunk(z, t, DR // 2), heads) for z in (COS, SIN))
                    x1, x2 = x[:, :, 0:DR // 2], x[:, :, DR // 2:]
                    m = [tmp[:, i * heads * DR // 2:(i + 1) * heads * DR // 2].rearrange("p (h d) -> p h d", h=heads) for i in range(4)]
                    dve.tensor_tensor(m[0], x1, cos, ALU.mult)
                    dve.tensor_tensor(m[1], x2, sin, ALU.mult)
                    dve.tensor_tensor(m[2], x2, cos, ALU.mult)
                    after(dve.tensor_tensor(m[3], x1, sin, ALU.mult))
                    dve.tensor_tensor(x1, m[0], m[1], ALU.subtract)
                    after(dve.tensor_tensor(x2, m[2], m[3], ALU.add))

                with loop(dve, TT, (seq, 14), (hsq, 3), (hstd, 2)) as t:
                    q, k = heads(chunk(QTOK, t, H * DQ)), heads(chunk(KTOK, t, H * DQ))
                    kr = chunk(KRT, t, DR).unsqueeze(1)
                    split_next(U_GATE, t, 0)
                    dve.wait_ge(head_sq, hsq.add(3))
                    dve.tensor_reduce(STAT[:, 0:H], heads(TQ0[:, :])[:, :, 0:DN], AX.X, ALU.add)
                    dve.tensor_reduce(STAT[:, H:2 * H], TQ1[:, 0:H * DN].rearrange("p (h d) -> p h d", h=H), AX.X, ALU.add)
                    dve.tensor_reduce(STAT[:, 2 * H:3 * H], heads(TQ0[:, :])[:, :, DN:], AX.X, ALU.add)
                    dve.tensor_reduce(STAT[:, 3 * H:3 * H + 1], TQ1[:, H * DN:H * DN + DR], AX.X, ALU.add).then_inc(head_sum, 1)
                    split_next(U_GATE, t, 1)
                    dve.wait_ge(head_std, hstd.add(2))
                    after(dve.reciprocal(STAT[:, 32:32 + 3 * H + 1], STAT[:, 0:3 * H + 1]))
                    scaled(q[:, :, 0:DN], STAT[:, 32:32 + H], wq)
                    scaled(q[:, :, DN:], STAT[:, 32 + 2 * H:32 + 3 * H], wqr)
                    rotated(q[:, :, DN:], t, RINV[:, :])
                    split_next(U_GATE, t, 2)
                    scaled(k[:, :, 0:DN], STAT[:, 32 + H:32 + 2 * H], wk)
                    scaled(kr, STAT[:, 32 + 3 * H:32 + 3 * H + 1], wkr)
                    rotated(kr, t, UN[:, 800:])
                    after(dve.tensor_copy(k[:, :, DN:], kr.to_broadcast([P, H, DR])))
                    dve.sem_inc(k_ready, 1)
                    split_next(U_GATE, t, 3)
                for n in range(1, 2 * H + TT, 2):
                    dve.wait_ge(turned, n + 1)
                    if n < 2 * H:
                        ins = dve.tensor_copy(chunk(KT, n // 2), bank[4 + n % 4][0:DQ, :])
                    else:
                        ins = dve.tensor_copy(chunk(V, n - 2 * H), bank[4 + n % 4][:, :])
                    ins.then_inc(turn_dve, 1)
                def causal(n, scores):
                    last = scores[:, n % TT * P:(n % TT + 1) * P]
                    return dve.tensor_tensor(last, last, CAUSAL[:, :], ALU.add)

                attend(0, lambda n: (n % TT + 1) * P, causal, DQ ** -0.5, PROB,
                       lambda c, src: dve.tensor_tensor(chunk(A_LO, c), src, chunk(A_HI, c).bitcast(F32), ALU.subtract))
                with loop(dve, KC // RING, (seq, 2 * RING)) as it:
                    for j in range(RING):
                        b, un = (U_BRANCH + j) % RING, UN[:, j % 2 * S:(j % 2 + 1) * S]
                        split_next(U_BRANCH, it, j)
                        dve.wait_ge(strip_done, it * RING + (U_BRANCH + j + 1 + RING))
                        after(dve.tensor_tensor(un, bank[b][:, :], chunk(GATES, it * RING + j), ALU.mult))
                        after(dve.tensor_tensor(RINV[:, :], bank[4 + b][:, :], chunk(GATES, it * RING + (KC + j)), ALU.mult))
                        dve.sem_inc(bank_free, 1)
                        dve.tensor_tensor(un, un, RINV[:, :], ALU.add).then_inc(merged, 1)
                        dve.wait_ge(mhi_ready, it * RING + (j + 1))
                        dve.tensor_tensor(chunk(H_LO, it * RING + j), un, chunk(H_HI, it * RING + j).bitcast(F32),
                                          ALU.subtract).then_inc(mlo_ready, 1)
                down(U_OUT, MOD, 40)

            def mixer2():
                dve.wait_ge(gem_done, T_2)

                def context_strip(s):
                    split_next(U_CTX, 0, s)
                    dve.wait_ge(strip_done, U_CTX + s + 1 + RING)
                    dst = KT2[:, s * KEYS + S:(s + 1) * KEYS] if s < 4 else chunk(VTC, s - 4, CTX)
                    dve.tensor_copy(dst, bank[(U_CTX + s) % RING][:, 0:CTX]).then_inc(bank_free, 1)

                for s in range(4):
                    context_strip(s)
                norm(A_2, M_2, lambda i: context_strip(4 + i))
                cv = [CV[:, c * CPAD:(c + 1) * CPAD] for c in range(2)]
                for c in range(2):
                    dve.memset(cv[c][:, 0:PAD2], 0.0)
                    ins = dve.memset(cv[c][:, PAD2 + S:], 0.0)
                after(ins)
                taps = [(c, t) for c in range(2) for t in range(CK2)]

                def convolve(count):
                    for c, t in taps[:count]:
                        tap, v = COL3[:, 2 * t + c:2 * t + c + 1], cv[c][:, t:t + S]
                        if t == 0:
                            ins = dve.tensor_scalar(chunk(ACC, c), v, tap, COL1[:, V_DWB + c:V_DWB + c + 1], ALU.mult, ALU.add)
                        else:
                            ins = dve.scalar_tensor_tensor(out=chunk(ACC, c), in0=v, scalar=tap, in1=chunk(ACC, c),
                                                           op0=ALU.mult, op1=ALU.add)
                        after(ins)
                        if t == CK2 - 1:
                            dve.sem_inc(conv_ready, 1)
                    del taps[:count]

                def turned_values(n):
                    dve.wait_ge(vw_turned, n + 1)
                    dve.tensor_copy(window_values(n), window_bank(n)).then_inc(vw_dve, 1)

                for s in range(len(IN2_COLS)):
                    u = U_IN2 + s
                    split_next(U_IN2, 0, s)
                    if s < 2:
                        dve.wait_ge(strip_done, u + 1 + RING)
                        dve.tensor_copy(chunk(UT, s), bank[u % RING][:, :]).then_inc(bank_free, 1)
                    elif s in (3, 5):
                        c = s // 2 - 1
                        dve.wait_ge(strip_done, u + 1 + RING)
                        dve.wait_ge(sig_ready, c + 1)
                        ins = dve.tensor_tensor(cv[c][:, PAD2:PAD2 + S], bank[u % RING][:, :], SQ[:, c * S:(c + 1) * S], ALU.mult)
                        ins.then_inc(bank_free, 2)
                        dve.wait_ge(bank_free, u + 1 + RING)
                    if s >= 3:
                        convolve(5)
                    if s >= 15:
                        turned_values(2 * (s - 15) + 1)
                for t in (1, 3):
                    dve.wait_ge(uc_done, t + 1)
                    dve.tensor_copy(chunk(UC, t), bank[t][:, :]).then_inc(uc_dve, 1)
                for n in (7, 9):
                    turned_values(n)
                dve.wait_ge(ln_sum, 1)
                for c in range(2):
                    dve.scalar_tensor_tensor(out=chunk(ACC, c), in0=bank[4][:, :], scalar=-1.0 / CW2, in1=chunk(ACC, c),
                                             op0=ALU.mult, op1=ALU.add).then_inc(dev_ready, 1)
                dve.wait_ge(ft_done, 2)
                dve.tensor_copy(chunk(FT, 1), bank[1][:, :]).then_inc(ft_dve, 1)
                dve.wait_ge(ln_std, 1)
                after(dve.reciprocal(bank[4][:, :], bank[4][:, :]))
                for c in range(2):
                    dve.tensor_tensor(chunk(ACC, c), chunk(ACC, c), bank[4][:, :], ALU.mult).then_inc(z_ready, 1)
                for h in range(H):
                    dve.wait_ge(rpb_turned, h + 1)
                    span = bank[5 + h % 3][:, 0:SPAN]
                    for v in range(3):
                        first = WIN - v * WIN // 2
                        ins = dve.tensor_tensor(chunk(BIAS, v * H + h, ROWS * KW).rearrange("p (k c) -> p k c", k=ROWS),
                                                bass.AP(span.tensor, span.offset + first, [span.ap[0], [RPB_C, ROWS], [1, KW]]),
                                                MASK[:, v * KW:(v + 1) * KW].unsqueeze(1).to_broadcast([P, ROWS, KW]), ALU.add)
                    ins.then_inc(bias_ready, 1)
                for m in range(4):
                    dve.wait_ge(mix_hi, m + 1)
                    lo, hi = chunk(A_LO, m), chunk(A_HI, m).bitcast(F32)
                    if m < 2:
                        ins = dve.tensor_tensor(lo, bank[2 + m][:, :], hi, ALU.subtract)
                    else:
                        ins = dve.scalar_tensor_tensor(out=lo, in0=bank[m - 2][:, :], scalar=COL1[:, V_PWB + m - 2:V_PWB + m - 1],
                                                       in1=hi, op0=ALU.add, op1=ALU.subtract)
                    ins.then_inc(mixed, 1)

                def biased(n, scores):
                    h, j = n // TT, n % TT
                    return dve.tensor_tensor(scores[:, 0:ROWS * KW], scores[:, 0:ROWS * KW],
                                             chunk(BIAS, VARIANT[j] * H + h, ROWS * KW), ALU.add)

                attend(TT * H, lambda n: S, biased, 1.0, PROB2,
                       lambda c, src: dve.tensor_tensor(by_rows(chunk(A_LO, 4 + c)), by_tiles(src),
                                                        by_rows(chunk(A_HI, 4 + c).bitcast(F32)), ALU.subtract))
                down(U_OUT2, MOD, M_2 + 2 * KC)

            def mlp():
                norm(A_2 + KC, M_2 + 3 * KC)
                for part in range(MLP_PARTS):
                    u = U_MLP + 2 * KC * part
                    with loop(dve, KC // RING, (silu, RING), (ahi, RING), (alo_own, RING)) as it:
                        for j in range(RING):
                            hf = HF[:, j % 2 * S:(j % 2 + 1) * S]
                            split_next(u, it, j)
                            dve.wait_ge(alo_ready, alo_own.add(0))
                            alo_own.add()
                            dve.wait_ge(silu_ready, silu.add())
                            dve.tensor_tensor(hf, SG[:, j % 2 * S:(j % 2 + 1) * S], bank[(u + j) % RING][:, :],
                                              ALU.mult).then_inc(bank_free, 1)
                            dve.wait_ge(ahi_ready, ahi.add())
                            dve.tensor_tensor(chunk(A_LO, it * RING + j), hf, chunk(A_HI, it * RING + j).bitcast(F32),
                                              ALU.subtract).then_inc(alo_ready, 1)
                    down(u + KC, MOD, M_2 + 5 * KC)

            def nothing():
                pass

            def first_gate():
                mod_columns(16, 24, 16)
                after(half_gate(0))

            def mixer_modulation():
                mod_columns(24, 64, 24)
                factors(A_1 + KC, 24 + KC, V_NORM + KC)
                after(factors(A_1 + 2 * KC, 48 + KC, V_NORM + 2 * KC))

            def last_gate():
                mod_columns(64, M_2, 64)
                after(half_gate(2))

            def second_modulation():
                mod_columns(M_2, M_CTX, M_2)
                factors(A_2, M_2 + KC, V_N1G)
                after(factors(A_2 + KC, M_2 + 4 * KC, V_N2G))

            def context_rms():
                dve.wait_ge(ctx_std, 1)
                after(dve.reciprocal(STAT[:, 204:206], STAT[:, 200:202]))
                for j in range(2):
                    dve.tensor_scalar(CTOK[:, j * D:(j + 1) * D], CTOK[:, j * D:(j + 1) * D], STAT[:, 204 + j:205 + j], None,
                                      ALU.mult).then_inc(ctx_ready, 1)

            def context():
                mod_columns(M_CTX, M_COLS, M_2)
                dve.sem_inc(ctx_mod, 1)
                after(factors(A_CTX, M_CTX + KC, V_N1G))
                for k in range(KC + 1):
                    if k < KC:
                        dve.wait_ge(ctx_turned, k // 2 + 1)
                        if k >= 4:
                            dve.wait_ge(clo_ready, k - 3)
                        dve.tensor_scalar(chunk(HF, k % 4, CTX), bank[(4, 6, 7, 5)[k // 2]][:, k % 2 * CTX:(k % 2 + 1) * CTX],
                                          AMOD[:, A_CTX + k:A_CTX + k + 1], MOD[:, M_CTX + k:M_CTX + k + 1],
                                          ALU.mult, ALU.add).then_inc(ctx_full, 1)
                    if k >= 1:
                        dve.wait_ge(chi_ready, k)
                        dve.tensor_tensor(chunk(C_LO, k - 1, CTX), chunk(HF, (k - 1) % 4, CTX),
                                          chunk(C_HI, k - 1, CTX).bitcast(F32), ALU.subtract).then_inc(clo_ready, 1)

            dve.sem_inc(lo_ready, RING)
            dve.sem_inc(h_ready, 2)
            dve.sem_inc(alo_ready, 2)
            dve.wait_ge(cond_ready, 1)
            for t in range(8):
                gem_step(t % GEM_RING, t, C_1, t)
            for u in range(LEAD):
                split_lo(u, u)
            dve.wait_ge(cols_ready, 2)
            mod_columns(0, 16, 0)
            after(factors(A_1, KC, V_NORM))
            norm(A_1, 0)
            ffn(U_FFN0, 0, 8, C_1, 0, None, [first_gate, nothing, mixer_modulation], [nothing] * 3)
            mixer1()
            norm(A_1 + 2 * KC, 48)
            ffn(U_FFN1, 1, T_ADA, C_2, 2 * KC, C_CTX, [last_gate, context_rms, second_modulation], [nothing, context, nothing])
            mixer2()
            mlp()
            dve.wait_ge(std_ready, std.add())
            after(dve.reciprocal(RINV[:, :], RINV[:, :]))
            for k in range(KC):
                dve.scalar_tensor_tensor(out=chunk(YT, k), in0=chunk(X, k), scalar=COL1[:, V_FIN + k:V_FIN + k + 1],
                                         in1=RINV[:, :], op0=ALU.mult, op1=ALU.mult).then_inc(y_ready, 1)
            for t in range(TT):
                dve.wait_ge(y_turned, 2 * t + 2)
                dve.tensor_copy(YTOK[:, t * D + S:(t + 1) * D], bank[7][:, :]).then_inc(ytok_ready, 1)


_INS = ["x", "c", "positions", "w_ada", "b_ada", "norm_w", "ffn_w13", "ffn_w2", "w_in", "q_a_norm", "w_uq", "kv_a_norm",
        "w_ukv", "q_norm_nope", "k_norm_nope", "q_norm_rope", "k_norm_rope", "conv_w", "w_branch", "w_out", "c_2",
        "ctx_2", "c_ctx_2", "ada_w_2", "ada_b_2", "norm1_g_2", "norm2_g_2", "w_in_2", "w_fourier_2", "conv_dw_w_2",
        "conv_dw_b_2", "conv_norm_g_2", "conv_norm_b_2", "conv_pw_w_2", "conv_pw_b_2", "na_rpb_2", "w_out_2",
        "mlp_w1_2", "mlp_w2_2", "final_norm_g_2"]


def constants():
    f = 1.0 / np.float32(10000) ** (np.arange(0, DR, 2, dtype=np.float32) / np.float32(DR))
    feat = np.arange(DH)
    turn = 2 * np.pi * np.outer(feat, feat) / DH
    two = np.kron(np.eye(2), np.cos(turn)), np.kron(np.eye(2), np.sin(turn))
    tok = np.arange(S)
    turn = 2 * np.pi * (np.outer(tok, tok) % S) / S
    scale = 1.0 / np.sqrt(S * DH)
    q, k = np.arange(P)[:, None], np.arange(P)[None, :]
    near = np.zeros((P, 3, KW), np.float32)
    for v, (tile, w) in enumerate(((0, 0), (1, 8), (3, 32))):
        col, key = QC * tile + np.arange(P)[:, None] % QC, w + np.arange(KW)[None, :]
        first = np.clip(col - WIN // 2, 0, COLS - WIN)
        near[:, v] = np.where((key >= first) & (key < first + WIN), 0.0, NEG)
    return {
        "rope_freq": np.tile(f.astype(np.float32), (P, 1)),
        "dft_feat": np.concatenate(two, axis=1).astype(np.float32),
        "dft_tok": np.stack([np.cos(turn) * scale, -np.sin(turn) * scale]).astype(np.float32),
        "causal": np.where(k <= q, 0.0, NEG).astype(np.float32),
        "near": near,
    }


def kernel(**inputs):
    import concourse.bacc as bacc
    from concourse.bass_utils import run_bass_kernel_spmd as run

    nc = bacc.Bacc("TRN2", target_bir_lowering=False, num_devices=1)
    arrays, aps = {}, {}
    given = {n: np.ascontiguousarray(inputs[n]) for n in _INS}
    for name, v in {**given, **constants()}.items():
        arrays[f"in_{name}"] = v
        aps[name] = nc.dram_tensor(f"in_{name}", v.shape, mybir.dt.from_np(v.dtype), kind="ExternalInput").ap()
    out = nc.dram_tensor("out_0", (1, S, D), F32, kind="ExternalOutput").ap()
    block_pair_kernel(nc, aps, out)
    r = run(nc, [arrays], core_ids=[0])
    return r.results[0]["out_0"]
```

```python
import numpy as np
import concourse.bass as bass
from concourse import mybir
from contextlib import ExitStack, contextmanager

F32 = mybir.dt.float32
F32R = mybir.dt.float32r
I32 = mybir.dt.int32
ALU = mybir.AluOpType
ACT = mybir.ActivationFunctionType
AX = mybir.AxisListType

P = 128
D = 1024
KC = D // P
S = 512
TT = S // P
CTX = 256
FF = 2816
EPS, LN_EPS = 1e-6, 1e-5
H = 8
DN, DR, DV = 64, 32, 64
DQ = DN + DR
QR, KR = 256, 128
CW, CK = 512, 3
COLS, ROWS = 64, 8
WIN = 16
QC = 16
KW = 32
NEAR = (0, QC // 2, QC // 2 + WIN, 2 * WIN)
VARIANT = (0, 1, 1, 2)
RPB_R, RPB_C = 2 * ROWS - 1, 2 * WIN - 1
SPAN = (ROWS - 1) * RPB_C + KW + WIN
BIAS_BANKS = (2, 3, 5)
SPAN_IN = SPAN - SPAN % 16
CW2, CK2 = 256, 31
PAD2 = CK2 // 2
DH = 64
NEG = -1e30
ROUND = 1.5 * 2.0 ** 23
HALF_TURN = float(np.float32(np.pi)) - 2.0 ** -22
TURN = (6.28125, 0.0019354820251464844, -1.7484555314695172e-07)

RING = 4
LEAD = 3
STRIP = KC * P
GEM = 256
GEM_RING = 4
FOLD = GEM // 32

FFN_PARTS = [(0, 8), (8, 8), (16, 6)]
FFN_STRIPS = sum(2 * n + KC for _, n in FFN_PARTS)
U_FFN0 = 0
U_LATENT = U_FFN0 + FFN_STRIPS
U_CONV = U_LATENT + 4
U_GATE = U_CONV + 12
U_BRANCH = U_GATE + 16
U_OUT = U_BRANCH + KC
U_FFN1 = U_OUT + KC
U_CTX = U_FFN1 + FFN_STRIPS
U_IN2 = U_CTX + 8
U_OUT2 = U_IN2 + 18
U_MLP = U_OUT2 + KC
MLP_PARTS = 4
STRIPS = U_MLP + MLP_PARTS * 2 * KC

V_NORM, V_N1G, V_N2G, V_FIN = 0, 24, 32, 40
V_QA, V_KVA, V_DWB, V_LNG, V_LNB, V_PWB, V_CONV, V_ROWS = 48, 50, 51, 53, 55, 57, 59, 71
C_1, C_2, C_CTX = 0, 8, 16
M_2, M_CTX, M_COLS = 72, 120, 136
A_1, A_2, A_CTX, A_COLS = 0, 24, 40, 48


class Tally:

    def __init__(self, sem):
        self.sem, self.n, self.it, self.per, self.start = sem, 0, None, 0, 0

    def enter(self, it, per):
        self.it, self.per, self.start = it, per, self.n

    def leave(self, times):
        assert self.n == self.start + self.per, (self.sem, self.n, self.start, self.per)
        self.n, self.it = self.start + self.per * times, None

    def add(self, k=1):
        self.n += k
        return self.n if self.it is None else self.it * self.per + self.n


@contextmanager
def loop(eng, times, *tallies):
    if times == 1:
        yield 0
        return
    with eng.Fori(0, times) as it:
        for t, per in tallies:
            t.enter(it, per)
        yield it
        for t, per in tallies:
            t.leave(times)


def block_pair_kernel(nc, a, out):
    with ExitStack() as ctx:
        place = [(nc.sbuf_base + 63) // 64 * 64]

        def sb(name, shape, dt=F32, over=None):
            size = int(np.prod(shape[1:])) * 4
            offset = place[0] if over is None else over
            if over is None:
                place[0] += (size + 63) // 64 * 64
            t = nc.alloc_sbuf_tensor_at(name, shape, dt, offset=offset)
            where[name] = offset
            return t

        where = {}
        X = sb("X", [P, KC * S])
        H_HI = sb("H_HI", [P, KC * S], F32R)
        H_LO = sb("H_LO", [P, KC * S], F32R)
        place[0] += 64
        A_HI = sb("A_HI", [P, KC * S], F32R)
        A_LO = sb("A_LO", [P, KC * S], F32R)
        RAW = sb("RAW", [P, RING * STRIP])
        W_HI = sb("W_HI", [P, RING * STRIP], F32R)
        W_LO = sb("W_LO", [P, RING * STRIP], F32R)
        COL1 = sb("COL1", [P, V_ROWS + 1])
        CRAW = sb("CRAW", [P, 3 * KC])
        COL2 = sb("COL2", [P, M_CTX])
        COL3 = sb("COL3", [P, 2 * CK2])
        CSIL = sb("CSIL", [P, 3 * KC])
        IDENT = sb("IDENT", [P, P])
        ONES = sb("ONES", [P, P])
        FLIP = sb("FLIP", [P, P])
        SUM32 = sb("SUM32", [P, 32])
        MOD = sb("MOD", [P, M_COLS])
        AMOD = sb("AMOD", [P, A_COLS])
        GHALF = sb("GHALF", [P, 3 * KC])
        CONST = sb("CONST", [P, 4])
        STAT = sb("STAT", [P, 256])
        FOLDED = sb("FOLDED", [P, M_COLS * 4])
        SQ = sb("SQ", [P, 2 * S])
        UN = sb("UN", [P, 2 * S])
        NRM = sb("NRM", [P, 4 * S], over=where["SQ"])
        RINV = sb("RINV", [P, S])
        DIAG = sb("DIAG", [P, S], over=where["RINV"])
        RMS = sb("RMS", [P, 2 * TT])
        SG = sb("SG", [P, 2 * S], over=where["SQ"])
        HF = sb("HF", [P, 2 * S], over=where["UN"])
        SSUM = sb("SSUM", [P, S])
        scratch = place[0]
        assert scratch + 60 * 1024 <= nc.sbuf_usable_end, (scratch, nc.sbuf_usable_end)
        GBUF = sb("GBUF", [P, GEM_RING * KC * GEM], over=scratch)
        GACC = sb("GACC", [P, 2 * GEM], over=scratch + GEM_RING * KC * GEM * 4)
        PBUF = sb("PBUF", [P, 3 * KC * GEM], over=scratch + 35 * 1024)
        GTURN = sb("GTURN", [P, GEM], over=where["GACC"] + 2 * GEM * 4)
        GATES = sb("GATES", [P, 2 * KC * S], over=scratch)
        XV = sb("XV", [P, 4 * S], over=scratch)
        UPAD = S + CK - 1
        UB = sb("UB", [P, 4 * UPAD], over=scratch + 4 * S * 4)
        QTOK = sb("QTOK", [P, TT * H * DQ], over=scratch + 2 * KC * S * 4)
        KTOK = sb("KTOK", [P, TT * H * DQ], over=where["QTOK"] + TT * H * DQ * 4)
        KRF = sb("KRF", [DR, S], over=where["QTOK"])
        V = sb("V", [P, TT * H * DV], over=where["QTOK"])
        small = [where["KTOK"] + TT * H * DQ * 4]

        def small_sb(name, shape, dt=F32):
            t = sb(name, shape, dt, over=small[0])
            small[0] += (int(np.prod(shape[1:])) * 4 + 31) // 32 * 32
            assert small[0] <= nc.sbuf_usable_end
            return t

        POS = small_sb("POS", [P, TT], I32)
        FREQ = small_sb("FREQ", [P, DR // 2])
        HEADW = small_sb("HEADW", [P, 2 * DN + 2 * DR])
        KRT = small_sb("KRT", [P, TT * DR])
        CAUSAL = small_sb("CAUSAL", [P, P])
        ANGLE = small_sb("ANGLE", [P, 3 * TT * DR // 2])
        COS = small_sb("COS", [P, TT * DR // 2])
        SIN = small_sb("SIN", [P, TT * DR // 2])
        UQ = sb("UQ", [P, 2 * H * DQ], over=where["A_HI"])
        CKVT = sb("CKVT", [P, S], over=where["A_HI"] + 2 * H * DQ * 4)
        UKV = sb("UKV", [P, H * (DN + DV)], over=where["A_LO"])
        CQT = sb("CQT", [P, 2 * S], over=where["A_LO"] + H * (DN + DV) * 4)
        QT = sb("QT", [DQ, H * S], over=where["H_HI"])
        KT = sb("KT", [DQ, H * S], over=where["H_LO"])
        PROB = sb("PROB", [P, 4 * S], over=where["V"] + TT * H * DV * 4)
        PT = sb("PT", [P, 3 * S], over=where["PROB"] + 4 * S * 4)
        assert where["PT"] + 3 * S * 4 <= where["KTOK"] + TT * H * DQ * 4
        TQ0 = sb("TQ0", [P, H * DQ], over=where["SQ"])
        TQ1 = sb("TQ1", [P, H * DQ], over=where["UN"])
        CTOK = sb("CTOK", [P, 2 * D], over=scratch + 51 * 1024)
        C_HI = sb("C_HI", [P, KC * CTX], F32R, over=scratch + 35 * 1024)
        C_LO = sb("C_LO", [P, KC * CTX], F32R, over=scratch + 43 * 1024)
        KEYS = S + CTX
        KT2 = sb("KT2", [P, 4 * KEYS], over=scratch)
        QZ = sb("QZ", [P, 8 * S], over=scratch + 12 * 1024)
        VT = sb("VT", [P, 2 * TT * ROWS * KW], over=scratch + 28 * 1024)
        VW = sb("VW", [P, 8 * H * DH], over=scratch + 36 * 1024)
        VTC = sb("VTC", [P, 4 * CTX], over=scratch + 52 * 1024)
        VC = sb("VC", [P, 2 * H * DH], over=scratch + 56 * 1024)
        MASK = sb("MASK", [P, 3 * KW], over=scratch + 60 * 1024)
        assert scratch + 60 * 1024 + 3 * KW * 4 <= nc.sbuf_usable_end
        TCOS = sb("TCOS", [P, TT * S], over=where["A_HI"])
        TSIN = sb("TSIN", [P, TT * S], over=where["A_LO"])
        UT = sb("UT", [P, 2 * S], over=where["A_HI"] + 4 * S * 4)
        FT = sb("FT", [P, 2 * S], over=where["A_HI"] + 4 * S * 4)
        ACC = sb("ACC", [P, 2 * S], over=where["A_HI"] + 6 * S * 4)
        CPAD = S + CK2 - 1
        CV = sb("CV", [P, 2 * CPAD], over=where["A_LO"] + 4 * S * 4)
        DFEAT = sb("DFEAT", [P, 2 * P], over=where["CV"] + 2 * CPAD * 4 // 64 * 64 + 64)
        WF = sb("WF", [P, 2 * 2 * P], over=where["DFEAT"] + 2 * P * 4)
        assert where["WF"] + 4 * P * 4 <= where["A_LO"] + KC * S * 4
        PW = sb("PW", [P, 2 * CW2], over=where["RINV"])
        BIAS = sb("BIAS", [P, 3 * H * ROWS * KW], over=where["H_HI"])
        RPB = sb("RPB", [P, H * SPAN_IN + 16], over=where["H_LO"] + 4 * S * 4)
        assert where["RPB"] + H * SPAN_IN * 4 + 64 == where["A_HI"]
        CSQ = sb("CSQ", [P, 2 * S], over=where["CV"])
        UC = sb("UC", [P, TT * S], over=where["SQ"])
        PT2 = sb("PT2", [P, 3 * S], over=where["RPB"])
        PROB2 = sb("PROB2", [P, 4 * S], over=where["SQ"])
        XTOK = sb("XTOK", [P, TT * D], over=where["A_HI"])
        ROWS1 = sb("ROWS1", [V_ROWS, P], over=where["A_LO"])
        ROWS2 = sb("ROWS2", [M_CTX, P], over=where["A_LO"] + 512)
        ROWS3 = sb("ROWS3", [2 * CK2, P], over=where["A_LO"] + 1024)
        GROW = sb("GROW", [1, 3 * GEM], over=where["A_LO"] + 2048)
        YT = sb("YT", [P, KC * S], over=where["H_HI"])
        YTOK = sb("YTOK", [P, TT * D], over=where["A_HI"])

        bank = [ctx.enter_context(nc.psum_tensor(f"bank{i}", [P, S], F32)) for i in range(8)]

        def sem(name):
            return ctx.enter_context(nc.semaphore(name))

        raw_in = [sem(f"raw_in{i}") for i in range(RING)]
        hi_ready = sem("hi_ready")
        lo_ready = sem("lo_ready")
        strip_done = sem("strip_done")
        bank_free = sem("bank_free")
        rows_in = sem("rows_in")
        x_in = sem("x_in")
        gem_in = [sem(f"gem_in{i}") for i in range(GEM_RING)]
        gem_done = sem("gem_done")
        pe_gem_in = [sem(f"pe_gem_in{i}") for i in range(3)]
        pe_gem_done = sem("pe_gem_done")
        grow_ready = sem("grow_ready")
        ident_ready = sem("ident_ready")
        const_ready = sem("const_ready")
        cols_turned = sem("cols_turned")
        cols_ready = sem("cols_ready")
        cond_in = sem("cond_in")
        cond_ready = sem("cond_ready")
        x_turned = sem("x_turned")
        x_ready = sem("x_ready")
        mod_summed = sem("mod_summed")
        sq_ready = sem("sq_ready")
        sq_used = sem("sq_used")
        stat_ready = sem("stat_ready")
        std_ready = sem("std_ready")
        diag_ready = sem("diag_ready")
        rinv_ready = sem("rinv_ready")
        un_ready = sem("un_ready")
        nhi_ready = sem("nhi_ready")
        h_ready = sem("h_ready")
        silu_ready = sem("silu_ready")
        ahi_ready = sem("ahi_ready")
        alo_ready = sem("alo_ready")
        dve_seq = sem("dve_seq")
        pool_seq = sem("pool_seq")
        up_in = sem("up_in")
        head_in = sem("head_in")
        lat_sq = sem("lat_sq")
        lat_sum = sem("lat_sum")
        lat_std = sem("lat_std")
        lat_ready = sem("lat_ready")
        kr_turned = sem("kr_turned")
        angle_ready = sem("angle_ready")
        sin_ready = sem("sin_ready")
        up_done = sem("up_done")
        up_read = sem("up_read")
        head_sq = sem("head_sq")
        head_sum = sem("head_sum")
        head_std = sem("head_std")
        k_ready = sem("k_ready")
        turned = sem("turned")
        turn_act = sem("turn_act")
        turn_dve = sem("turn_dve")
        score_done = sem("score_done")
        neg_ready = sem("neg_ready")
        exp_done = sem("exp_done")
        prob_ready = sem("prob_ready")
        prob_turned = sem("prob_turned")
        pt_ready = sem("pt_ready")
        pv_done = sem("pv_done")
        ohi_ready = sem("ohi_ready")
        olo_ready = sem("olo_ready")
        mixed = sem("mixed")
        merged = sem("merged")
        mhi_ready = sem("mhi_ready")
        mlo_ready = sem("mlo_ready")
        ctx_in = sem("ctx_in")
        ctx_sq = sem("ctx_sq")
        ctx_std = sem("ctx_std")
        ctx_ready = sem("ctx_ready")
        ctx_mod = sem("ctx_mod")
        ctx_turned = sem("ctx_turned")
        ctx_full = sem("ctx_full")
        chi_ready = sem("chi_ready")
        clo_ready = sem("clo_ready")
        flip_ready = sem("flip_ready")
        rpb_in = sem("rpb_in")
        table_in = sem("table_in")
        zeros_ready = sem("zeros_ready")
        sig_ready = sem("sig_ready")
        conv_ready = sem("conv_ready")
        ln_sum = sem("ln_sum")
        dev_ready = sem("dev_ready")
        ln_sq = sem("ln_sq")
        ln_std = sem("ln_std")
        z_ready = sem("z_ready")
        act_ready = sem("act_ready")
        uc_done = sem("uc_done")
        uc_act = sem("uc_act")
        uc_dve = sem("uc_dve")
        ft_done = sem("ft_done")
        ft_act = sem("ft_act")
        ft_dve = sem("ft_dve")
        rpb_turned = sem("rpb_turned")
        bias_ready = sem("bias_ready")
        vw_turned = sem("vw_turned")
        vw_act = sem("vw_act")
        vw_dve = sem("vw_dve")
        mix_done = sem("mix_done")
        mix_hi = sem("mix_hi")
        y_ready = sem("y_ready")
        y_turned = sem("y_turned")
        y_scaled = sem("y_scaled")
        ytok_act = sem("ytok_act")
        ytok_dve = sem("ytok_dve")
        out_done = sem("out_done")

        def chunk(t, k, n=S):
            return t[:, bass.ds(k * n, n)]

        def heads(t):
            return t.rearrange("p (h d) -> p h d", h=H)

        def soft(n, i):
            return STAT[:, 128 + n % 4 * 3 + i:128 + n % 4 * 3 + i + 1]

        def by_rows(t):
            return t.rearrange("p (r j c) -> p j r c", r=ROWS, j=TT)

        def by_tiles(t):
            return t.rearrange("p (j r c) -> p j r c", j=TT, r=ROWS)

        def window_values(n):
            if n >= 8:
                return chunk(VC, n - 8)
            c, half = n // 2, n % 2
            return VW[:, half * 4 * S:(half + 1) * 4 * S].rearrange("p (t f) -> p t f", t=4)[:, :, c * P:(c + 1) * P]

        def window_bank(n):
            b = bank[4 + n % 4][:, :]
            return b if n >= 8 else b.rearrange("p (t f) -> p t f", t=4)

        def strip_of(t, slot):
            return t[:, slot * STRIP:(slot + 1) * STRIP]

        def rows_of(w):
            return w.rearrange("(k p) n -> p k n", p=P)

        w13 = [rows_of(a["ffn_w13"][0, f]) for f in range(2)]
        w2 = [rows_of(a["ffn_w2"][0, f]) for f in range(2)]
        w_in, w_out = rows_of(a["w_in"][0]), rows_of(a["w_out"][0])
        w_branch = rows_of(a["w_branch"][0].rearrange("g k d -> (g k) d"))
        w_ada, ada_2 = rows_of(a["w_ada"][0]), rows_of(a["ada_w_2"][0])
        w_in2, w_out2 = rows_of(a["w_in_2"][0]), rows_of(a["w_out_2"][0])
        w_mlp1, w_mlp2 = rows_of(a["mlp_w1_2"][0]), rows_of(a["mlp_w2_2"][0])

        def gem_ffn0(seq):
            return lambda it, g: it * GEM_RING + (seq + g)

        def gem_up1(part):
            def tile(it, g):
                return it * 2 + (T_ADA + g // 2 + (4 * part if g % 2 else 8 + 8 * part))
            return tile

        def gem_down1(part):
            return lambda it, g: T_ADA + 12 + 8 * part + g

        GEM_PLAN = [[(8, gem_ffn0(8), 4, gem_ffn0(16)), (8, gem_ffn0(20), 4, gem_ffn0(28)), (4, gem_ffn0(32), 0, None)],
                    [(8, gem_up1(0), 4, gem_down1(0)), (8, gem_up1(1), 4, gem_down1(1)), (0, None, 0, None)]]

        GEM_AFTER = (0, 2, 4, 6)

        def up_turn(ups, chunks):
            return 2 if not ups else GEM_RING if ups == chunks else chunks

        T_ADA = 9 * D // GEM
        T_2 = T_ADA + 6 * D // GEM

        rpb = nc.dram_tensor("rpb_padded", (2 * WIN + H * RPB_R * RPB_C,), F32, kind="Internal").ap()
        IN2_COLS = [c * P for c in (0, 1, 4, 2, 5, 3)] + [c * P for c in range(6, 18)]

        block = ctx.enter_context(nc.Block())

        @block.sync
        def _(sp):
            def load_strip(u, slot, src):
                dst = strip_of(RAW, slot)[:, 0:src.shape[1] * src.shape[2]]
                sp.wait_ge(lo_ready, u + 1)
                sp.dma_start(dst.rearrange("p (k n) -> p k n", k=src.shape[1]), src).then_inc(raw_in[slot], 16)

            def load_gem(slot, src):
                dst = GBUF[:, slot * KC * GEM:(slot + 1) * KC * GEM].rearrange("p (k n) -> p k n", k=KC)
                sp.dma_start(dst, src).then_inc(gem_in[slot], 16)

            def load_strips(u0, count, src):
                with loop(sp, count // RING) as it:
                    for j in range(RING):
                        load_strip(it * RING + (u0 + j), (u0 + j) % RING, src(it * RING + j))

            def load_gem_after(slot, seq, src):
                sp.wait_ge(gem_done, seq - (GEM_RING - 1))
                load_gem(slot, src)

            def load_ffn(u, f, seq, w13, w2, src):
                for part, (c0, chunks) in enumerate(FFN_PARTS):
                    ups, tile_up, downs, tile_down = GEM_PLAN[f][part]
                    per = up_turn(ups, chunks)

                    def turn(it, first=0):
                        for j in range(2 * per):
                            col = (it * per + (j // 2 + c0)) * P + (j % 2) * FF
                            if j >= first:
                                load_strip(it * 2 * per + (u + j), (u + j) % RING, w13[:, :, bass.ds(col, P)])
                            if ups and j % 2 and j // 2 < GEM_RING:
                                load_gem_after(j // 2, it * GEM_RING + (seq + j // 2), src(tile_up(it, j // 2)))

                    if u == U_FFN0:
                        turn(0, LEAD)
                        for it in range(1, chunks // per):
                            turn(it)
                    else:
                        with loop(sp, chunks // per) as it:
                            turn(it)
                    u, seq = u + 2 * chunks, seq + ups
                    for m in range(KC):
                        load_strip(u + m, (u + m) % RING, w2[:, c0:c0 + chunks, m * P:(m + 1) * P])
                        if downs and m in GEM_AFTER:
                            g = GEM_AFTER.index(m)
                            load_gem_after(g, seq + g, src(tile_down(0, g)))
                    u, seq = u + KC, seq + downs

            def rows(dst, names):
                at = 0
                for name in names:
                    v = a[name]
                    flat = v.rearrange(" ".join("abc"[:len(v.shape)]) + " -> (" + " ".join("abc"[:len(v.shape)]) + ")") if len(v.shape) > 1 else v
                    n = int(np.prod(v.shape)) // P
                    sp.dma_start(dst[at:at + n, :], flat.rearrange("(r p) -> r p", p=P)).then_inc(rows_in, 16)
                    at += n

            def ada(t):
                return w_ada[:, :, bass.ds(t * GEM, GEM)]

            def ada2(t):
                return ada_2[:, :, bass.ds((t - T_ADA) * GEM, GEM)]

            with nc.allow_non_contiguous_dma(reason="1024 numbers, 8 to a partition"):
                for i, name in enumerate(("c", "c_2", "c_ctx_2")):
                    v = a[name] if len(a[name].shape) > 1 else a[name].unsqueeze(0)
                    sp.dma_start(CRAW[:, i * KC:(i + 1) * KC], v.rearrange("a (k p) -> p (a k)", p=P)).then_inc(cond_in, 16)
            for t in range(GEM_RING):
                load_gem(t, ada(t))
                if t == 1:
                    rows(ROWS1, ["norm_w", "norm1_g_2", "norm2_g_2", "final_norm_g_2", "q_a_norm", "kv_a_norm", "conv_dw_b_2",
                                 "conv_norm_g_2", "conv_norm_b_2", "conv_pw_b_2", "conv_w"])
                    rows(ROWS2, ["b_ada", "ada_b_2"])
                    rows(ROWS3, ["conv_dw_w_2"])
                    for i in range(TT):
                        sp.dma_start(XTOK[:, i * D:(i + 1) * D], a["x"][0, i * P:(i + 1) * P, :]).then_inc(x_in, 16)
                else:
                    i = (0, None, 1, 2)[t]
                    sp.dma_start(PBUF[:, i * KC * GEM:(i + 1) * KC * GEM].rearrange("p (k n) -> p k n", k=KC),
                                 ada(5 + i)).then_inc(pe_gem_in[i], 16)
            load_gem_after(0, GEM_RING, ada(GEM_RING))
            for j in range(LEAD):
                load_strip(U_FFN0 + j, j, w13[0][:, :, j // 2 * P + j % 2 * FF:j // 2 * P + j % 2 * FF + P])
            load_ffn(U_FFN0, 0, 8, w13[0], w2[0], ada)
            with nc.allow_non_contiguous_dma(reason="512 positions, one to a partition"):
                sp.dma_start(POS[:, :], a["positions"].rearrange("a (t p) -> p (a t)", p=P)).then_inc(head_in, 16)
            sp.dma_start(FREQ[:, :], a["rope_freq"]).then_inc(head_in, 16)
            sp.dma_start(CAUSAL[:, :], a["causal"]).then_inc(head_in, 16)
            flat = a["na_rpb_2"].rearrange("a h r c -> (a h r c)")
            n, pad = H * RPB_R * RPB_C, WIN
            for to, frm, size in ((pad, 0, n), (0, 0, pad), (pad + n, n - pad, pad)):
                sp.dma_start(rpb[to:to + size], flat[frm:frm + size]).then_inc(rpb_in, 16)
            at = 0
            for name, n in (("q_norm_nope", DN), ("k_norm_nope", DN), ("q_norm_rope", DR), ("k_norm_rope", DR)):
                sp.dma_start(HEADW[:, at:at + n], a[name].to_broadcast([P, n])).then_inc(head_in, 16)
                at += n
            for j, cols in enumerate((P, P, P, DR)):
                load_strip(U_LATENT + j, (U_LATENT + j) % RING, w_in[:, :, j * P:j * P + cols])
            i3 = QR + KR + DR
            for part in (0, 2, 1):
                u = U_CONV + 4 * (0, 2, 1)[part]
                load_strips(u, 4, lambda m: w_in[:, :, i3 + part * CW + m * P:i3 + part * CW + (m + 1) * P])
                if part == 0:
                    sp.wait_ge(strip_done, U_LATENT + RING)
                    sp.dma_start(UQ[:, :].rearrange("p (k n) -> p k n", k=2), rows_of(a["w_uq"][0])).then_inc(up_in, 16)
                    sp.dma_start(UKV[:, :], a["w_ukv"][0]).then_inc(up_in, 16)
            load_strips(U_GATE, 2 * KC, lambda m: w_in[:, :, bass.ds(m * P + (i3 + 3 * CW), P)])
            load_strips(U_BRANCH, KC, lambda m: w_branch[:, :, bass.ds(m * P, P)])
            load_strips(U_OUT, KC, lambda m: w_out[:, :, bass.ds(m * P, P)])
            sp.wait_ge(mlo_ready, KC)
            sp.dma_start(CTOK[:, :].rearrange("p (t d) -> p t d", t=2),
                         a["ctx_2"][0].rearrange("(t p) d -> p t d", p=P)).then_inc(ctx_in, 16)
            load_ffn(U_FFN1, 1, T_ADA, w13[1], w2[1], ada2)
            load_strips(U_CTX, 8, lambda m: w_in2[:, :, bass.ds(m * P + 10 * P, P)])
            for s, col in enumerate(IN2_COLS):
                load_strip(U_IN2 + s, (U_IN2 + s) % RING, w_in2[:, :, col:col + P])
                if s == 8:
                    sp.wait_ge(strip_done, U_IN2 + 1 + RING)
                    for dst, i in ((TCOS, 0), (TSIN, 1)):
                        sp.dma_start(dst[:, :].rearrange("p (t s) -> p t s", t=TT),
                                     a["dft_tok"][i].rearrange("(t p) s -> p t s", p=P)).then_inc(table_in, 16)
                    sp.dma_start(DFEAT[:, :], a["dft_feat"]).then_inc(table_in, 16)
                    sp.dma_start(MASK[:, :], a["near"].rearrange("p v k -> p (v k)")).then_inc(table_in, 16)
                    sp.dma_start(WF[:, :].rearrange("p (k n) -> p k n", k=2), rows_of(a["w_fourier_2"][0])).then_inc(table_in, 16)
                    sp.dma_start(PW[:, :].rearrange("p (k n) -> p k n", k=2), rows_of(a["conv_pw_w_2"][0])).then_inc(table_in, 16)
            load_strips(U_OUT2, RING, lambda m: w_out2[:, :, bass.ds(m * P, P)])
            sp.wait_ge(strip_done, U_OUT2 + RING)
            sp.wait_ge(rpb_in, 16 * 3)
            for r in range(ROWS):
                src = bass.AP(rpb.tensor, r * RPB_C, [[1, QC], [RPB_R * RPB_C, H], [1, SPAN_IN]])
                sp.dma_start(RPB[r * QC:(r + 1) * QC, 0:H * SPAN_IN].rearrange("p (h c) -> p h c", h=H), src).then_inc(table_in, 16)
            load_strips(U_OUT2 + RING, RING, lambda m: w_out2[:, :, bass.ds((m + RING) * P, P)])
            for part in range(MLP_PARTS):
                u = U_MLP + 2 * KC * part
                load_strips(u, KC, lambda m: w_mlp1[:, :, bass.ds(m * P + part * D, P)])
                load_strips(u + KC, KC, lambda m: w_mlp2[:, part * KC:(part + 1) * KC, bass.ds(m * P, P)])
            for t in range(TT):
                sp.wait_ge(ytok_act, t + 1)
                sp.wait_ge(ytok_dve, t + 1)
                sp.dma_start(out[0, t * P:(t + 1) * P, :], YTOK[:, t * D:(t + 1) * D]).then_inc(out_done, 16)
            sp.wait_ge(out_done, 16 * TT)

        @block.gpsimd
        def _(pool):
            pool.memset(IDENT[:, :], 0.0).then_inc(pool_seq, 1)
            pool.memset(ONES[:, :], 1.0).then_inc(const_ready, 1)
            pool.memset(CONST[:, 0:1], EPS).then_inc(const_ready, 1)
            pool.memset(CONST[:, 1:2], LN_EPS).then_inc(const_ready, 1)
            pool.memset(RPB[:, H * SPAN_IN:], 0.0)
            pool.memset(SSUM[:, :], 0.0).then_inc(pool_seq, 1)
            pool.wait_ge(pool_seq, 1)
            pool.affine_select(out=IDENT[:, :], in_=IDENT[:, :], compare_op=ALU.not_equal, fill=1.0, base=0,
                               pattern=[[-1, P]], channel_multiplier=1).then_inc(ident_ready, 1)
            pool.wait_ge(ident_ready, 1)
            pool.tensor_tensor(SUM32[:, :], IDENT[:, 0:32], IDENT[:, 32:64], ALU.add).then_inc(pool_seq, 1)
            for i in (2, 3):
                pool.wait_ge(pool_seq, i + 1)
                pool.tensor_tensor(SUM32[:, :], SUM32[:, :], IDENT[:, 32 * i:32 * i + 32], ALU.add).then_inc(pool_seq, 1)
            pool.wait_ge(pool_seq, 5)
            pool.sem_inc(const_ready, 1)
            pool.memset(FLIP[:, :], 0.0).then_inc(pool_seq, 1)
            pool.wait_ge(pool_seq, 6)
            pool.affine_select(out=FLIP[:, :], in_=FLIP[:, :], compare_op=ALU.not_equal, fill=1.0, base=1 - P,
                               pattern=[[1, P]], channel_multiplier=1).then_inc(flip_ready, 1)
            sq, seq = Tally(sq_ready), Tally(pool_seq)
            seq.n = 6

            def sum_squares(clear):
                if clear:
                    pool.wait_ge(stat_ready, clear)
                    pool.memset(SSUM[:, :], 0.0).then_inc(pool_seq, 1)
                    seq.add()
                pool.wait_ge(pool_seq, seq.n)
                for k in range(KC - 1):
                    pool.wait_ge(sq_ready, sq.add())
                    pool.tensor_tensor(SSUM[:, :], SSUM[:, :], SQ[:, k % 2 * S:(k % 2 + 1) * S], ALU.add).then_inc(pool_seq, 1)
                    pool.wait_ge(pool_seq, seq.add())
                    pool.sem_inc(sq_used, 1)
                sq.add()

            sum_squares(0)
            for norms in range(1, 4):
                sum_squares(norms)
            pool.wait_ge(stat_ready, 4)
            pool.memset(QZ[:, :], 0.0).then_inc(zeros_ready, 1)
            for norms in range(4, 6):
                sum_squares(norms)
        @block.tensor
        def _(pe):
            def wait_strip(u):
                pe.wait_ge(lo_ready, u + (1 + RING))
                pe.wait_ge(bank_free, u + 1)

            def products(dst, slot, blocks, hi, lo, n, cols=P, first=True, last=True):
                for i, (b, k) in enumerate(blocks):
                    w_hi = W_HI[:, slot * STRIP + b * cols:slot * STRIP + (b + 1) * cols]
                    w_lo = W_LO[:, slot * STRIP + b * cols:slot * STRIP + (b + 1) * cols]
                    x_hi, x_lo = hi[:, k * n:(k + 1) * n], lo[:, k * n:(k + 1) * n]
                    pe.matmul(dst, w_hi, x_hi, start=first and i == 0, stop=False)
                    pe.matmul(dst, w_hi, x_lo, start=False, stop=False)
                    mm = pe.matmul(dst, w_lo, x_hi, start=False, stop=last and i == len(blocks) - 1)
                return mm

            def strip(u, slot, hi, lo, chunks=KC, n=S, cols=P, each=None):
                wait_strip(u)
                for k in range(chunks):
                    if each is not None:
                        pe.wait_ge(each[0], each[1] + k + 1)
                    mm = products(bank[slot][0:cols, 0:n], slot, [(k, k)], hi, lo, n, cols,
                                  first=k == 0, last=k == chunks - 1)
                mm.then_inc(strip_done, 1)

            def strips(u0, count, hi, lo, chunks=KC, n=S, each=None):
                with loop(pe, count // RING) as it:
                    for j in range(RING):
                        strip(it * RING + (u0 + j), (u0 + j) % RING, hi, lo, chunks, n, each=each if j == 0 else None)

            def first_strips(u0, hi, lo, each):
                for j in range(LEAD):
                    wait_strip(u0 + j)
                slots = [(u0 + j) % RING for j in range(LEAD)]
                for k in range(KC):
                    at = [slice(s * STRIP + k * P, s * STRIP + (k + 1) * P) for s in slots]
                    pe.wait_ge(each[0], each[1] + k + 1)
                    for s, cut in zip(slots, at):
                        pe.matmul(bank[s][:, :], W_HI[:, cut], chunk(hi, k), start=k == 0, stop=False)
                        pe.matmul(bank[s][:, :], W_LO[:, cut], chunk(hi, k), start=False, stop=False)
                    pe.wait_ge(each[2], each[3] + k + 1)
                    for s, cut in zip(slots, at):
                        mm = pe.matmul(bank[s][:, :], W_HI[:, cut], chunk(lo, k), start=False, stop=k == KC - 1)
                        if k == KC - 1:
                            mm.then_inc(strip_done, 1)

            def new_strips(u0, count, hi, lo, each):
                first_strips(u0, hi, lo, each)
                strip(u0 + LEAD, (u0 + LEAD) % RING, hi, lo)
                strips(u0 + RING, count - RING, hi, lo)

            sq, sq_last, diag = Tally(sq_used), Tally(sq_ready), Tally(diag_ready)
            h, nhi, alo = Tally(h_ready), Tally(nhi_ready), Tally(alo_ready)
            h.n = alo.n = 2
            pe.sem_inc(strip_done, RING)

            def keep_warm(count, b=7):
                for _ in range(count):
                    pe.matmul(bank[b][:, 0:P], IDENT[:, :], ONES[:, :], start=True, stop=True)

            def stat(b=4, warm=4):
                pe.wait_ge(sq_used, sq.add(KC - 1))
                for t in range(TT):
                    pe.matmul(bank[b][:, t:t + 1], SSUM[:, t * P:(t + 1) * P], ONES[:, 0:1], start=t == 0, stop=False)
                keep_warm(warm)
                pe.wait_ge(sq_ready, sq_last.add(KC))
                for t in range(TT):
                    mm = pe.matmul(bank[b][:, t:t + 1], SQ[:, S + t * P:S + (t + 1) * P], ONES[:, 0:1], start=False, stop=t == TT - 1)
                mm.then_inc(stat_ready, 1)

            def spread(warm=4):
                keep_warm(warm)
                for t in range(TT):
                    pe.wait_ge(diag_ready, diag.add())
                    mm = pe.matmul(bank[4][:, t * P:(t + 1) * P], ONES[:, :], DIAG[:, t * P:(t + 1) * P], start=True, stop=True)
                mm.then_inc(rinv_ready, 1)
                keep_warm(2 * warm)

            def fold(c0, c1, tiles):
                pe.wait_ge(gem_done, tiles)
                for r in range(4):
                    mm = pe.matmul(bank[5][32 * r:32 * r + 32, c0:c1], SUM32[:, :],
                                   FOLDED[:, 4 * c0 + r:4 * c1:4], start=True, stop=True)
                mm.then_inc(mod_summed, 1)

            def normed():
                return nhi_ready, nhi.add(KC) - KC, h_ready, h.add(KC) - KC

            def widened(chunks):
                return alo_ready, alo.add(chunks) - chunks

            def ffn(u, after_up, after_down):
                for i, (_, chunks) in enumerate(FFN_PARTS):
                    if i == 0:
                        new_strips(u, 2 * chunks, H_HI, H_LO, normed())
                    else:
                        strips(u, 2 * chunks, H_HI, H_LO)
                    u += 2 * chunks
                    after_up[i]()
                    strips(u, KC, A_HI, A_LO, chunks, each=widened(chunks))
                    u += KC
                    after_down[i]()

            def attend(n0, scores, keys, prob, pt, values, meanwhile):
                for n in range(TT * H + 5):
                    if n < TT * H:
                        if n >= 4:
                            pe.wait_ge(exp_done, n0 + n - 3)
                        scores(n, bank[n % 4]).then_inc(score_done, 1)
                    meanwhile(n)
                    if 0 <= n - 3 < TT * H:
                        m = n - 3
                        pe.wait_ge(prob_ready, n0 + m + 1)
                        if m >= 2:
                            pe.wait_ge(pt_ready, n0 + m - 1)
                        for k in range(keys(m)):
                            mm = pe.transpose(bank[4 + m % 2][:, k * P:(k + 1) * P],
                                              prob[:, m % 4 * S + k * P:m % 4 * S + (k + 1) * P], IDENT[:, :])
                        mm.then_inc(prob_turned, 1)
                    if n >= 5:
                        m = n - 5
                        h, i = m // TT, m % TT
                        pe.wait_ge(pt_ready, n0 + m + 1)
                        if h >= 4 and h % 2 == 0 and i == 0:
                            pe.wait_ge(olo_ready, (n0 // TT + h) // 2 - 1)
                        for k in range(keys(m)):
                            mm = pe.matmul(bank[6 + h // 2 % 2][DV * (h % 2):DV * (h % 2) + DV, i * P:(i + 1) * P],
                                           values(m, k), pt[:, m % 3 * S + k * P:m % 3 * S + (k + 1) * P],
                                           start=k == 0, stop=k == keys(m) - 1)
                        mm.then_inc(pv_done, 1)
                pe.wait_ge(exp_done, n0 + TT * H)
                keep_warm(8, 0)
                pe.wait_ge(olo_ready, (n0 // TT + H) // 2)

            def mixer1():
                stat()
                spread()
                first_strips(U_LATENT, H_HI, H_LO, normed())
                strip(U_LATENT + 3, (U_LATENT + 3) % RING, H_HI, H_LO, cols=DR)
                strips(U_CONV, 4, H_HI, H_LO)
                pe.wait_ge(lat_sq, 3)
                pe.matmul(bank[4][:, :], ONES[:, :], SQ[:, 0:S], start=True, stop=False)
                pe.matmul(bank[4][:, :], ONES[:, :], SQ[:, S:2 * S], start=False, stop=True)
                pe.matmul(bank[5][:, :], ONES[:, :], UN[:, 0:S], start=True, stop=True).then_inc(lat_sum, 1)
                pe.wait_ge(bank_free, U_CONV + RING)
                for t in range(TT):
                    mm = pe.transpose(bank[6][:, t * DR:(t + 1) * DR], KRF[:, t * P:(t + 1) * P], IDENT[0:DR, 0:DR])
                mm.then_inc(kr_turned, 1)
                strips(U_CONV + 4, 8, H_HI, H_LO)
                pe.wait_ge(up_in, 32)
                pe.wait_ge(lat_ready, 1)
                half = H * DQ // 2
                for n in range(3 * TT):
                    b = bank[4 + n % 4]
                    if n >= 4:
                        pe.wait_ge(up_read, n - 3)
                    if n < 2 * TT:
                        t, c = n // 2, n % 2 * half
                        for k in range(2):
                            mm = pe.matmul(b[:, 0:half], CQT[:, k * S + t * P:k * S + (t + 1) * P],
                                           UQ[:, k * H * DQ + c:k * H * DQ + c + half], start=k == 0, stop=k == 1)
                    else:
                        t = n - 2 * TT
                        mm = pe.matmul(b[:, :], CKVT[:, t * P:(t + 1) * P],
                                       UKV[:, :].rearrange("p (h d) -> p h d", h=H)[:, :, 0:DN], start=True, stop=True)
                    mm.then_inc(up_done, 1)
                strips(U_GATE, 2 * KC, H_HI, H_LO)
                pe.wait_ge(k_ready, TT)
                for n in range(2 * H):
                    if n >= 4:
                        pe.wait_ge((turn_act, turn_dve)[n % 2], n // 2 - 1)
                    for t in range(TT):
                        at = (t * H + n // 2) * DQ
                        mm = pe.transpose(bank[4 + n % 4][0:DQ, t * P:(t + 1) * P], (QTOK, KTOK)[n % 2][:, at:at + DQ], IDENT[:, :])
                    mm.then_inc(turned, 1)
                pe.wait_ge(turn_act, H)
                pe.wait_ge(turn_dve, H)
                pe.wait_ge(bank_free, U_BRANCH + RING)
                def scores(n, dst):
                    h, i = n // TT, n % TT
                    pe.matmul(dst[:, 0:(i + 1) * P], QT[:, h * S + i * P:h * S + (i + 1) * P], KT[:, h * S:h * S + (i + 1) * P],
                              start=True, stop=False)
                    return pe.matmul(dst[:, i * P:(i + 1) * P], IDENT[:, :], CAUSAL[:, :], start=False, stop=True)

                def make_values(step):
                    if step != 3:
                        return
                    for n in range(2 * H, 2 * H + TT):
                        t = n - 2 * H
                        pe.wait_ge((turn_act, turn_dve)[n % 2], n // 2 - 1)
                        pe.matmul(bank[4 + n % 4][:, :], CKVT[:, t * P:(t + 1) * P],
                                  UKV[:, :].rearrange("p (h d) -> p h d", h=H)[:, :, DN:], start=True, stop=True).then_inc(turned, 1)
                    pe.wait_ge(turn_act, H + TT // 2)
                    pe.wait_ge(turn_dve, H + TT // 2)

                attend(0, scores, lambda n: n % TT + 1, PROB, PT,
                       lambda n, k: V[:, (k * H + n // TT) * DV:(k * H + n // TT + 1) * DV], make_values)
                with loop(pe, KC // RING) as it:
                    for j in range(RING):
                        u = it * RING + (U_BRANCH + j)
                        slot = (U_BRANCH + j) % RING
                        wait_strip(u)
                        products(bank[slot][:, :], slot, [(k, k) for k in range(4)], A_HI, A_LO, S)
                        products(bank[4 + slot][:, :], slot, [(k, k) for k in range(4, KC)], A_HI, A_LO, S).then_inc(strip_done, 1)
                new_strips(U_OUT, KC, H_HI, H_LO, (mhi_ready, 0, mlo_ready, 0))

            def context():
                fold(M_CTX, M_COLS, T_2)
                pe.wait_ge(ctx_ready, 2)
                for i, b in enumerate((4, 6, 7, 5)):
                    if b == 5:
                        pe.wait_ge(ctx_mod, 1)
                    for k in (2 * i, 2 * i + 1):
                        for t in range(2):
                            mm = pe.transpose(bank[b][:, k % 2 * CTX + t * P:k % 2 * CTX + (t + 1) * P],
                                              CTOK[:, t * D + k * P:t * D + (k + 1) * P], IDENT[:, :])
                    mm.then_inc(ctx_turned, 1)

            def mixer2():
                pe.wait_ge(clo_ready, KC)
                strips(U_CTX, 4, C_HI, C_LO, n=CTX)
                stat()
                strip(U_CTX + 4, U_CTX % RING, C_HI, C_LO, n=CTX)
                spread()
                for j in range(1, 4):
                    strip(U_CTX + 4 + j, (U_CTX + j) % RING, C_HI, C_LO, n=CTX)

                def turn_values(c):
                    for n in (2 * c, 2 * c + 1):
                        if n >= 4:
                            pe.wait_ge((vw_act, vw_dve)[n % 2], n // 2 - 1)
                        for i in range(4):
                            tile = n % 2 * 4 + i
                            mm = pe.transpose(bank[4 + n % 4][:, i * P:(i + 1) * P],
                                              VT[:, (c % 2 * 8 + tile) * P:(c % 2 * 8 + tile + 1) * P], IDENT[:, :])
                        mm.then_inc(vw_turned, 1)

                each = normed()[2:]
                for s in range(len(IN2_COLS)):
                    strip(U_IN2 + s, (U_IN2 + s) % RING, H_HI, H_LO, each=each if s == 0 else None)
                    if s >= 15:
                        pe.wait_ge(bank_free, U_IN2 + s + RING)
                        turn_values(s - 15)
                pe.wait_ge(table_in, 16 * 6)
                pe.wait_ge(bank_free, U_OUT2 + RING)
                for t in range(TT):
                    for c in range(2):
                        mm = pe.matmul(bank[t][:, c * 2 * P:(c + 1) * 2 * P], UT[:, c * S + t * P:c * S + (t + 1) * P],
                                       DFEAT[:, :], start=True, stop=True)
                    mm.then_inc(uc_done, 1)
                turn_values(3)
                for t in range(2):
                    pe.wait_ge((vw_act, vw_dve)[t], 3)
                    for c in range(4):
                        mm = pe.transpose(bank[4 + t][:, c * P:(c + 1) * P], VTC[:, c * CTX + t * P:c * CTX + (t + 1) * P],
                                          IDENT[:, :])
                    mm.then_inc(vw_turned, 1)
                pe.wait_ge(vw_act, 5)
                pe.wait_ge(vw_dve, 5)
                pe.wait_ge(conv_ready, 2)
                for c in range(2):
                    mm = pe.matmul(bank[4][:, :], ONES[:, :], chunk(ACC, c), start=c == 0, stop=c == 1)
                mm.then_inc(ln_sum, 1)
                pe.wait_ge(uc_act, 2)
                pe.wait_ge(uc_dve, 2)

                def over_tokens(c, tiles=range(TT)):
                    for t in tiles:
                        for i, table in enumerate((TCOS, TSIN)):
                            at = t * S + (2 * c + i) * P
                            mm = pe.matmul(bank[c][:, :], UC[:, at:at + P], chunk(table, t), start=t + i == 0, stop=t + i == TT)
                    if tiles[-1] == TT - 1:
                        mm.then_inc(ft_done, 1)

                def turn_biases(heads):
                    for h in heads:
                        if h >= 3:
                            pe.wait_ge(bias_ready, h - 2)
                        pe.matmul(bank[BIAS_BANKS[h % 3]][:, 0:SPAN], FLIP[:, :], RPB[:, h * SPAN_IN:h * SPAN_IN + SPAN],
                                  start=True, stop=True).then_inc(rpb_turned, 1)

                pe.wait_ge(flip_ready, 1)
                pe.wait_ge(table_in, 16 * (6 + ROWS))
                turn_biases(range(3))
                over_tokens(0, range(TT // 2))
                pe.wait_ge(ln_sq, 2)
                for c in range(2):
                    mm = pe.matmul(bank[4][:, :], ONES[:, :], chunk(CSQ, c), start=c == 0, stop=c == 1)
                mm.then_inc(ln_sum, 1)
                turn_biases(range(3, 6))
                over_tokens(0, range(TT // 2, TT))
                turn_biases(range(6, H))
                over_tokens(1)
                pe.wait_ge(ft_act, 1)

                def make_outputs(step):
                    if step == 3:
                        pe.wait_ge(act_ready, 2)
                        for i, (w, x) in enumerate(((PW, ACC), (WF, FT))):
                            for m in range(2):
                                for c in range(2):
                                    mm = pe.matmul(bank[4 + 2 * i + m][:, :], w[:, (2 * c + m) * P:(2 * c + m + 1) * P], chunk(x, c),
                                                   start=c == 0, stop=c == 1)
                                mm.then_inc(mix_done, 1)
                        pe.wait_ge(mixed, 6)
                    if step == 5:
                        pe.wait_ge(mixed, 8)

                def scores(n, dst):
                    h, j = n // TT, n % TT
                    c = h // 2
                    if n == 1:
                        pe.wait_ge(ft_dve, 1)
                    if n == 2:
                        pe.wait_ge(bias_ready, H)
                    q = QZ[:, h * S + j * P:h * S + (j + 1) * P]
                    near = KT2[:, c * KEYS:c * KEYS + S].rearrange("p (r c) -> p r c", r=ROWS)[:, :, NEAR[j]:NEAR[j] + KW]
                    pe.matmul(dst[:, 0:CTX], q, near, start=True, stop=True)
                    return pe.matmul(dst[:, CTX:], q, KT2[:, c * KEYS + S:(c + 1) * KEYS], start=True, stop=True)

                def values(n, k):
                    h, j = n // TT, n % TT
                    if k < 2:
                        return VW[:, ((2 * j + k) * H + h) * DH:((2 * j + k) * H + h + 1) * DH]
                    return VC[:, ((k - 2) * H + h) * DH:((k - 2) * H + h + 1) * DH]

                attend(TT * H, scores, lambda n: 4, PROB2, PT2, values, make_outputs)
                strips(U_OUT2, KC, A_HI, A_LO)

            def mlp():
                stat()
                spread()
                for part in range(MLP_PARTS):
                    u = U_MLP + 2 * KC * part
                    if part == 0:
                        new_strips(u, KC, H_HI, H_LO, normed())
                    else:
                        strips(u, KC, H_HI, H_LO)
                    if part < MLP_PARTS - 1:
                        strips(u + KC, KC, A_HI, A_LO, each=widened(KC))
                        continue
                    strips(u + KC, RING, A_HI, A_LO, each=widened(KC))
                    for j in range(RING, KC):
                        strip(u + KC + j, (u + j) % RING, A_HI, A_LO)
                        if j == 5:
                            turn_back(0)

            def turn_back(half):
                for t in range(TT):
                    if t == TT - 1 and half:
                        pe.wait_ge(std_ready, 6)
                    for k in range(4 * half, 4 * half + 4):
                        if t == 0:
                            pe.wait_ge(y_ready, k + 1)
                        mm = pe.transpose(bank[4 - 4 * half + t][:, k % 4 * P:(k % 4 + 1) * P],
                                          YT[:, k * S + t * P:k * S + (t + 1) * P], IDENT[:, :])
                    mm.then_inc(y_turned, 1)

            def nothing():
                pass

            def modulate(i):
                pe.wait_ge(pe_gem_in[i], 16)
                for k in range(KC):
                    mm = pe.matmul(bank[(6, 7, 5)[i]][0:1, 0:GEM], CSIL[:, C_1 + k:C_1 + k + 1],
                                   PBUF[:, (i * KC + k) * GEM:(i * KC + k + 1) * GEM], start=k == 0, stop=k == KC - 1)
                mm.then_inc(pe_gem_done, 1)

            pe.wait_ge(ident_ready, 1)
            pe.wait_ge(cond_ready, 1)
            modulate(0)
            pe.wait_ge(x_in, 16 * TT)
            for k in range(KC):
                if k >= RING:
                    pe.wait_ge(x_ready, k - RING + 1)
                for t in range(TT):
                    mm = pe.transpose(bank[k % RING][:, t * P:(t + 1) * P], XTOK[:, t * D + k * P:t * D + (k + 1) * P],
                                      IDENT[:, :])
                mm.then_inc(x_turned, 1)
            modulate(1)
            pe.wait_ge(const_ready, 4)
            stat(warm=0)
            pe.wait_ge(x_ready, KC)
            pe.wait_ge(rows_in, 16 * 14)
            for b, rows, dst in ((0, ROWS1, V_ROWS), (1, ROWS2, M_CTX), (2, ROWS3, 2 * CK2)):
                pe.transpose(bank[b][:, 0:dst], rows[:, :], IDENT[0:dst, 0:dst]).then_inc(cols_turned, 1)
            modulate(2)
            spread(warm=0)
            pe.wait_ge(grow_ready, 3)
            for c in range(3 * GEM // P):
                pe.matmul(bank[5][:, 10 + c:11 + c], GROW[0:1, c * P:(c + 1) * P], ONES[0:1, 0:1], start=True, stop=True)
            fold(0, 10, 5)
            keep_warm(8)
            ffn(U_FFN0, [lambda: fold(16, 24, 12),
                         nothing, lambda: fold(24, 64, 32)], [nothing] * 3)
            mixer1()
            stat()
            spread()
            ffn(U_FFN1, [lambda: fold(64, M_2, T_ADA),
                         nothing, lambda: fold(M_2, M_CTX, T_2)], [nothing, context, nothing])
            mixer2()
            mlp()
            stat(TT - 1, warm=0)
            turn_back(1)

        @block.scalar
        def _(act):
            def split_hi(u, slot, turn):
                act.wait_ge(raw_in[slot], turn * 16 + 16)
                act.wait_ge(strip_done, u + 1)
                act.activation(strip_of(W_HI, slot), strip_of(RAW, slot), ACT.Copy).then_inc(hi_ready, 1)

            def split_next(u0, it, j):
                u = u0 + j + LEAD
                if not isinstance(it, int) or it * RING + u < STRIPS:
                    split_hi(it * RING + u, u % RING, it + u // RING)

            silu, ahi, un = Tally(silu_ready), Tally(ahi_ready), Tally(un_ready)
            std, nhi, hsum = Tally(stat_ready), Tally(nhi_ready), Tally(head_sum)

            def square(k, j):
                act.activation(SQ[:, j * S:(j + 1) * S], chunk(X, k), ACT.Square).then_inc(sq_ready, 1)

            def token_rms(b=4):
                act.wait_ge(stat_ready, std.add())
                act.activation(RMS[:, 0:TT], bank[b][:, 0:TT], ACT.Sqrt, bias=CONST[:, 0:1], scale=1.0 / D).then_inc(std_ready, 1)

            def norm(shift, between=None):

                for k in range(KC):
                    act.wait_ge(un_ready, un.add())
                    act.activation(chunk(H_HI, k), chunk(NRM, k % 4), ACT.Identity,
                                   bias=MOD[:, shift + k:shift + k + 1]).then_inc(nhi_ready, 1)
                    if between is not None and k % 2:
                        between(k // 2)

            def ffn_up(u0, chunks):
                with loop(act, chunks // 2) as it:
                    for p in range(2):
                        split_next(u0, it, 2 * p)
                        split_next(u0, it, 2 * p + 1)
                        g = u0 + 2 * p
                        act.wait_ge(strip_done, it * RING + (g + 1 + RING))
                        act.activation(SG[:, p * S:(p + 1) * S], bank[g % RING][:, :], ACT.Silu).then_inc(silu_ready, 1)
                        act.wait_ge(bank_free, it * RING + (g + 2 + RING))
                        act.activation(chunk(A_HI, it * 2 + p), HF[:, p * S:(p + 1) * S], ACT.Copy).then_inc(ahi_ready, 1)

            def down(u0, squares):
                if squares:
                    for k in range(KC + 1):
                        if k < KC:
                            split_next(u0, 0, k)
                        if k:
                            act.wait_ge(bank_free, u0 + k + RING)
                            act.wait_ge(sq_used, squares + k - 2)
                            square(k - 1, (k - 1) % 2)
                    return
                with loop(act, KC // RING) as it:
                    for j in range(RING):
                        split_next(u0, it, j)

            def attend(n0, keys, prob, pt, output, meanwhile):
                for n in range(TT * H + 6):
                    if n < TT * H:
                        act.wait_ge(neg_ready, n0 + n + 1)
                        if n >= 4:
                            act.wait_ge(prob_turned, n0 + n - 3)
                        act.activation(prob[:, n % 4 * S:n % 4 * S + keys(n)], bank[n % 4][:, 0:keys(n)], ACT.Exp,
                                       bias=soft(n, 0), accum_out=soft(n, 1)).then_inc(exp_done, 1)
                    if n == 3:
                        meanwhile()
                    if 0 <= n - 3 < TT * H:
                        m = n - 3
                        act.wait_ge(prob_turned, n0 + m + 1)
                        if m >= 3:
                            act.wait_ge(pv_done, n0 + m - 2)
                        act.activation(pt[:, m % 3 * S:m % 3 * S + keys(m)], bank[4 + m % 2][:, 0:keys(m)],
                                       ACT.Copy).then_inc(pt_ready, 1)
                    if n >= 6 and (n - 5) % (2 * TT) == 0:
                        c = (n - 5) // (2 * TT) - 1
                        act.wait_ge(pv_done, n0 + (c + 1) * 2 * TT)
                        output(c, bank[6 + c % 2][:, :]).then_inc(ohi_ready, 1)

            def mixer1():
                token_rms()
                norm(24)
                for j in range(4):
                    split_next(U_LATENT, 0, j)
                    if j < 3:
                        act.wait_ge(bank_free, U_LATENT + j + 1 + RING)
                        act.activation((SQ[:, 0:S], SQ[:, S:2 * S], UN[:, 0:S])[j],
                                       (CQT[:, 0:S], CQT[:, S:2 * S], CKVT[:, :])[j], ACT.Square).then_inc(lat_sq, 1)
                for j in range(4):
                    split_next(U_CONV, 0, j)
                act.wait_ge(lat_sum, 1)
                act.activation(UN[:, S:2 * S], bank[4][:, :], ACT.Sqrt, bias=CONST[:, 0:1], scale=1.0 / QR).then_inc(lat_std, 1)
                act.activation(RINV[:, :], bank[5][:, :], ACT.Sqrt, bias=CONST[:, 0:1], scale=1.0 / KR).then_inc(lat_std, 1)
                with loop(act, 2) as it:
                    for j in range(4):
                        split_next(U_CONV + 4, it, j)
                act.wait_ge(angle_ready, 1)
                act.activation(SIN[:, :], ANGLE[:, TT * DR // 2:TT * DR], ACT.Sin).then_inc(sin_ready, 1)
                act.activation(COS[:, :], ANGLE[:, TT * DR:], ACT.Sin).then_inc(sin_ready, 1)
                half = H * DQ // 2
                for n in range(3 * TT):
                    act.wait_ge(up_done, n + 1)
                    if n < 2 * TT:
                        act.activation(chunk(QTOK, n, half), bank[4 + n % 4][:, 0:half], ACT.Copy).then_inc(up_read, 1)
                    else:
                        act.activation(heads(chunk(KTOK, n - 2 * TT, H * DQ))[:, :, 0:DN],
                                       bank[4 + n % 4][:, :].rearrange("p (h d) -> p h d", h=H), ACT.Copy).then_inc(up_read, 1)
                act.wait_ge(bank_free, U_GATE + RING)
                act.wait_ge(mixed, 4)
                act.wait_ge(up_read, 3 * TT)
                with loop(act, TT, (hsum, 1)) as t:
                    act.activation(TQ0[:, :], chunk(QTOK, t, H * DQ), ACT.Square).then_inc(head_sq, 1)
                    act.activation(TQ1[:, 0:H * DN], heads(chunk(KTOK, t, H * DQ))[:, :, 0:DN], ACT.Square).then_inc(head_sq, 1)
                    act.activation(TQ1[:, H * DN:H * DN + DR], chunk(KRT, t, DR), ACT.Square).then_inc(head_sq, 1)
                    for j in range(RING):
                        split_next(U_GATE, t, j)
                        act.wait_ge(strip_done, t * RING + (U_GATE + j + 1 + RING))
                        act.activation(chunk(GATES, t * RING + j), bank[(U_GATE + j) % RING][:, :],
                                       ACT.Sigmoid).then_inc(bank_free, 1)
                        if j == 0:
                            act.wait_ge(head_sum, hsum.add())
                            act.activation(STAT[:, 0:2 * H], STAT[:, 0:2 * H], ACT.Sqrt, bias=CONST[:, 0:1],
                                           scale=1.0 / DN).then_inc(head_std, 1)
                            act.activation(STAT[:, 2 * H:3 * H + 1], STAT[:, 2 * H:3 * H + 1], ACT.Sqrt, bias=CONST[:, 0:1],
                                           scale=1.0 / DR).then_inc(head_std, 1)
                for n in range(0, 2 * H, 2):
                    act.wait_ge(turned, n + 1)
                    act.activation(chunk(QT, n // 2), bank[4 + n % 4][0:DQ, :], ACT.Copy).then_inc(turn_act, 1)

                def values():
                    for n in range(2 * H, 2 * H + TT, 2):
                        act.wait_ge(turned, n + 1)
                        act.activation(chunk(V, n - 2 * H), bank[4 + n % 4][:, :], ACT.Copy).then_inc(turn_act, 1)

                attend(0, lambda n: (n % TT + 1) * P, PROB, PT,
                       lambda c, src: act.activation(chunk(A_HI, c), src, ACT.Copy), values)
                with loop(act, KC // RING) as it:
                    for j in range(RING):
                        split_next(U_BRANCH, it, j)
                        act.wait_ge(merged, it * RING + (j + 1))
                        act.activation(chunk(H_HI, it * RING + j), UN[:, j % 2 * S:(j % 2 + 1) * S], ACT.Copy).then_inc(mhi_ready, 1)
                down(U_OUT, 2 * (KC - 1))

            def mixer2():
                act.wait_ge(gem_done, T_2)

                def context_strip(s):
                    split_next(U_CTX, 0, s)
                    act.wait_ge(strip_done, U_CTX + s + 1 + RING)
                    dst = KT2[:, s * KEYS + S:(s + 1) * KEYS] if s < 4 else chunk(VTC, s - 4, CTX)
                    act.activation(dst, bank[(U_CTX + s) % RING][:, 0:CTX], ACT.Copy).then_inc(bank_free, 1)

                act.wait_ge(bank_free, U_CTX + RING)
                for s in range(4):
                    context_strip(s)
                token_rms()
                norm(M_2, lambda i: context_strip(4 + i))

                def turned_values(n):
                    act.wait_ge(vw_turned, n + 1)
                    act.activation(window_values(n), window_bank(n), ACT.Copy).then_inc(vw_act, 1)

                for s in range(len(IN2_COLS)):
                    u = U_IN2 + s
                    split_next(U_IN2, 0, s)
                    src = bank[u % RING]
                    if s in (2, 4):
                        act.wait_ge(strip_done, u + 1 + RING)
                        p = s // 2 - 1
                        act.activation(SQ[:, p * S:(p + 1) * S], src[:, :], ACT.Sigmoid).then_inc(sig_ready, 1)
                    if s == 6:
                        act.wait_ge(bank_free, u + RING)
                        act.wait_ge(zeros_ready, 1)
                    if s >= 6:
                        act.wait_ge(strip_done, u + 1 + RING)
                        part, c = (s - 6) // 4, (s - 6) % 4
                        if part == 0:
                            for i in range(2):
                                rows = slice(DH * i, DH * i + DH)
                                ins = act.activation(
                                    by_tiles(chunk(QZ, 2 * c + i)[rows, :]), by_rows(src[rows, :]), ACT.Copy, scale=DH ** -0.5)
                        elif part == 1:
                            ins = act.activation(KT2[:, c * KEYS:c * KEYS + S], src[:, :], ACT.Copy)
                        else:
                            if c >= 2:
                                act.wait_ge(vw_turned, 2 * c - 2)
                            for j in range(TT):
                                ins = act.activation(
                                    chunk(VT, c % 2 * TT + j, ROWS * KW).rearrange("p (r c) -> p r c", r=ROWS),
                                    src[:, :].rearrange("p (r c) -> p r c", r=ROWS)[:, :, NEAR[j]:NEAR[j] + KW], ACT.Copy)
                        ins.then_inc(bank_free, 1)
                        if s >= 15:
                            turned_values(2 * (s - 15))
                for t in (0, 2):
                    act.wait_ge(uc_done, t + 1)
                    act.activation(chunk(UC, t), bank[t][:, :], ACT.Copy).then_inc(uc_act, 1)
                for n in (6, 8):
                    turned_values(n)
                for c in range(2):
                    act.wait_ge(dev_ready, c + 1)
                    act.activation(chunk(CSQ, c), chunk(ACC, c), ACT.Square).then_inc(ln_sq, 1)
                act.wait_ge(ln_sum, 2)
                act.activation(bank[4][:, :], bank[4][:, :], ACT.Sqrt, bias=CONST[:, 1:2], scale=1.0 / CW2).then_inc(ln_std, 1)
                act.wait_ge(ft_done, 1)
                act.activation(chunk(FT, 0), bank[0][:, :], ACT.Copy).then_inc(ft_act, 1)
                for c in range(2):
                    act.wait_ge(z_ready, c + 1)
                    act.activation(chunk(ACC, c), chunk(ACC, c), ACT.Silu, bias=COL1[:, V_LNB + c:V_LNB + c + 1],
                                   scale=COL1[:, V_LNG + c:V_LNG + c + 1]).then_inc(act_ready, 1)

                def outputs():
                    for i, m in enumerate((2, 3, 0, 1)):
                        act.wait_ge(mix_done, i + 1)
                        if m < 2:
                            ins = act.activation(chunk(A_HI, m), bank[4 + i][:, :], ACT.Copy)
                        else:
                            ins = act.activation(chunk(A_HI, m), bank[4 + i][:, :], ACT.Identity,
                                                 bias=COL1[:, V_PWB + m - 2:V_PWB + m - 1])
                        ins.then_inc(mix_hi, 1)

                attend(TT * H, lambda n: S, PROB2, PT2,
                       lambda c, src: act.activation(by_rows(chunk(A_HI, 4 + c)), by_tiles(src), ACT.Copy), outputs)
                down(U_OUT2, 4 * (KC - 1))

            def mlp():
                token_rms()
                norm(M_2 + 3 * KC)
                for part in range(MLP_PARTS):
                    u = U_MLP + 2 * KC * part
                    with loop(act, KC // RING) as it:
                        for j in range(RING):
                            split_next(u, it, j)
                            act.wait_ge(strip_done, it * RING + (u + j + 1 + RING))
                            act.activation(SG[:, j % 2 * S:(j % 2 + 1) * S], bank[(u + j) % RING][:, :],
                                           ACT.Relu).then_inc(silu_ready, 1)
                            act.wait_ge(bank_free, it * RING + (u + j + 1 + RING))
                            act.activation(chunk(A_HI, it * RING + j), HF[:, j % 2 * S:(j % 2 + 1) * S],
                                           ACT.Copy).then_inc(ahi_ready, 1)
                    down(u + KC, 5 * (KC - 1) if part == MLP_PARTS - 1 else 0)

            act.wait_ge(cond_in, 16 * 3)
            act.activation(CSIL[:, :], CRAW[:, :], ACT.Silu).then_inc(cond_ready, 1)
            for k in range(KC):
                act.wait_ge(x_turned, k + 1)
                act.activation(chunk(X, k), bank[k % RING][:, :], ACT.Copy).then_inc(x_ready, 1)
                act.wait_ge(x_ready, k + 1)
                if k >= 2:
                    act.wait_ge(sq_used, k - 1)
                square(k, k % 2)
            token_rms()
            for i, (dst, b) in enumerate(((COL1[:, 0:V_ROWS], 0), (COL2[:, :], 1), (COL3[:, :], 2))):
                act.wait_ge(cols_turned, i + 1)
                act.activation(dst, bank[b][:, 0:dst.shape[1]], ACT.Copy).then_inc(cols_ready, 1)
            act.sem_inc(bank_free, RING)
            for u in range(LEAD):
                act.wait_ge(raw_in[u], 16)
                act.activation(strip_of(W_HI, u), strip_of(RAW, u), ACT.Copy).then_inc(hi_ready, 1)
            for i in range(3):
                act.wait_ge(pe_gem_done, i + 1)
                act.activation(GROW[:, i * GEM:(i + 1) * GEM], bank[(6, 7, 5)[i]][0:1, 0:GEM], ACT.Copy).then_inc(grow_ready, 1)
            norm(0)
            u = U_FFN0
            for i, (_, chunks) in enumerate(FFN_PARTS):
                ffn_up(u, chunks)
                u += 2 * chunks
                down(u, KC - 1 if i == 2 else 0)
                u += KC
            mixer1()
            token_rms()
            norm(48)
            u = U_FFN1
            for i, (_, chunks) in enumerate(FFN_PARTS):
                ffn_up(u, chunks)
                u += 2 * chunks
                if i == 1:
                    act.wait_ge(ctx_in, 16)
                    for t in range(2):
                        act.activation(SQ[:, :], CTOK[:, t * D:(t + 1) * D], ACT.Square,
                                       accum_out=STAT[:, 200 + t:201 + t]).then_inc(ctx_sq, 1)
                        act.wait_ge(ctx_sq, t + 1)
                    act.activation(STAT[:, 200:202], STAT[:, 200:202], ACT.Sqrt, bias=CONST[:, 0:1],
                                   scale=1.0 / D).then_inc(ctx_std, 1)
                down(u, 3 * (KC - 1) if i == 2 else 0)
                u += KC
                if i == 1:
                    for k in range(KC):
                        act.wait_ge(ctx_full, k + 1)
                        act.activation(chunk(C_HI, k, CTX), chunk(HF, k % 4, CTX), ACT.Copy).then_inc(chi_ready, 1)
            mixer2()
            mlp()
            token_rms(TT - 1)
            act.wait_ge(y_scaled, 1)
            for t in range(TT):
                act.wait_ge(y_turned, t + 1)
                act.activation(YTOK[:, t * D:t * D + S], bank[4 + t][:, :], ACT.Copy,
                               scale=RMS[:, TT + t:TT + t + 1]).then_inc(ytok_act, 1)

        @block.vector
        def _(dve):
            seq = Tally(dve_seq)

            def after(ins):
                ins.then_inc(dve_seq, 1)
                dve.wait_ge(dve_seq, seq.add())

            def split_lo(u, slot):
                dve.wait_ge(hi_ready, u + 1)
                dve.tensor_tensor(strip_of(W_LO, slot), strip_of(RAW, slot), strip_of(W_HI, slot).bitcast(F32),
                                  ALU.subtract).then_inc(lo_ready, 1)

            def split_next(u0, it, j, per=RING):
                u = u0 + j + LEAD
                if not isinstance(it, int) or it * per + u < STRIPS:
                    split_lo(it * per + u, u % RING)

            silu, ahi, nhi, std = Tally(silu_ready), Tally(ahi_ready), Tally(nhi_ready), Tally(std_ready)
            hsq, hstd, rinv = Tally(head_sq), Tally(head_std), Tally(rinv_ready)
            gem_seq = KC + 2
            h_own, alo_own = Tally(h_ready), Tally(alo_ready)
            h_own.n = alo_own.n = 2
            gem_of = [Tally(gem_in[i]) for i in range(GEM_RING)]

            def gem_tile(slot, vec, at):
                g = GBUF[:, slot * KC * GEM:(slot + 1) * KC * GEM]
                acc = GACC[:, 0:GEM], GACC[:, GEM:]
                for k in range(KC):
                    if k < 2:
                        ins = dve.tensor_scalar(acc[k], g[:, k * GEM:(k + 1) * GEM], CSIL[:, vec + k:vec + k + 1], None, ALU.mult)
                    else:
                        dve.wait_ge(dve_seq, seq.add(0) - 1)
                        ins = dve.scalar_tensor_tensor(out=acc[k % 2], in0=g[:, k * GEM:(k + 1) * GEM],
                                                       scalar=CSIL[:, vec + k:vec + k + 1], in1=acc[k % 2],
                                                       op0=ALU.mult, op1=ALU.add)
                    ins.then_inc(dve_seq, 1)
                    seq.add()
                dve.wait_ge(dve_seq, seq.add(0))
                after(dve.tensor_tensor(acc[0], acc[0], acc[1], ALU.add))
                after(dve.transpose(GTURN[:, :], acc[0]))
                return dve.tensor_reduce(FOLDED[:, bass.ds(at * FOLD, FOLD)],
                                         GTURN[:, :].rearrange("p (b i) -> p b i", i=32), AX.X, ALU.add)

            def gem_step(slot, seq_no, vec, at, also=None):
                dve.wait_ge(gem_in[slot], gem_of[slot].add(16))
                if not isinstance(seq_no, int) or seq_no:
                    dve.wait_ge(gem_done, seq_no)
                if also is not None:
                    after(gem_tile(slot, also, at + (T_2 - T_ADA)))
                gem_tile(slot, vec, at).then_inc(gem_done, 1)

            summed = [0]

            def mod_columns(c0, c1, bias):
                summed[0] += 1
                dve.wait_ge(mod_summed, summed[0])
                after(dve.tensor_tensor(MOD[:, c0:c1], bank[5][:, c0:c1], COL2[:, bias:bias + c1 - c0], ALU.add))

            def factors(dst, scale, weight):
                return dve.scalar_tensor_tensor(out=AMOD[:, dst:dst + KC], in0=MOD[:, scale:scale + KC], scalar=1.0,
                                                in1=COL1[:, weight:weight + KC], op0=ALU.add, op1=ALU.mult)

            def half_gate(i):
                return dve.tensor_scalar(GHALF[:, i * KC:(i + 1) * KC], MOD[:, i * 24 + 16:i * 24 + 24], 0.5, None, ALU.mult)

            def token_factors():
                dve.wait_ge(std_ready, std.add())
                after(dve.reciprocal(RMS[:, TT:], RMS[:, 0:TT]))
                for t in range(TT):
                    dve.tensor_scalar(DIAG[:, t * P:(t + 1) * P], IDENT[:, :], RMS[:, TT + t:TT + t + 1], None,
                                      ALU.mult).then_inc(diag_ready, 1)

            def norm(factor, shift, between=None):
                dve.wait_ge(rinv_ready, rinv.add())
                start = h_own.n

                def normed(k):
                    if k >= 4:
                        dve.wait_ge(h_ready, start + k - 3)
                    dve.scalar_tensor_tensor(out=chunk(NRM, k % 4), in0=chunk(X, k), scalar=AMOD[:, factor + k:factor + k + 1],
                                             in1=bank[4][:, :], op0=ALU.mult, op1=ALU.mult).then_inc(un_ready, 1)

                normed(0)
                normed(1)
                for k in range(KC):
                    dve.wait_ge(nhi_ready, nhi.add())
                    dve.scalar_tensor_tensor(out=chunk(H_LO, k), in0=chunk(NRM, k % 4), scalar=MOD[:, shift + k:shift + k + 1],
                                             in1=chunk(H_HI, k).bitcast(F32), op0=ALU.add, op1=ALU.subtract).then_inc(h_ready, 1)
                    h_own.add()
                    if k + 2 < KC:
                        normed(k + 2)
                    if between is not None and k % 2:
                        between(k // 2)

            def ffn_up(u0, chunks, ups, seq_no, vec, tile, also):
                gem, per = [], up_turn(ups, chunks)
                if ups:
                    gem = [(t, 16) for t in gem_of] + [(seq, 4 * gem_seq + (2 * (gem_seq + 1) if also is not None else 0))]
                with loop(dve, chunks // per, (silu, per), (ahi, per), (alo_own, per), *gem) as it:
                    for c in range(per):
                        p, g = c % 2, u0 + 2 * c
                        split_next(u0, it, 2 * c, 2 * per)
                        dve.wait_ge(alo_ready, alo_own.add(0) - 1)
                        alo_own.add()
                        dve.wait_ge(silu_ready, silu.add())
                        dve.wait_ge(strip_done, it * 2 * per + (g + 2 + RING))
                        dve.tensor_tensor(HF[:, p * S:(p + 1) * S], SG[:, p * S:(p + 1) * S], bank[(g + 1) % RING][:, :],
                                          ALU.mult).then_inc(bank_free, 2)
                        split_next(u0, it, 2 * c + 1, 2 * per)
                        dve.wait_ge(ahi_ready, ahi.add())
                        dve.tensor_tensor(chunk(A_LO, it * per + c), HF[:, p * S:(p + 1) * S],
                                          chunk(A_HI, it * per + c).bitcast(F32), ALU.subtract).then_inc(alo_ready, 1)
                        if ups and c < GEM_RING:
                            gem_step(c, it * GEM_RING + (seq_no + c), vec, tile(it, c), also if c % 2 else None)

            def down(u0, gate, gate0, seq_no=0, vec=None, tile=None, gem_at=()):
                def turn(it, strips):
                    for j in strips:
                        split_next(u0, it, j)
                        dve.wait_ge(strip_done, it * RING + (u0 + j + 1 + RING))
                        dve.scalar_tensor_tensor(out=chunk(X, it * RING + j), in0=bank[(u0 + j) % RING][:, :],
                                                 scalar=gate[:, bass.ds(it * RING + (gate0 + j), 1)],
                                                 in1=chunk(X, it * RING + j), op0=ALU.mult, op1=ALU.add).then_inc(bank_free, 1)
                        if u0 + KC == STRIPS:
                            dve.wait_ge(bank_free, u0 + j + 1 + RING)
                            dve.tensor_scalar(chunk(YT, j), chunk(X, j), COL1[:, V_FIN + j:V_FIN + j + 1], None,
                                              ALU.mult).then_inc(y_ready, 1)
                        if j in gem_at:
                            g = gem_at.index(j)
                            gem_step(g, seq_no + g, vec, tile(0, g))

                if gem_at or u0 + KC == STRIPS:
                    turn(0, range(KC))
                else:
                    with loop(dve, KC // RING) as it:
                        turn(it, range(RING))

            def ffn(u, f, seq_no, vec, gate0, also, after_up, after_down):
                for part, (_, chunks) in enumerate(FFN_PARTS):
                    ups, tile_up, downs, tile_down = GEM_PLAN[f][part]
                    ffn_up(u, chunks, ups, seq_no, vec, tile_up, also)
                    after_up[part]()
                    u, seq_no = u + 2 * chunks, seq_no + ups
                    down(u, GHALF, gate0, seq_no, vec, tile_down, GEM_AFTER if downs else ())
                    after_down[part]()
                    u, seq_no = u + KC, seq_no + downs

            def attend(n0, keys, masked, prob, output, meanwhile):
                for n in range(TT * H + 6):
                    if n < TT * H:
                        dve.wait_ge(score_done, n0 + n + 1)
                        if masked is not None:
                            after(masked(n, bank[n % 4]))
                        dve.tensor_reduce(soft(n, 0), bank[n % 4][:, 0:keys(n)], AX.X, ALU.max, negate=True).then_inc(neg_ready, 1)
                    if 0 <= n - 1 < TT * H:
                        m = n - 1
                        dve.wait_ge(exp_done, n0 + m + 1)
                        after(dve.reciprocal(soft(m, 2), soft(m, 1)))
                        p = prob[:, m % 4 * S:m % 4 * S + keys(m)]
                        dve.tensor_scalar(p, p, soft(m, 2), None, ALU.mult).then_inc(prob_ready, 1)
                    if n == 3:
                        meanwhile()
                    if n >= 6 and (n - 5) % (2 * TT) == 0:
                        c = (n - 5) // (2 * TT) - 1
                        dve.wait_ge(ohi_ready, n0 // (2 * TT) + c + 1)
                        output(c, bank[6 + c % 2][:, :]).then_inc(olo_ready, 1)

            def mixer1():
                token_factors()
                norm(A_1 + KC, 24)
                for j in range(4):
                    split_next(U_LATENT, 0, j)
                    dve.wait_ge(strip_done, U_LATENT + j + 1 + RING)
                    cols = DR if j == 3 else P
                    dve.tensor_copy((CQT[:, 0:S], CQT[:, S:2 * S], CKVT[:, :], KRF[:, :])[j],
                                    bank[(U_LATENT + j) % RING][0:cols, :]).then_inc(bank_free, 1)
                ub = [UB[:, j * UPAD:(j + 1) * UPAD] for j in range(4)]
                for j in range(4):
                    ins = dve.memset(ub[j][:, 0:CK - 1], 0.0)
                after(ins)
                for j in range(4):
                    split_next(U_CONV, 0, j)
                    dve.wait_ge(strip_done, U_CONV + j + 1 + RING)
                    dve.tensor_copy(chunk(XV, j), bank[(U_CONV + j) % RING][:, :]).then_inc(bank_free, 1)
                dve.wait_ge(lat_std, 2)
                after(dve.reciprocal(UN[:, S:2 * S], UN[:, S:2 * S]))
                after(dve.reciprocal(RINV[:, :], RINV[:, :]))
                for k in range(2):
                    after(dve.scalar_tensor_tensor(out=chunk(CQT, k), in0=chunk(CQT, k), scalar=COL1[:, V_QA + k:V_QA + k + 1],
                                                   in1=UN[:, S:2 * S], op0=ALU.mult, op1=ALU.mult))
                after(dve.scalar_tensor_tensor(out=CKVT[:, :], in0=CKVT[:, :], scalar=COL1[:, V_KVA:V_KVA + 1],
                                               in1=RINV[:, :], op0=ALU.mult, op1=ALU.mult))
                dve.wait_ge(kr_turned, 1)
                after(dve.tensor_copy(KRT[:, :], bank[6][:, 0:TT * DR]))
                dve.sem_inc(lat_ready, 1)
                for j in range(4):
                    split_next(U_CONV + 4, 0, j)
                    dve.wait_ge(strip_done, U_CONV + 4 + j + 1 + RING)
                    ins = dve.tensor_tensor(ub[j][:, CK - 1:], bank[(U_CONV + j) % RING][:, :], chunk(XV, j), ALU.mult)
                    ins.then_inc(bank_free, 1)
                    dve.wait_ge(bank_free, U_CONV + 4 + j + 1 + RING)
                    taps = [COL1[:, V_CONV + t * 4 + j:V_CONV + t * 4 + j + 1] for t in range(CK)]
                    after(dve.tensor_scalar(chunk(XV, j), ub[j][:, 0:S], taps[0], None, ALU.mult))
                    for t in range(1, CK):
                        after(dve.scalar_tensor_tensor(out=chunk(XV, j), in0=ub[j][:, t:t + S], scalar=taps[t],
                                                       in1=chunk(XV, j), op0=ALU.mult, op1=ALU.add))
                dve.wait_ge(head_in, 16 * 7)
                n = TT * DR // 2
                ang, tmp = ANGLE[:, 0:n], SIN[:, :]
                after(dve.tensor_copy(STAT[:, 100:100 + TT], POS[:, :]))
                for t in range(TT):
                    ins = dve.tensor_scalar(ang[:, t * DR // 2:(t + 1) * DR // 2], FREQ[:, :], STAT[:, 100 + t:101 + t], None, ALU.mult)
                after(ins)
                for i, (quarter, add) in enumerate(((0.0, 0.0), (0.25, np.pi / 2))):
                    r = ANGLE[:, (i + 1) * n:(i + 2) * n]
                    after(dve.tensor_scalar(tmp, ang, 1 / (2 * np.pi), quarter, ALU.mult, ALU.add))
                    after(dve.tensor_scalar(tmp, tmp, ROUND, ROUND, ALU.add, ALU.subtract))
                    src = ang
                    for part in TURN:
                        after(dve.scalar_tensor_tensor(out=r, in0=tmp, scalar=-part, in1=src, op0=ALU.mult, op1=ALU.add))
                        src = r
                    after(dve.tensor_scalar(r, r, float(add), None, ALU.add))
                    after(dve.tensor_scalar(r, r, HALF_TURN, -HALF_TURN, ALU.min, ALU.max))
                dve.sem_inc(angle_ready, 1)
                for j in range(4):
                    split_next(U_CONV + 8, 0, j)
                    dve.wait_ge(strip_done, U_CONV + 8 + j + 1 + RING)
                    dve.tensor_tensor(chunk(XV, j), bank[(U_CONV + j) % RING][:, :], chunk(XV, j), ALU.mult).then_inc(bank_free, 1)
                    dve.wait_ge(bank_free, U_CONV + 8 + j + 1 + RING)
                    after(dve.tensor_copy(chunk(A_HI, 4 + j), chunk(XV, j)))
                    dve.tensor_tensor(chunk(A_LO, 4 + j), chunk(XV, j), chunk(A_HI, 4 + j).bitcast(F32),
                                      ALU.subtract).then_inc(mixed, 1)
                dve.wait_ge(sin_ready, 2)
                dve.wait_ge(mixed, 4)
                wq, wk = HEADW[:, 0:DN], HEADW[:, DN:2 * DN]
                wqr, wkr = HEADW[:, 2 * DN:2 * DN + DR], HEADW[:, 2 * DN + DR:]
                for w in (wq, wqr):
                    after(dve.tensor_scalar(w, w, DQ ** -0.5, None, ALU.mult))

                def over_heads(ap, heads=H):
                    return ap.unsqueeze(1).to_broadcast([P, heads, ap.shape[1]])

                def over_features(ap, n):
                    return ap.unsqueeze(2).to_broadcast([P, ap.shape[1], n])

                def scaled(x, inv, w):
                    after(dve.tensor_tensor(x, x, over_features(inv, x.shape[2]), ALU.mult))
                    after(dve.tensor_tensor(x, x, over_heads(w, x.shape[1]), ALU.mult))

                def rotated(x, t, tmp):
                    heads = x.shape[1]
                    cos, sin = (over_heads(chunk(z, t, DR // 2), heads) for z in (COS, SIN))
                    x1, x2 = x[:, :, 0:DR // 2], x[:, :, DR // 2:]
                    m = [tmp[:, i * heads * DR // 2:(i + 1) * heads * DR // 2].rearrange("p (h d) -> p h d", h=heads) for i in range(4)]
                    dve.tensor_tensor(m[0], x1, cos, ALU.mult)
                    dve.tensor_tensor(m[1], x2, sin, ALU.mult)
                    dve.tensor_tensor(m[2], x2, cos, ALU.mult)
                    after(dve.tensor_tensor(m[3], x1, sin, ALU.mult))
                    dve.tensor_tensor(x1, m[0], m[1], ALU.subtract)
                    after(dve.tensor_tensor(x2, m[2], m[3], ALU.add))

                with loop(dve, TT, (seq, 14), (hsq, 3), (hstd, 2)) as t:
                    q, k = heads(chunk(QTOK, t, H * DQ)), heads(chunk(KTOK, t, H * DQ))
                    kr = chunk(KRT, t, DR).unsqueeze(1)
                    split_next(U_GATE, t, 0)
                    dve.wait_ge(head_sq, hsq.add(3))
                    dve.tensor_reduce(STAT[:, 0:H], heads(TQ0[:, :])[:, :, 0:DN], AX.X, ALU.add)
                    dve.tensor_reduce(STAT[:, H:2 * H], TQ1[:, 0:H * DN].rearrange("p (h d) -> p h d", h=H), AX.X, ALU.add)
                    dve.tensor_reduce(STAT[:, 2 * H:3 * H], heads(TQ0[:, :])[:, :, DN:], AX.X, ALU.add)
                    dve.tensor_reduce(STAT[:, 3 * H:3 * H + 1], TQ1[:, H * DN:H * DN + DR], AX.X, ALU.add).then_inc(head_sum, 1)
                    split_next(U_GATE, t, 1)
                    dve.wait_ge(head_std, hstd.add(2))
                    after(dve.reciprocal(STAT[:, 32:32 + 3 * H + 1], STAT[:, 0:3 * H + 1]))
                    scaled(q[:, :, 0:DN], STAT[:, 32:32 + H], wq)
                    scaled(q[:, :, DN:], STAT[:, 32 + 2 * H:32 + 3 * H], wqr)
                    rotated(q[:, :, DN:], t, RINV[:, :])
                    split_next(U_GATE, t, 2)
                    scaled(k[:, :, 0:DN], STAT[:, 32 + H:32 + 2 * H], wk)
                    scaled(kr, STAT[:, 32 + 3 * H:32 + 3 * H + 1], wkr)
                    rotated(kr, t, UN[:, 800:])
                    after(dve.tensor_copy(k[:, :, DN:], kr.to_broadcast([P, H, DR])))
                    dve.sem_inc(k_ready, 1)
                    split_next(U_GATE, t, 3)
                for n in range(1, 2 * H, 2):
                    dve.wait_ge(turned, n + 1)
                    dve.tensor_copy(chunk(KT, n // 2), bank[4 + n % 4][0:DQ, :]).then_inc(turn_dve, 1)

                def values():
                    for n in range(2 * H + 1, 2 * H + TT, 2):
                        dve.wait_ge(turned, n + 1)
                        dve.tensor_copy(chunk(V, n - 2 * H), bank[4 + n % 4][:, :]).then_inc(turn_dve, 1)

                attend(0, lambda n: (n % TT + 1) * P, None, PROB,
                       lambda c, src: dve.tensor_tensor(chunk(A_LO, c), src, chunk(A_HI, c).bitcast(F32), ALU.subtract), values)
                with loop(dve, KC // RING, (seq, 2 * RING)) as it:
                    for j in range(RING):
                        b, un = (U_BRANCH + j) % RING, UN[:, j % 2 * S:(j % 2 + 1) * S]
                        split_next(U_BRANCH, it, j)
                        dve.wait_ge(strip_done, it * RING + (U_BRANCH + j + 1 + RING))
                        after(dve.tensor_tensor(un, bank[b][:, :], chunk(GATES, it * RING + j), ALU.mult))
                        after(dve.tensor_tensor(RINV[:, :], bank[4 + b][:, :], chunk(GATES, it * RING + (KC + j)), ALU.mult))
                        dve.sem_inc(bank_free, 1)
                        dve.tensor_tensor(un, un, RINV[:, :], ALU.add).then_inc(merged, 1)
                        dve.wait_ge(mhi_ready, it * RING + (j + 1))
                        dve.tensor_tensor(chunk(H_LO, it * RING + j), un, chunk(H_HI, it * RING + j).bitcast(F32),
                                          ALU.subtract).then_inc(mlo_ready, 1)
                down(U_OUT, MOD, 40)

            def mixer2():
                for s in range(4):
                    split_next(U_CTX, 0, s)
                token_factors()
                norm(A_2, M_2, lambda i: split_next(U_CTX + 4, 0, i))
                dve.wait_ge(bank_free, U_IN2 + RING)
                cv = [CV[:, c * CPAD:(c + 1) * CPAD] for c in range(2)]
                for c in range(2):
                    dve.memset(cv[c][:, 0:PAD2], 0.0)
                    ins = dve.memset(cv[c][:, PAD2 + S:], 0.0)
                after(ins)
                taps = [(c, t) for c in range(2) for t in range(CK2)]

                def convolve(count):
                    for c, t in taps[:count]:
                        tap, v = COL3[:, 2 * t + c:2 * t + c + 1], cv[c][:, t:t + S]
                        if t == 0:
                            ins = dve.tensor_scalar(chunk(ACC, c), v, tap, COL1[:, V_DWB + c:V_DWB + c + 1], ALU.mult, ALU.add)
                        else:
                            ins = dve.scalar_tensor_tensor(out=chunk(ACC, c), in0=v, scalar=tap, in1=chunk(ACC, c),
                                                           op0=ALU.mult, op1=ALU.add)
                        after(ins)
                        if t == CK2 - 1:
                            dve.sem_inc(conv_ready, 1)
                    del taps[:count]

                def turned_values(n):
                    dve.wait_ge(vw_turned, n + 1)
                    dve.tensor_copy(window_values(n), window_bank(n)).then_inc(vw_dve, 1)

                for s in range(len(IN2_COLS)):
                    u = U_IN2 + s
                    split_next(U_IN2, 0, s)
                    if s < 2:
                        dve.wait_ge(strip_done, u + 1 + RING)
                        dve.tensor_copy(chunk(UT, s), bank[u % RING][:, :]).then_inc(bank_free, 1)
                    elif s in (3, 5):
                        c = s // 2 - 1
                        dve.wait_ge(strip_done, u + 1 + RING)
                        dve.wait_ge(sig_ready, c + 1)
                        ins = dve.tensor_tensor(cv[c][:, PAD2:PAD2 + S], bank[u % RING][:, :], SQ[:, c * S:(c + 1) * S], ALU.mult)
                        ins.then_inc(bank_free, 2)
                        dve.wait_ge(bank_free, u + 1 + RING)
                    if s >= 3:
                        convolve(5)
                    if s >= 15:
                        turned_values(2 * (s - 15) + 1)
                for t in (1, 3):
                    dve.wait_ge(uc_done, t + 1)
                    dve.tensor_copy(chunk(UC, t), bank[t][:, :]).then_inc(uc_dve, 1)
                for n in (7, 9):
                    turned_values(n)
                dve.wait_ge(ln_sum, 1)
                for c in range(2):
                    dve.scalar_tensor_tensor(out=chunk(ACC, c), in0=bank[4][:, :], scalar=-1.0 / CW2, in1=chunk(ACC, c),
                                             op0=ALU.mult, op1=ALU.add).then_inc(dev_ready, 1)
                def biases(heads):
                    for h in heads:
                        dve.wait_ge(rpb_turned, h + 1)
                        span = bank[BIAS_BANKS[h % 3]][:, 0:SPAN]
                        for v in range(3):
                            first = WIN - v * WIN // 2
                            ins = dve.tensor_tensor(chunk(BIAS, v * H + h, ROWS * KW).rearrange("p (k c) -> p k c", k=ROWS),
                                                    bass.AP(span.tensor, span.offset + first, [span.ap[0], [RPB_C, ROWS], [1, KW]]),
                                                    MASK[:, v * KW:(v + 1) * KW].unsqueeze(1).to_broadcast([P, ROWS, KW]), ALU.add)
                        ins.then_inc(bias_ready, 1)

                biases(range(6))
                dve.wait_ge(ln_std, 1)
                after(dve.reciprocal(bank[4][:, :], bank[4][:, :]))
                for c in range(2):
                    dve.tensor_tensor(chunk(ACC, c), chunk(ACC, c), bank[4][:, :], ALU.mult).then_inc(z_ready, 1)
                biases(range(6, H))
                dve.wait_ge(ft_done, 2)
                dve.tensor_copy(chunk(FT, 1), bank[1][:, :]).then_inc(ft_dve, 1)

                def outputs():
                    for i, m in enumerate((2, 3, 0, 1)):
                        dve.wait_ge(mix_hi, i + 1)
                        lo, hi = chunk(A_LO, m), chunk(A_HI, m).bitcast(F32)
                        if m < 2:
                            ins = dve.tensor_tensor(lo, bank[4 + i][:, :], hi, ALU.subtract)
                        else:
                            ins = dve.scalar_tensor_tensor(out=lo, in0=bank[4 + i][:, :], scalar=COL1[:, V_PWB + m - 2:V_PWB + m - 1],
                                                           in1=hi, op0=ALU.add, op1=ALU.subtract)
                        ins.then_inc(mixed, 1)

                def biased(n, scores):
                    h, j = n // TT, n % TT
                    return dve.tensor_tensor(scores[:, 0:ROWS * KW], scores[:, 0:ROWS * KW],
                                             chunk(BIAS, VARIANT[j] * H + h, ROWS * KW), ALU.add)

                attend(TT * H, lambda n: S, biased, PROB2,
                       lambda c, src: dve.tensor_tensor(by_rows(chunk(A_LO, 4 + c)), by_tiles(src),
                                                        by_rows(chunk(A_HI, 4 + c).bitcast(F32)), ALU.subtract), outputs)
                down(U_OUT2, MOD, M_2 + 2 * KC)

            def mlp():
                token_factors()
                norm(A_2 + KC, M_2 + 3 * KC)
                for part in range(MLP_PARTS):
                    u = U_MLP + 2 * KC * part
                    with loop(dve, KC // RING, (silu, RING), (ahi, RING), (alo_own, RING)) as it:
                        for j in range(RING):
                            hf = HF[:, j % 2 * S:(j % 2 + 1) * S]
                            split_next(u, it, j)
                            dve.wait_ge(alo_ready, alo_own.add(0))
                            alo_own.add()
                            dve.wait_ge(silu_ready, silu.add())
                            dve.tensor_tensor(hf, SG[:, j % 2 * S:(j % 2 + 1) * S], bank[(u + j) % RING][:, :],
                                              ALU.mult).then_inc(bank_free, 1)
                            dve.wait_ge(ahi_ready, ahi.add())
                            dve.tensor_tensor(chunk(A_LO, it * RING + j), hf, chunk(A_HI, it * RING + j).bitcast(F32),
                                              ALU.subtract).then_inc(alo_ready, 1)
                    down(u + KC, MOD, M_2 + 5 * KC)

            def nothing():
                pass

            def first_gate():
                mod_columns(16, 24, 16)
                after(half_gate(0))

            def mixer_modulation():
                mod_columns(24, 64, 24)
                factors(A_1 + KC, 24 + KC, V_NORM + KC)
                after(factors(A_1 + 2 * KC, 48 + KC, V_NORM + 2 * KC))

            def last_gate():
                mod_columns(64, M_2, 64)
                after(half_gate(2))

            def second_modulation():
                mod_columns(M_2, M_CTX, M_2)
                factors(A_2, M_2 + KC, V_N1G)
                after(factors(A_2 + KC, M_2 + 4 * KC, V_N2G))

            def context_rms():
                dve.wait_ge(ctx_std, 1)
                after(dve.reciprocal(STAT[:, 204:206], STAT[:, 200:202]))
                for j in range(2):
                    dve.tensor_scalar(CTOK[:, j * D:(j + 1) * D], CTOK[:, j * D:(j + 1) * D], STAT[:, 204 + j:205 + j], None,
                                      ALU.mult).then_inc(ctx_ready, 1)

            def context():
                mod_columns(M_CTX, M_COLS, M_2)
                dve.sem_inc(ctx_mod, 1)
                after(factors(A_CTX, M_CTX + KC, V_N1G))
                for k in range(KC + 1):
                    if k < KC:
                        dve.wait_ge(ctx_turned, k // 2 + 1)
                        if k >= 4:
                            dve.wait_ge(clo_ready, k - 3)
                        dve.tensor_scalar(chunk(HF, k % 4, CTX), bank[(4, 6, 7, 5)[k // 2]][:, k % 2 * CTX:(k % 2 + 1) * CTX],
                                          AMOD[:, A_CTX + k:A_CTX + k + 1], MOD[:, M_CTX + k:M_CTX + k + 1],
                                          ALU.mult, ALU.add).then_inc(ctx_full, 1)
                    if k >= 1:
                        dve.wait_ge(chi_ready, k)
                        dve.tensor_tensor(chunk(C_LO, k - 1, CTX), chunk(HF, (k - 1) % 4, CTX),
                                          chunk(C_HI, k - 1, CTX).bitcast(F32), ALU.subtract).then_inc(clo_ready, 1)

            dve.sem_inc(lo_ready, RING)
            dve.sem_inc(h_ready, 2)
            dve.sem_inc(alo_ready, 2)
            dve.wait_ge(cond_ready, 1)
            for t in range(5):
                gem_step(t % GEM_RING, t, C_1, t)
            token_factors()
            for u in range(LEAD):
                split_lo(u, u)
            dve.wait_ge(cols_ready, 2)
            mod_columns(0, 16, 0)
            after(factors(A_1, KC, V_NORM))
            dve.sem_inc(gem_done, 3)
            norm(A_1, 0)
            ffn(U_FFN0, 0, 8, C_1, 0, None, [first_gate, nothing, mixer_modulation], [nothing] * 3)
            mixer1()
            token_factors()
            norm(A_1 + 2 * KC, 48)
            ffn(U_FFN1, 1, T_ADA, C_2, 2 * KC, C_CTX, [last_gate, context_rms, second_modulation], [nothing, context, nothing])
            mixer2()
            mlp()
            dve.wait_ge(std_ready, std.add())
            after(dve.reciprocal(RMS[:, TT:], RMS[:, 0:TT]))
            dve.sem_inc(y_scaled, 1)
            for t in range(TT):
                dve.wait_ge(y_turned, TT + t + 1)
                dve.tensor_scalar(YTOK[:, t * D + S:(t + 1) * D], bank[t][:, :], RMS[:, TT + t:TT + t + 1],
                                  None, ALU.mult).then_inc(ytok_dve, 1)


_INS = ["x", "c", "positions", "w_ada", "b_ada", "norm_w", "ffn_w13", "ffn_w2", "w_in", "q_a_norm", "w_uq", "kv_a_norm",
        "w_ukv", "q_norm_nope", "k_norm_nope", "q_norm_rope", "k_norm_rope", "conv_w", "w_branch", "w_out", "c_2",
        "ctx_2", "c_ctx_2", "ada_w_2", "ada_b_2", "norm1_g_2", "norm2_g_2", "w_in_2", "w_fourier_2", "conv_dw_w_2",
        "conv_dw_b_2", "conv_norm_g_2", "conv_norm_b_2", "conv_pw_w_2", "conv_pw_b_2", "na_rpb_2", "w_out_2",
        "mlp_w1_2", "mlp_w2_2", "final_norm_g_2"]


def constants():
    f = 1.0 / np.float32(10000) ** (np.arange(0, DR, 2, dtype=np.float32) / np.float32(DR))
    feat = np.arange(DH)
    turn = 2 * np.pi * np.outer(feat, feat) / DH
    two = np.kron(np.eye(2), np.cos(turn)), np.kron(np.eye(2), np.sin(turn))
    tok = np.arange(S)
    turn = 2 * np.pi * (np.outer(tok, tok) % S) / S
    scale = 1.0 / np.sqrt(S * DH)
    q, k = np.arange(P)[:, None], np.arange(P)[None, :]
    near = np.zeros((P, 3, KW), np.float32)
    for v, (tile, w) in enumerate(((0, 0), (1, 8), (3, 32))):
        col, key = QC * tile + np.arange(P)[:, None] % QC, w + np.arange(KW)[None, :]
        first = np.clip(col - WIN // 2, 0, COLS - WIN)
        near[:, v] = np.where((key >= first) & (key < first + WIN), 0.0, NEG)
    return {
        "rope_freq": np.tile(f.astype(np.float32), (P, 1)),
        "dft_feat": np.concatenate(two, axis=1).astype(np.float32),
        "dft_tok": np.stack([np.cos(turn) * scale, -np.sin(turn) * scale]).astype(np.float32),
        "causal": np.where(k <= q, 0.0, NEG).astype(np.float32),
        "near": near,
    }


def kernel(**inputs):
    import concourse.bacc as bacc
    from concourse.bass_utils import run_bass_kernel_spmd as run

    nc = bacc.Bacc("TRN2", target_bir_lowering=False, num_devices=1)
    arrays, aps = {}, {}
    given = {n: np.ascontiguousarray(inputs[n]) for n in _INS}
    for name, v in {**given, **constants()}.items():
        arrays[f"in_{name}"] = v
        aps[name] = nc.dram_tensor(f"in_{name}", v.shape, mybir.dt.from_np(v.dtype), kind="ExternalInput").ap()
    out = nc.dram_tensor("out_0", (1, S, D), F32, kind="ExternalOutput").ap()
    block_pair_kernel(nc, aps, out)
    r = run(nc, [arrays], core_ids=[0])
    return r.results[0]["out_0"]
```
